# Optimizing a Trainium2 kernel written in Bass

```python
import math
import jax, jax.numpy as jnp
from jax import lax
import numpy as np

D_MODEL = 1024
BATCH = 1
SEQ = 512
DEPTH = 1

GRID_W = 64
CTX_LEN = 256
EPS = 1e-6
N_MOD = 6
SSD_EXPAND = 2
D_SSD = SSD_EXPAND * D_MODEL
SSD_HEADDIM = 64
SSD_HEADS = D_SSD // SSD_HEADDIM
SSD_GROUPS = 4
SSD_HPG = SSD_HEADS // SSD_GROUPS
SSD_STATE = 128
SSD_CONV = 3
SSD_CHUNK = 128
D_BC = SSD_GROUPS * SSD_STATE
D_XBC = D_SSD + 2 * D_BC
DT_MIN = 1e-3
DT_MAX = 1e-1
ATT_HEADS = 16
ATT_KV_HEADS = 4
ATT_GROUP = ATT_HEADS // ATT_KV_HEADS
ATT_HEADDIM = 64
WINDOW = 128
ATT_BLOCK = 128
D_Q = ATT_HEADS * ATT_HEADDIM
D_KV = ATT_KV_HEADS * ATT_HEADDIM
ROPE_BASE = 10000.0
D_FF = 2816
FFN_CONV = 3
N_BRANCH = 2
Z0 = 0
XBC0 = Z0 + D_SSD
DT0 = XBC0 + D_XBC
Q0 = DT0 + 2 * SSD_HEADS
K0 = Q0 + D_Q
V0 = K0 + D_KV
G0 = V0 + D_KV
D_IN = G0 + N_BRANCH * D_MODEL


def rmsnorm(x, g):
    x32 = x.astype(jnp.float32)
    y = x32 * lax.rsqrt(jnp.mean(x32 * x32, axis=-1, keepdims=True) + EPS)
    return (y * g.astype(jnp.float32)).astype(x.dtype)

def modulate(x, g, shift, scale):
    return rmsnorm(x, g) * (1 + scale) + shift

def dwconv_centred(x, w, b):
    K, C = w.shape
    y = lax.conv_general_dilated(x, w[:, None, :].astype(x.dtype), window_strides=(1,),
                                 padding=[(K // 2, K // 2)],
                                 dimension_numbers=('NWC', 'WIO', 'NWC'),
                                 feature_group_count=C)
    return y + b.astype(x.dtype)

def segsum(a):
    T = a.shape[-1]
    cs = jnp.cumsum(a, axis=-1)
    diff = cs[..., :, None] - cs[..., None, :]
    return jnp.where(jnp.tril(jnp.ones((T, T), dtype=bool)), diff, -jnp.inf)

def ssd_scan(xs, la, bm, cm, h0, with_output):
    f32 = jnp.float32
    Bsz, L, G, R, P = xs.shape
    N = bm.shape[-1]
    T = SSD_CHUNK
    nc = L // T
    xc = xs.astype(f32).reshape(Bsz, nc, T, G, R, P)
    bc = bm.astype(f32).reshape(Bsz, nc, T, G, N)
    cc = cm.astype(f32).reshape(Bsz, nc, T, G, N)
    ac = la.astype(f32).reshape(Bsz, nc, T, G, R).transpose(0, 3, 4, 1, 2)
    cs = jnp.cumsum(ac, axis=-1)
    decay_to_end = jnp.exp(cs[..., -1:] - cs)
    states = jnp.einsum('bcsgn,bgrcs,bcsgrp->bcgrpn', bc, decay_to_end, xc)
    if h0 is None:
        h0 = jnp.zeros((Bsz, G, R, P, N), f32)
    states = jnp.concatenate([h0[:, None].astype(f32), states], axis=1)
    chunk_decay = jnp.exp(segsum(jnp.pad(cs[..., -1], ((0, 0), (0, 0), (0, 0), (1, 0)))))
    states = jnp.einsum('bgrzc,bcgrpn->bzgrpn', chunk_decay, states)
    final = states[:, -1]
    if not with_output:
        return None, final
    cb = jnp.einsum('bclgn,bcsgn->bgcls', cc, bc)
    scores = cb[:, :, None] * jnp.exp(segsum(ac))
    y_diag = jnp.einsum('bgrcls,bcsgrp->bclgrp', scores, xc)
    y_off = jnp.einsum('bclgn,bcgrpn,bgrcl->bclgrp', cc, states[:, :-1], jnp.exp(cs))
    return (y_diag + y_off).reshape(Bsz, L, G, R, P).astype(xs.dtype), final

def ssd_prepare(xbc_raw, dt_raw, conv_w, conv_b, dt_bias, a_log):
    xbc = jax.nn.silu(dwconv_centred(xbc_raw, conv_w, conv_b))
    Bsz, L, _ = xbc.shape
    xs = xbc[..., :D_SSD].reshape(Bsz, L, SSD_GROUPS, SSD_HPG, SSD_HEADDIM)
    bm = xbc[..., D_SSD:D_SSD + D_BC].reshape(Bsz, L, SSD_GROUPS, SSD_STATE)
    cm = xbc[..., D_SSD + D_BC:].reshape(Bsz, L, SSD_GROUPS, SSD_STATE)
    dt = jax.nn.softplus(dt_raw.astype(jnp.float32).reshape(Bsz, L, 2, SSD_HEADS)
                         + dt_bias.astype(jnp.float32))
    la = dt * (-jnp.exp(a_log.astype(jnp.float32)))
    dt = dt.reshape(Bsz, L, 2, SSD_GROUPS, SSD_HPG)
    la = la.reshape(Bsz, L, 2, SSD_GROUPS, SSD_HPG)
    return xs, bm, cm, dt, la

def ssd_bidir(xs, bm, cm, dt, la, h0f, h0b, with_output):
    xf = xs * dt[:, :, 0, :, :, None].astype(xs.dtype)
    xb = xs * dt[:, :, 1, :, :, None].astype(xs.dtype)
    yf, hf = ssd_scan(xf, la[:, :, 0], bm, cm, h0f, with_output)
    yb, hb = ssd_scan(jnp.flip(xb, axis=1), jnp.flip(la[:, :, 1], axis=1), jnp.flip(bm, axis=1),
                      jnp.flip(cm, axis=1), h0b, with_output)
    y = yf + jnp.flip(yb, axis=1) if with_output else None
    return y, hf, hb

def ssd_output(y, xs, z, d_skip, g):
    Bsz, L = y.shape[:2]
    y = y + d_skip.reshape(SSD_GROUPS, SSD_HPG, 1).astype(y.dtype) * xs
    return rmsnorm(y.reshape(Bsz, L, D_SSD) * jax.nn.silu(z), g)

def axial_rope(t, row, col):
    half = ATT_HEADDIM // 2
    inv = ROPE_BASE ** (-jnp.arange(0, half, 2, dtype=jnp.float32) / half)

    def rot(u, pos):
        ang = pos.astype(jnp.float32)[:, None] * inv[None]
        cos = jnp.cos(ang)[None, :, None, :].astype(u.dtype)
        sin = jnp.sin(ang)[None, :, None, :].astype(u.dtype)
        u1, u2 = u[..., :half // 2], u[..., half // 2:]
        return jnp.concatenate([u1 * cos - u2 * sin, u2 * cos + u1 * sin], axis=-1)

    return jnp.concatenate([rot(t[..., :half], row), rot(t[..., half:], col)], axis=-1)

def window_ctx_attention(q, k, v, kc, vc, sink):
    Bsz, L, H, Dh = q.shape
    nb = L // ATT_BLOCK
    scale = Dh ** -0.5
    qb = q.reshape(Bsz, nb, ATT_BLOCK, ATT_KV_HEADS, ATT_GROUP, Dh)

    def band(t):
        tb = t.reshape(Bsz, nb, ATT_BLOCK, ATT_KV_HEADS, Dh)
        tp = jnp.pad(tb, ((0, 0), (1, 1), (0, 0), (0, 0), (0, 0)))
        return jnp.concatenate([tp[:, :-2], tp[:, 1:-1], tp[:, 2:]], axis=2)

    kb, vb = band(k), band(v)
    s_win = jnp.einsum('bnqkgd,bnjkd->bnkgqj', qb, kb) * scale
    s_ctx = jnp.einsum('bnqkgd,bckd->bnkgqc', qb, kc) * scale
    qpos = jnp.arange(nb)[:, None] * ATT_BLOCK + jnp.arange(ATT_BLOCK)[None]
    kpos = (jnp.arange(nb)[:, None] - 1) * ATT_BLOCK + jnp.arange(3 * ATT_BLOCK)[None]
    valid = ((jnp.abs(qpos[:, :, None] - kpos[:, None, :]) <= WINDOW)
             & (kpos >= 0)[:, None, :] & (kpos < L)[:, None, :])
    s_win = jnp.where(valid[None, :, None, None], s_win, -jnp.inf)
    s_sink = jnp.broadcast_to(sink.reshape(1, 1, ATT_KV_HEADS, ATT_GROUP, 1, 1).astype(s_win.dtype),
                              s_win.shape[:-1] + (1,))
    logits = jnp.concatenate([s_win, s_ctx, s_sink], axis=-1).astype(jnp.float32)
    p = jax.nn.softmax(logits, axis=-1).astype(v.dtype)
    nw = 3 * ATT_BLOCK
    Lc = kc.shape[1]
    o = (jnp.einsum('bnkgqj,bnjkd->bnqkgd', p[..., :nw], vb)
         + jnp.einsum('bnkgqc,bckd->bnqkgd', p[..., nw:nw + Lc], vc))
    return o.reshape(Bsz, L, H * Dh)

def ctx_self_attention(q, k, v, sink):
    Bsz, Lc, H, Dh = q.shape
    qg = q.reshape(Bsz, Lc, ATT_KV_HEADS, ATT_GROUP, Dh)
    s = jnp.einsum('bqkgd,bckd->bkgqc', qg, k) * (Dh ** -0.5)
    s_sink = jnp.broadcast_to(sink.reshape(1, ATT_KV_HEADS, ATT_GROUP, 1, 1).astype(s.dtype),
                              s.shape[:-1] + (1,))
    p = jax.nn.softmax(jnp.concatenate([s, s_sink], axis=-1).astype(jnp.float32), axis=-1)
    o = jnp.einsum('bkgqc,bckd->bqkgd', p[..., :Lc].astype(v.dtype), v)
    return o.reshape(Bsz, Lc, H * Dh)

def merge_branches(p, y_ssd, y_att, w_o_ssd, w_o_att, w_out):
    gates = jax.nn.sigmoid(p[..., G0:D_IN])
    g_ssd, g_att = gates[..., :D_MODEL], gates[..., D_MODEL:]
    return (g_ssd * (y_ssd @ w_o_ssd) + g_att * (y_att @ w_o_att)) @ w_out

def token_mixer(h_lat, h_ctx, row, col, w_in, conv_w, conv_b, dt_bias, a_log, d_skip, ssd_g,
                w_o_ssd, w_o_att, sink, w_out, with_ctx_out):
    Bsz, L, _ = h_lat.shape
    Lc = h_ctx.shape[1]
    p_lat = h_lat @ w_in
    p_ctx = h_ctx @ w_in
    xs_c, bm_c, cm_c, dt_c, la_c = ssd_prepare(p_ctx[..., XBC0:DT0], p_ctx[..., DT0:Q0],
                                               conv_w, conv_b, dt_bias, a_log)
    y_c, hf_c, hb_c = ssd_bidir(xs_c, bm_c, cm_c, dt_c, la_c, None, None, with_ctx_out)
    xs_l, bm_l, cm_l, dt_l, la_l = ssd_prepare(p_lat[..., XBC0:DT0], p_lat[..., DT0:Q0],
                                               conv_w, conv_b, dt_bias, a_log)
    y_l, _, _ = ssd_bidir(xs_l, bm_l, cm_l, dt_l, la_l, hf_c, hb_c, True)
    ssd_lat = ssd_output(y_l, xs_l, p_lat[..., Z0:XBC0], d_skip, ssd_g)
    q_l = axial_rope(p_lat[..., Q0:K0].reshape(Bsz, L, ATT_HEADS, ATT_HEADDIM), row, col)
    k_l = axial_rope(p_lat[..., K0:V0].reshape(Bsz, L, ATT_KV_HEADS, ATT_HEADDIM), row, col)
    v_l = p_lat[..., V0:G0].reshape(Bsz, L, ATT_KV_HEADS, ATT_HEADDIM)
    k_c = p_ctx[..., K0:V0].reshape(Bsz, Lc, ATT_KV_HEADS, ATT_HEADDIM)
    v_c = p_ctx[..., V0:G0].reshape(Bsz, Lc, ATT_KV_HEADS, ATT_HEADDIM)
    att_lat = window_ctx_attention(q_l, k_l, v_l, k_c, v_c, sink)
    out_lat = merge_branches(p_lat, ssd_lat, att_lat, w_o_ssd, w_o_att, w_out)
    if not with_ctx_out:
        return out_lat, None
    ssd_ctx = ssd_output(y_c, xs_c, p_ctx[..., Z0:XBC0], d_skip, ssd_g)
    q_c = p_ctx[..., Q0:K0].reshape(Bsz, Lc, ATT_HEADS, ATT_HEADDIM)
    att_ctx = ctx_self_attention(q_c, k_c, v_c, sink)
    out_ctx = merge_branches(p_ctx, ssd_ctx, att_ctx, w_o_ssd, w_o_att, w_out)
    return out_lat, out_ctx

def conv_ffn(h, w_up, conv_w, conv_b, w_down):
    u = dwconv_centred(h @ w_up, conv_w, conv_b)
    a, b = u[..., :D_FF], u[..., D_FF:]
    return (jax.nn.silu(a) * b) @ w_down

def first_inputs(seed: int = 0) -> dict:
    key = jax.random.key(seed)
    ks = jax.random.split(key, 24)
    f32 = jnp.float32

    def nrm(k, shape, scale):
        return jax.random.normal(k, shape, f32) * scale

    dt0 = jnp.exp(jax.random.uniform(ks[10], (DEPTH, 2, SSD_HEADS), f32,
                                     math.log(DT_MIN), math.log(DT_MAX)))
    return {
        'x': nrm(ks[0], (BATCH, SEQ, D_MODEL), 1.0),
        'c': nrm(ks[1], (BATCH, D_MODEL), 1.0),
        'ctx': nrm(ks[2], (BATCH, CTX_LEN, D_MODEL), 1.0),
        'c_ctx': nrm(ks[3], (D_MODEL,), 1.0),
        'w_mod': nrm(ks[4], (DEPTH, D_MODEL, N_MOD * D_MODEL), 0.5 * D_MODEL ** -0.5),
        'b_mod': nrm(ks[5], (DEPTH, N_MOD * D_MODEL), 0.01),
        'norm1_g': 1.0 + nrm(ks[6], (DEPTH, D_MODEL), 0.05),
        'norm2_g': 1.0 + nrm(ks[7], (DEPTH, D_MODEL), 0.05),
        'w_in': nrm(ks[8], (DEPTH, D_MODEL, D_IN), D_MODEL ** -0.5),
        'ssd_conv_w': nrm(ks[9], (DEPTH, SSD_CONV, D_XBC), SSD_CONV ** -0.5),
        'ssd_conv_b': nrm(ks[11], (DEPTH, D_XBC), 0.01),
        'ssd_dt_bias': dt0 + jnp.log(-jnp.expm1(-dt0)),
        'ssd_a_log': jnp.log(jax.random.uniform(ks[12], (DEPTH, 2, SSD_HEADS), f32, 1.0, 16.0)),
        'ssd_d': 1.0 + nrm(ks[13], (DEPTH, SSD_HEADS), 0.1),
        'ssd_norm_g': 1.0 + nrm(ks[14], (DEPTH, D_SSD), 0.05),
        'w_o_ssd': nrm(ks[15], (DEPTH, D_SSD, D_MODEL), D_SSD ** -0.5),
        'w_o_att': nrm(ks[16], (DEPTH, D_Q, D_MODEL), D_Q ** -0.5),
        'att_sink': nrm(ks[17], (DEPTH, ATT_HEADS), 0.5),
        'w_out': nrm(ks[18], (DEPTH, D_MODEL, D_MODEL), D_MODEL ** -0.5),
        'w_up': nrm(ks[19], (DEPTH, D_MODEL, 2 * D_FF), D_MODEL ** -0.5),
        'ffn_conv_w': nrm(ks[20], (DEPTH, FFN_CONV, 2 * D_FF), FFN_CONV ** -0.5),
        'ffn_conv_b': nrm(ks[21], (DEPTH, 2 * D_FF), 0.01),
        'w_down': nrm(ks[22], (DEPTH, D_FF, D_MODEL), D_FF ** -0.5),
        'final_g': 1.0 + nrm(ks[23], (D_MODEL,), 0.05),
    }

def first_block(x, c, ctx, c_ctx, w_mod, b_mod, norm1_g, norm2_g, w_in, ssd_conv_w, ssd_conv_b,
              ssd_dt_bias, ssd_a_log, ssd_d, ssd_norm_g, w_o_ssd, w_o_att, att_sink, w_out,
              w_up, ffn_conv_w, ffn_conv_b, w_down, final_g):
    L = x.shape[1]
    ROWS = L // GRID_W
    row = jnp.broadcast_to(jnp.arange(ROWS)[:, None], (ROWS, GRID_W)).reshape(-1)
    col = jnp.broadcast_to(jnp.arange(GRID_W)[None, :], (ROWS, GRID_W)).reshape(-1)
    for l in range(DEPTH):
        last = l == DEPTH - 1
        mod = jax.nn.silu(c) @ w_mod[l] + b_mod[l]
        sh1, sc1, gt1, sh2, sc2, gt2 = jnp.split(mod[:, None, :], N_MOD, axis=-1)
        mod_c = jax.nn.silu(c_ctx) @ w_mod[l] + b_mod[l]
        csh1, csc1, cgt1, csh2, csc2, cgt2 = jnp.split(mod_c, N_MOD, axis=-1)
        h_lat = modulate(x, norm1_g[l], sh1, sc1)
        h_ctx = modulate(ctx, norm1_g[l], csh1, csc1)
        o_lat, o_ctx = token_mixer(h_lat, h_ctx, row, col, w_in[l], ssd_conv_w[l], ssd_conv_b[l],
                                   ssd_dt_bias[l], ssd_a_log[l], ssd_d[l], ssd_norm_g[l],
                                   w_o_ssd[l], w_o_att[l], att_sink[l], w_out[l], not last)
        x = x + gt1 * o_lat
        x = x + gt2 * conv_ffn(modulate(x, norm2_g[l], sh2, sc2), w_up[l], ffn_conv_w[l],
                               ffn_conv_b[l], w_down[l])
        if not last:
            ctx = ctx + cgt1 * o_ctx
            ctx = ctx + cgt2 * conv_ffn(modulate(ctx, norm2_g[l], csh2, csc2), w_up[l],
                                        ffn_conv_w[l], ffn_conv_b[l], w_down[l])
    return rmsnorm(x, final_g)


DEPTH_2 = 4

N_MIXERS = 3
N_SGU_LAYERS = (DEPTH_2 + 2) // 3
N_RWKV_LAYERS = (DEPTH_2 + 1) // 3
N_MLA_LAYERS = DEPTH_2 // 3
RMS_EPS = 1e-6
SGU_WIDTH = 2 * D_MODEL
SGU_CHUNK = 128
SGU_GROUPS = 8
SGU_GROUP_W = SGU_WIDTH // SGU_GROUPS
RWKV_HEAD = 64
RWKV_WIDTH = D_MODEL
RWKV_HEADS = RWKV_WIDTH // RWKV_HEAD
RWKV_DECAY_LORA = 64
RWKV_ICLR_LORA = 64
RWKV_LN_EPS = 64e-5
RWKV_N_LERP = 6
MLA_HEADS = 16
MLA_NOPE = 128
MLA_ROPE = 64
MLA_QK_DIM = MLA_NOPE + MLA_ROPE
MLA_VDIM = 128
MLA_Q_RANK = 768
MLA_KV_RANK = 256
MLA_WIDTH = MLA_HEADS * MLA_VDIM
MLA_QBLOCK = 128
MLA_SCALE = MLA_QK_DIM ** -0.5
ROPE_FREQS_PER_AXIS = MLA_ROPE // 4


def rms_norm(t, gain=None):
    tf = t.astype(jnp.float32)
    y = tf * lax.rsqrt(jnp.mean(tf * tf, axis=-1, keepdims=True) + RMS_EPS)
    if gain is not None:
        y = y * gain.astype(jnp.float32)
    return y.astype(t.dtype)

def ada_modulation(cond, w, b):
    m = jax.nn.silu(cond) @ w + b
    shift, scale, gate = jnp.split(m, 3, axis=-1)
    return shift[..., None, :], scale[..., None, :], gate[..., None, :]

def sgu_mixer(h, w_in, gain, w_s, b_s, w_out):
    bsz, length, _ = h.shape
    u, v, z = jnp.split(h @ w_in, 3, axis=-1)
    u = jax.nn.gelu(u)
    v = rms_norm(jax.nn.gelu(v), gain)
    vc = v.reshape(bsz, length // SGU_CHUNK, SGU_CHUNK, SGU_GROUPS, SGU_GROUP_W)
    mixed = jnp.einsum('gpq,bcqgd->bcpgd', w_s, vc) + b_s.T[:, :, None]
    s = u * mixed.reshape(bsz, length, SGU_WIDTH)
    return (s * jax.nn.silu(z)) @ w_out

def split_heads(t):
    return t.reshape(t.shape[:-1] + (RWKV_HEADS, RWKV_HEAD))

def center_shift(h):
    prev = jnp.pad(h[:, :-1], ((0, 0), (1, 0), (0, 0)))
    nxt = jnp.pad(h[:, 1:], ((0, 0), (0, 1), (0, 0)))
    return 0.5 * (prev + nxt) - h

def rwkv7_features(h, mu, w_in, w_lora1, w_lora2, w0, a_lora1, a_lora2, a0, k_k, k_a):
    xx = center_shift(h)
    xs = h[:, :, None, :] + xx[:, :, None, :] * mu
    rkvz = jnp.einsum('blcd,cde->blce', xs[:, :, :4], w_in)
    r, k, v, z = rkvz[:, :, 0], rkvz[:, :, 1], rkvz[:, :, 2], rkvz[:, :, 3]
    w_lora = jnp.einsum('nblr,nre->nble', jnp.tanh(jnp.einsum('bld,ndr->nblr', xs[:, :, 4], w_lora1)), w_lora2)
    log_w = -jax.nn.softplus(-(w0[:, None, None, :] + w_lora)) - 0.5
    decay = jnp.exp(-jnp.exp(log_w.astype(jnp.float32)))
    a = jax.nn.sigmoid(a0[:, None, None, :] + jnp.einsum('nblr,nre->nble', jnp.einsum('bld,ndr->nblr', xs[:, :, 5], a_lora1), a_lora2))
    kk = split_heads(k * k_k).astype(jnp.float32)
    kk = (kk * lax.rsqrt(jnp.sum(kk * kk, axis=-1, keepdims=True) + 1e-12)).reshape(k.shape)
    k_dir = k * (1 + (a - 1) * k_a)
    return r, decay, k_dir, v, kk, a, z

def to_scan_order(t_dir):
    return jnp.stack([t_dir[0], jnp.flip(t_dir[1], axis=1)])

def rwkv7_scan(state0, r, decay, k_dir, v, kk, a, emit):
    bsz, length = v.shape[:2]
    both = lambda t: jnp.broadcast_to(t, (2,) + t.shape)
    inputs = (decay, k_dir, both(v), both(kk), a) + ((both(r),) if emit else ())
    seqs = tuple(jnp.moveaxis(split_heads(to_scan_order(t).astype(jnp.float32)), 2, 0) for t in inputs)

    def step(S, inp):
        w_t, k_t, v_t, kk_t, a_t = inp[:5]
        s_kk = jnp.einsum('nbhvk,nbhk->nbhv', S, kk_t)
        S = S * w_t[..., None, :] - s_kk[..., :, None] * (kk_t * a_t)[..., None, :] + v_t[..., :, None] * k_t[..., None, :]
        y_t = jnp.einsum('nbhvk,nbhk->nbhv', S, inp[5]) if emit else None
        return S, y_t

    s_final, ys = lax.scan(step, state0, seqs)
    if not emit:
        return s_final, None
    ys = jnp.moveaxis(ys, 0, 2)
    y = ys[0] + jnp.flip(ys[1], axis=1)
    return s_final, y.reshape(bsz, length, RWKV_WIDTH)

def rwkv7_output(y, r, k_dir, v, z, r_k, ln_gain, ln_bias, w_out):
    yh = split_heads(y)
    mean = jnp.mean(yh, axis=-1, keepdims=True)
    var = jnp.mean(jnp.square(yh - mean), axis=-1, keepdims=True)
    yn = ((yh - mean) * lax.rsqrt(var + RWKV_LN_EPS)).reshape(y.shape) * ln_gain + ln_bias
    bonus = jnp.sum(split_heads(r)[None] * split_heads(k_dir) * r_k, axis=-1, keepdims=True) * split_heads(v)[None]
    out = (yn + jnp.sum(bonus, axis=0).reshape(y.shape)).astype(z.dtype)
    return (out * jax.nn.silu(z)) @ w_out

def axial_rope_tables(length):
    rows = length // GRID_W
    row = jnp.repeat(jnp.arange(rows, dtype=jnp.float32), GRID_W)
    col = jnp.tile(jnp.arange(GRID_W, dtype=jnp.float32), rows)
    inv_freq = ROPE_BASE ** (-jnp.arange(ROPE_FREQS_PER_AXIS, dtype=jnp.float32) / ROPE_FREQS_PER_AXIS)
    ang = jnp.concatenate([row[:, None] * inv_freq, col[:, None] * inv_freq], axis=-1)
    return jnp.cos(ang), jnp.sin(ang)

def apply_rope(t, cos, sin):
    t_nope, t_rope = jnp.split(t, [MLA_NOPE], axis=-1)
    x1, x2 = jnp.split(t_rope, 2, axis=-1)
    cs, sn = cos[:, None, :], sin[:, None, :]
    out = jnp.concatenate([t_nope, x1 * cs - x2 * sn, x1 * sn + x2 * cs], axis=-1)
    return out.astype(t.dtype)

def mla_project(h, w_in, q_norm, kv_norm, w_uq, w_ukv, qk_gain_q, qk_gain_k, need_q):
    bsz, length, _ = h.shape
    if need_q:
        c_q, c_kv, k_rope, z = jnp.split(h @ w_in, [MLA_Q_RANK, MLA_Q_RANK + MLA_KV_RANK, MLA_Q_RANK + MLA_KV_RANK + MLA_ROPE], axis=-1)
        q = (rms_norm(c_q, q_norm) @ w_uq).reshape(bsz, length, MLA_HEADS, MLA_QK_DIM)
        q = rms_norm(q, qk_gain_q)
    else:
        c_kv, k_rope = jnp.split(h @ w_in[:, MLA_Q_RANK:MLA_Q_RANK + MLA_KV_RANK + MLA_ROPE], [MLA_KV_RANK], axis=-1)
        q, z = None, None
    kv = (rms_norm(c_kv, kv_norm) @ w_ukv).reshape(bsz, length, MLA_HEADS, MLA_NOPE + MLA_VDIM)
    k_nope, v = jnp.split(kv, [MLA_NOPE], axis=-1)
    k = jnp.concatenate([k_nope, jnp.broadcast_to(k_rope[:, :, None, :], (bsz, length, MLA_HEADS, MLA_ROPE))], axis=-1)
    k = rms_norm(k, qk_gain_k)
    return q, k, v, z

def mla_latent_attention(q, k, v, k_ctx, v_ctx, cos, sin):
    bsz, length = q.shape[:2]
    n_ctx = k_ctx.shape[1]
    q_rot, k_rot = apply_rope(q, cos, sin), apply_rope(k, cos, sin)
    nblk = length // MLA_QBLOCK
    blocks = lambda t: jnp.moveaxis(t.reshape(bsz, nblk, MLA_QBLOCK, MLA_HEADS, MLA_QK_DIM), 1, 0)

    def one_block(qs):
        qr, qp = qs
        s = jnp.concatenate([jnp.einsum('bqhd,bkhd->bhqk', qp, k_ctx), jnp.einsum('bqhd,bkhd->bhqk', qr, k_rot)], axis=-1)
        p = jax.nn.softmax(s.astype(jnp.float32) * MLA_SCALE, axis=-1).astype(v.dtype)
        return jnp.einsum('bhqk,bkhd->bqhd', p[..., :n_ctx], v_ctx) + jnp.einsum('bhqk,bkhd->bqhd', p[..., n_ctx:], v)

    o = lax.map(one_block, (blocks(q_rot), blocks(q)))
    return jnp.moveaxis(o, 0, 1).reshape(bsz, length, MLA_WIDTH)

def mla_context_attention(q, k, v):
    bsz, n_ctx = q.shape[:2]
    p = jax.nn.softmax(jnp.einsum('bqhd,bkhd->bhqk', q, k).astype(jnp.float32) * MLA_SCALE, axis=-1).astype(v.dtype)
    return jnp.einsum('bhqk,bkhd->bqhd', p, v).reshape(bsz, n_ctx, MLA_WIDTH)

def second_inputs(seed: int = 0) -> dict:
    key = jax.random.key(seed)
    it = iter(jax.random.split(key, 48))
    nrm = lambda shape, scale: scale * jax.random.normal(next(it), shape, jnp.float32)
    D = D_MODEL
    nA, nB, nC = N_SGU_LAYERS, N_RWKV_LAYERS, N_MLA_LAYERS
    return {
        'x': nrm((BATCH, SEQ, D), 1.0),
        'c': nrm((BATCH, D), 1.0),
        'ctx': nrm((BATCH, CTX_LEN, D), 1.0),
        'c_ctx': nrm((D,), 1.0),
        'ada_w': nrm((DEPTH_2, D, 3 * D), 0.5 * D ** -0.5),
        'ada_b': nrm((DEPTH_2, 3 * D), 0.02),
        'sgu_w_in': nrm((nA, D, 3 * SGU_WIDTH), D ** -0.5),
        'sgu_gain': 1.0 + nrm((nA, SGU_WIDTH), 0.02),
        'sgu_w_s': nrm((nA, SGU_GROUPS, SGU_CHUNK, SGU_CHUNK), SGU_CHUNK ** -0.5),
        'sgu_b_s': 1.0 + nrm((nA, SGU_GROUPS, SGU_CHUNK), 0.02),
        'sgu_w_out': nrm((nA, SGU_WIDTH, D), SGU_WIDTH ** -0.5),
        'rwkv_mu': jax.random.uniform(next(it), (nB, RWKV_N_LERP, D), jnp.float32),
        'rwkv_w_in': nrm((nB, 4, D, RWKV_WIDTH), D ** -0.5),
        'rwkv_w_lora1': nrm((nB, 2, D, RWKV_DECAY_LORA), D ** -0.5),
        'rwkv_w_lora2': nrm((nB, 2, RWKV_DECAY_LORA, RWKV_WIDTH), 0.5 * RWKV_DECAY_LORA ** -0.5),
        'rwkv_w0': -1.0 + nrm((nB, 2, RWKV_WIDTH), 0.5),
        'rwkv_a_lora1': nrm((nB, 2, D, RWKV_ICLR_LORA), D ** -0.5),
        'rwkv_a_lora2': nrm((nB, 2, RWKV_ICLR_LORA, RWKV_WIDTH), 0.5 * RWKV_ICLR_LORA ** -0.5),
        'rwkv_a0': nrm((nB, 2, RWKV_WIDTH), 0.1),
        'rwkv_k_k': 0.85 + nrm((nB, RWKV_WIDTH), 0.02),
        'rwkv_k_a': 1.0 + nrm((nB, RWKV_WIDTH), 0.02),
        'rwkv_r_k': nrm((nB, RWKV_HEADS, RWKV_HEAD), 0.1),
        'rwkv_ln_gain': 1.0 + nrm((nB, RWKV_WIDTH), 0.02),
        'rwkv_ln_bias': nrm((nB, RWKV_WIDTH), 0.02),
        'rwkv_w_out': nrm((nB, RWKV_WIDTH, D), RWKV_WIDTH ** -0.5),
        'mla_w_in': nrm((nC, D, MLA_Q_RANK + MLA_KV_RANK + MLA_ROPE + MLA_WIDTH), D ** -0.5),
        'mla_q_norm': 1.0 + nrm((nC, MLA_Q_RANK), 0.02),
        'mla_kv_norm': 1.0 + nrm((nC, MLA_KV_RANK), 0.02),
        'mla_w_uq': nrm((nC, MLA_Q_RANK, MLA_HEADS * MLA_QK_DIM), MLA_Q_RANK ** -0.5),
        'mla_w_ukv': nrm((nC, MLA_KV_RANK, MLA_HEADS * (MLA_NOPE + MLA_VDIM)), MLA_KV_RANK ** -0.5),
        'mla_qk_gain_q': 1.0 + nrm((nC, MLA_QK_DIM), 0.02),
        'mla_qk_gain_k': 1.0 + nrm((nC, MLA_QK_DIM), 0.02),
        'mla_w_out': nrm((nC, MLA_WIDTH, D), MLA_WIDTH ** -0.5),
    }

def second_block(x, c, ctx, c_ctx, ada_w, ada_b, sgu_w_in, sgu_gain, sgu_w_s, sgu_b_s, sgu_w_out,
              rwkv_mu, rwkv_w_in, rwkv_w_lora1, rwkv_w_lora2, rwkv_w0, rwkv_a_lora1, rwkv_a_lora2, rwkv_a0,
              rwkv_k_k, rwkv_k_a, rwkv_r_k, rwkv_ln_gain, rwkv_ln_bias, rwkv_w_out,
              mla_w_in, mla_q_norm, mla_kv_norm, mla_w_uq, mla_w_ukv, mla_qk_gain_q, mla_qk_gain_k, mla_w_out):
    cos, sin = axial_rope_tables(x.shape[1])
    ctx_readers = [i for i in range(DEPTH_2) if i % N_MIXERS != 0]
    last_ctx_reader = ctx_readers[-1] if ctx_readers else -1
    for i in range(DEPTH_2):
        kind, j = i % N_MIXERS, i // N_MIXERS
        update_ctx = i < last_ctx_reader
        shift, scale, gate = ada_modulation(c, ada_w[i], ada_b[i])
        h = rms_norm(x) * (1 + scale) + shift
        if kind != 0 or update_ctx:
            c_shift, c_scale, c_gate = ada_modulation(c_ctx, ada_w[i], ada_b[i])
            hc = rms_norm(ctx) * (1 + c_scale) + c_shift
        if kind == 0:
            sgu_args = (sgu_w_in[j], sgu_gain[j], sgu_w_s[j], sgu_b_s[j], sgu_w_out[j])
            x = x + gate * sgu_mixer(h, *sgu_args)
            if update_ctx:
                ctx = ctx + c_gate * sgu_mixer(hc, *sgu_args)
        elif kind == 1:
            feat_args = (rwkv_mu[j], rwkv_w_in[j], rwkv_w_lora1[j], rwkv_w_lora2[j], rwkv_w0[j],
                         rwkv_a_lora1[j], rwkv_a_lora2[j], rwkv_a0[j], rwkv_k_k[j], rwkv_k_a[j])
            out_args = (rwkv_r_k[j], rwkv_ln_gain[j], rwkv_ln_bias[j], rwkv_w_out[j])
            r_c, w_c, kd_c, v_c, kk_c, a_c, z_c = rwkv7_features(hc, *feat_args)
            state0 = jnp.zeros((2, hc.shape[0], RWKV_HEADS, RWKV_HEAD, RWKV_HEAD), jnp.float32)
            s_ctx, y_c = rwkv7_scan(state0, r_c, w_c, kd_c, v_c, kk_c, a_c, emit=update_ctx)
            r_l, w_l, kd_l, v_l, kk_l, a_l, z_l = rwkv7_features(h, *feat_args)
            _, y_l = rwkv7_scan(s_ctx, r_l, w_l, kd_l, v_l, kk_l, a_l, emit=True)
            x = x + gate * rwkv7_output(y_l, r_l, kd_l, v_l, z_l, *out_args)
            if update_ctx:
                ctx = ctx + c_gate * rwkv7_output(y_c, r_c, kd_c, v_c, z_c, *out_args)
        else:
            mla_args = (mla_w_in[j], mla_q_norm[j], mla_kv_norm[j], mla_w_uq[j], mla_w_ukv[j],
                        mla_qk_gain_q[j], mla_qk_gain_k[j])
            q_c, k_c, v_c, z_c = mla_project(hc, *mla_args, need_q=update_ctx)
            q_l, k_l, v_l, z_l = mla_project(h, *mla_args, need_q=True)
            o_l = mla_latent_attention(q_l, k_l, v_l, k_c, v_c, cos, sin)
            x = x + gate * ((o_l * jax.nn.silu(z_l)) @ mla_w_out[j])
            if update_ctx:
                o_c = mla_context_attention(q_c, k_c, v_c)
                ctx = ctx + c_gate * ((o_c * jax.nn.silu(z_c)) @ mla_w_out[j])
    return x


def setup_inputs(seed=0):
    out = dict(first_inputs(seed))
    for name, value in second_inputs(seed + 1).items():
        if name != "x":
            out[name + "_2"] = value
    return out


def reference(
    x, c, ctx, c_ctx, w_mod, b_mod, norm1_g, norm2_g, w_in, ssd_conv_w, ssd_conv_b, ssd_dt_bias,
    ssd_a_log, ssd_d, ssd_norm_g, w_o_ssd, w_o_att, att_sink, w_out, w_up, ffn_conv_w,
    ffn_conv_b, w_down, final_g, c_2, ctx_2, c_ctx_2, ada_w_2, ada_b_2, sgu_w_in_2, sgu_gain_2,
    sgu_w_s_2, sgu_b_s_2, sgu_w_out_2, rwkv_mu_2, rwkv_w_in_2, rwkv_w_lora1_2, rwkv_w_lora2_2,
    rwkv_w0_2, rwkv_a_lora1_2, rwkv_a_lora2_2, rwkv_a0_2, rwkv_k_k_2, rwkv_k_a_2, rwkv_r_k_2,
    rwkv_ln_gain_2, rwkv_ln_bias_2, rwkv_w_out_2, mla_w_in_2, mla_q_norm_2, mla_kv_norm_2,
    mla_w_uq_2, mla_w_ukv_2, mla_qk_gain_q_2, mla_qk_gain_k_2, mla_w_out_2,
):
    x = first_block(
        x, c, ctx, c_ctx, w_mod, b_mod, norm1_g, norm2_g, w_in, ssd_conv_w, ssd_conv_b,
        ssd_dt_bias, ssd_a_log, ssd_d, ssd_norm_g, w_o_ssd, w_o_att, att_sink, w_out, w_up,
        ffn_conv_w, ffn_conv_b, w_down, final_g,
    )
    return second_block(
        x, c_2, ctx_2, c_ctx_2, ada_w_2, ada_b_2, sgu_w_in_2, sgu_gain_2, sgu_w_s_2, sgu_b_s_2,
        sgu_w_out_2, rwkv_mu_2, rwkv_w_in_2, rwkv_w_lora1_2, rwkv_w_lora2_2, rwkv_w0_2,
        rwkv_a_lora1_2, rwkv_a_lora2_2, rwkv_a0_2, rwkv_k_k_2, rwkv_k_a_2, rwkv_r_k_2,
        rwkv_ln_gain_2, rwkv_ln_bias_2, rwkv_w_out_2, mla_w_in_2, mla_q_norm_2, mla_kv_norm_2,
        mla_w_uq_2, mla_w_ukv_2, mla_qk_gain_q_2, mla_qk_gain_k_2, mla_w_out_2,
    )


_drawn_inputs = setup_inputs


def setup_inputs(seed=0):
    import zlib

    import numpy as np

    out = dict(_drawn_inputs(seed))
    spreads = {}
    factors = {'ctx': 3.501,
     'b_mod': 4.769,
     'norm1_g': 3.985,
     'norm2_g': 3.273,
     'ssd_conv_b': 8.0,
     'ssd_d': 26.944,
     'ssd_norm_g': 6.044,
     'att_sink': 8.0,
     'ffn_conv_b': 8.0,
     'ctx_2': 4.617,
     'c_ctx_2': 2.815,
     'sgu_gain_2': 8.0,
     'sgu_b_s_2': 8.0,
     'rwkv_w_lora1_2': 4.47,
     'rwkv_w_lora2_2': 4.64,
     'rwkv_a0_2': 8.0,
     'rwkv_k_k_2': 8.0,
     'rwkv_k_a_2': 8.0,
     'rwkv_ln_gain_2': 8.0,
     'rwkv_ln_bias_2': 8.0,
     'mla_q_norm_2': 8.0,
     'mla_kv_norm_2': 8.0,
     'mla_w_uq_2': 3.778,
     'mla_qk_gain_q_2': 8.0,
     'mla_qk_gain_k_2': 8.0}
    for name, (base, spread) in spreads.items():
        noise = np.random.default_rng([zlib.crc32(name.encode()), seed]).standard_normal(out[name].shape)
        drawn = base * np.exp(spread * noise) if base else spread * noise
        out[name] = __import__('jax').numpy.asarray(drawn.astype(out[name].dtype))
    for name, factor in factors.items():
        out[name] = (out[name] * factor).astype(out[name].dtype)
    return out
```

```python
from contextlib import ExitStack

import concourse.bass as bass
import numpy as np
from concourse import mybir
from concourse.alu_op_type import AluOpType as ALU

F32 = mybir.dt.float32
ACT = mybir.ActivationFunctionType
AX = mybir.AxisListType

P = 128
D = 1024
KD = D // P
TL, TC = 512, 256
T = TL + TC
NT = T // P
EPS = 1e-6

D_SSD, SSD_HEADS, SSD_P, GROUPS, STATE = 2048, 32, 64, 4, 128
D_BC = GROUPS * STATE
D_XBC = D_SSD + 2 * D_BC
KX, KS = D_XBC // P, D_SSD // P
HEADS, KV, DH = 16, 4, 64
D_Q, D_KV = HEADS * DH, KV * DH
D_FF = 2816
KF = D_FF // P
Z0, XBC0 = 0, D_SSD
DT0 = XBC0 + D_XBC
Q0 = DT0 + 2 * SSD_HEADS
K0 = Q0 + D_Q
V0 = K0 + D_KV
G0 = V0 + D_KV
SGU_W, SGU_G = 2048, 8
KG = SGU_W // P
RH, RW = 16, 64
CH = 64
NC = T // CH
LORA = 64
MH, NOPE, ROPE, VD = 16, 128, 64, 128
QK = NOPE + ROPE
QR, KVR = 768, 256
GRID_W, ROPE_BASE = 64, 10000.0

VEC = [("c", 8), ("c_ctx", 8),
       ("b_mod", 48), ("ada_b", 96), ("norm1_g", 8), ("norm2_g", 8), ("conv_w", 3 * KX), ("conv_b", KX),
       ("ssd_d", KS), ("ssd_g", KS), ("ffn_w", 6 * KF), ("ffn_b", 2 * KF), ("final_g", 8),
       ("dt_bias", 64), ("a_log", 64), ("sink", HEADS),
       ("sgu_gain", 2 * KG), ("mu", 48), ("w0", 16), ("a0", 16), ("k_k", 8), ("k_a", 8), ("r_k", 8),
       ("ln_gain", 8), ("ln_bias", 8), ("q_norm", 6), ("kv_norm", 2),
       ("gq_nope", 1), ("gq_rope", 1), ("gk_nope", 1), ("gk_rope", 1)]
VOFF, _n = {}, 0
for _name, _w in VEC:
    VOFF[_name] = (_n, _w)
    _n += _w
NVEC = _n
CONST = [("ident", P), ("ones", P), ("upto", P), ("from", P), ("after", P), ("before", P), ("pair_ones", P)]
COFF, _n = {}, 0
for _name, _w in CONST:
    COFF[_name] = (_n, _w)
    _n += _w
NCONST = _n

WSLOT = 5120
A_VEC = 0
A_CONST = A_VEC + NVEC
A_MOD1 = A_CONST + NCONST
A_MOD2 = A_MOD1 + 96
A_SIDE = A_MOD2 + 192
A_SMALL = A_SIDE + 6
A_XL = A_SMALL + 512
A_XC = A_XL + KD * TL
A_HL = A_XC + KD * TC
A_HC = A_HL + KD * TL
A_W = A_HC + KD * TC
A_WORK = A_W + 2 * WSLOT
A_END = 53200


def constants():
    i = np.arange(P)
    k, m = i[:, None], i[None, :]
    c = {"ident": k == m, "ones": k >= 0 * m, "upto": k <= m, "from": k >= m, "after": k > m, "before": k < m,
         "pair_ones": (k // RW) == (m // RW)}
    return np.ascontiguousarray(np.concatenate([np.broadcast_to(c[n], (P, P)) for n, _ in CONST], 1).astype(np.float32))


def rope_tables():
    t = np.arange(TL)
    row, col = (t // GRID_W).astype(np.float32), (t % GRID_W).astype(np.float32)
    inv = (ROPE_BASE ** (-np.arange(0, 32, 2, dtype=np.float32) / np.float32(32))).astype(np.float32)
    a = np.zeros((64, TL), np.float32)
    swap = np.zeros((P, P), np.float32)
    for f in range(64):
        a[f] = (row if f < 32 else col) * inv[f % 16]
        half, lo = f % 32, f % 32 < 16
        for h in (0, 64):
            swap[h + (f + 16 if lo else f - 16), h + f] = -1.0 if lo else 1.0
    att = np.stack([np.tile(np.cos(a), (2, 1)), np.tile(np.sin(a), (2, 1))], 1)
    b = np.zeros((P, TL), np.float32)
    mswap = np.zeros((P, P), np.float32)
    for f in range(64):
        i = f % 32
        b[f] = (row if i < 16 else col) * inv[i % 16]
        mswap[(f + 32 if f < 32 else f - 32), f] = -1.0 if f < 32 else 1.0
    mla = np.stack([np.cos(b), np.sin(b)], 1)
    pack = lambda x, s: np.ascontiguousarray(np.concatenate([x.reshape(P, -1), s], 1).astype(np.float32))
    return pack(att, swap), pack(mla, mswap)


def window_mask():
    q, k = np.arange(P)[:, None], np.arange(3 * P)[None, :] - P
    return np.where(np.abs(q - k) <= P, 0.0, -1e30).astype(np.float32)


def tiles(w):
    k, m = w.shape
    return w.reshape(k // P, P, m // P, P).transpose(2, 1, 0, 3).reshape(m // P, P, -1)


def columns(v):
    return v.reshape(-1, P).T


def feature_major(x):
    t, f = x.shape
    return x.reshape(t, f // P, P).transpose(2, 1, 0).reshape(P, -1)


def prepare(inp):
    g = {n: np.asarray(v) for n, v in inp.items()}
    rows = lambda v: np.broadcast_to(v.reshape(1, -1), (P, v.size))
    half = lambda v: np.concatenate([v, v]).reshape(P, 1)
    w_in = g["w_in"][0]
    vec = {
        "c": columns(g["c"][0]), "c_ctx": columns(g["c_ctx"]),
        "b_mod": columns(g["b_mod"][0]), "ada_b": columns(g["ada_b_2"].reshape(-1)),
        "norm1_g": columns(g["norm1_g"][0]), "norm2_g": columns(g["norm2_g"][0]),
        "conv_w": columns(g["ssd_conv_w"][0].reshape(-1)), "conv_b": columns(g["ssd_conv_b"][0]),
        "ssd_d": columns(np.repeat(g["ssd_d"][0], SSD_P)), "ssd_g": columns(g["ssd_norm_g"][0]),
        "ffn_w": columns(g["ffn_conv_w"][0].reshape(-1)), "ffn_b": columns(g["ffn_conv_b"][0]),
        "final_g": columns(g["final_g"]),
        "dt_bias": rows(g["ssd_dt_bias"][0]), "a_log": rows(g["ssd_a_log"][0]), "sink": rows(g["att_sink"][0]),
        "sgu_gain": columns(g["sgu_gain_2"].reshape(-1)), "mu": columns(g["rwkv_mu_2"][0].reshape(-1)),
        "w0": columns(g["rwkv_w0_2"][0].reshape(-1)), "a0": columns(g["rwkv_a0_2"][0].reshape(-1)),
        "k_k": columns(g["rwkv_k_k_2"][0]), "k_a": columns(g["rwkv_k_a_2"][0]), "r_k": columns(g["rwkv_r_k_2"][0].reshape(-1)),
        "ln_gain": columns(g["rwkv_ln_gain_2"][0]), "ln_bias": columns(g["rwkv_ln_bias_2"][0]),
        "q_norm": columns(g["mla_q_norm_2"][0]), "kv_norm": columns(g["mla_kv_norm_2"][0]),
        "gq_nope": g["mla_qk_gain_q_2"][0, :NOPE].reshape(P, 1), "gq_rope": half(g["mla_qk_gain_q_2"][0, NOPE:]),
        "gk_nope": g["mla_qk_gain_k_2"][0, :NOPE].reshape(P, 1), "gk_rope": half(g["mla_qk_gain_k_2"][0, NOPE:]),
    }
    a = {"vec": np.concatenate([vec[n] for n, _ in VEC], 1), "const": constants()}
    a["rope_att"], a["rope_mla"] = rope_tables()
    a["win_mask"] = window_mask()
    a["x_in"] = feature_major(g["x"][0])
    a["ctx1_in"] = feature_major(g["ctx"][0])
    a["ctx2_in"] = feature_major(g["ctx_2"][0])
    four = lambda w: tiles(w).reshape(-1, 4, P, w.shape[0] // P, P).transpose(0, 2, 3, 1, 4).reshape(-1, P, w.shape[0] * 4)
    a["w_mod1"] = four(g["w_mod"][0])
    a["w_mod2"] = np.concatenate([w.T.reshape(-1, P, D) for w in g["ada_w_2"]])
    a["cond_rows2"] = np.concatenate([rows(g["c_2"][0]), rows(g["c_ctx_2"])], 1)
    a["w_xbc"] = tiles(w_in[:, XBC0:DT0])
    ktile = lambda w: w.reshape(w.shape[0] // P, P, -1).transpose(1, 0, 2)
    a["w_dt"] = ktile(w_in[:, DT0:Q0]).reshape(1, P, -1)
    a["w_z"] = tiles(w_in[:, Z0:XBC0])
    qkv = []
    for h in range(KV):
        q = w_in[:, Q0 + h * 256:Q0 + (h + 1) * 256]
        k = w_in[:, K0 + h * DH:K0 + (h + 1) * DH]
        v = w_in[:, V0 + h * DH:V0 + (h + 1) * DH]
        qkv.append(ktile(np.concatenate([q, k, k, v], 1)).reshape(P, -1))
    a["w_qkv"] = np.stack(qkv)
    a["w_merge"] = np.concatenate([tiles(w_in[:, G0:G0 + D]), tiles(g["w_o_ssd"][0]),
                                   tiles(w_in[:, G0 + D:G0 + 2 * D]), tiles(g["w_o_att"][0])], 2)
    a["w_out1"] = tiles(g["w_out"][0])
    up = tiles(g["w_up"][0])
    a["w_up"] = np.concatenate([up[:KF], up[KF:]], 2)
    a["w_down"] = tiles(g["w_down"][0])
    return prepare2(g, a, ktile)


def scan_constants():
    i = np.arange(CH)
    r, c = i[:, None], i[None, :]
    two = lambda a: np.concatenate([a, a], 0).astype(np.float32)
    lo, up = r > c, r < c
    off = lambda s: (r // (2 * s) == c // (2 * s)) & (r // s != c // s)
    starts = np.broadcast_to(np.arange(T) % CH != 0, (P, T)).astype(np.float32)
    masks = [lo, up, r >= c, r <= c, -1.0 * (lo & off(1)), -1.0 * (up & off(1))] + [-1.0 * off(s) for s in (2, 4, 8, 16, 32)] + [r == c]
    return np.ascontiguousarray(np.concatenate([starts] + [two(x) for x in masks], 1))


def prepare2(g, a, ktile):
    a["scan_const"] = scan_constants()
    for j, layer in enumerate((0, 3)):
        w = g["sgu_w_in_2"][j]
        u, v, z = w[:, :SGU_W], w[:, SGU_W:2 * SGU_W], w[:, 2 * SGU_W:]
        a[f"w_sgu_v{layer}"] = np.stack([ktile(v[:, 512 * n:512 * n + 512]).reshape(P, -1) for n in range(4)])
        ws = np.repeat(g["sgu_w_s_2"][j].transpose(0, 2, 1), KG // SGU_G, 0)
        a[f"w_sgu_uz{layer}"] = np.concatenate([tiles(u), tiles(z), ws], 2)
        a[f"sgu_bs{layer}"] = np.broadcast_to(g["sgu_b_s_2"][j].reshape(1, -1), (P, SGU_G * P))
        a[f"w_sgu_out{layer}"] = tiles(g["sgu_w_out_2"][j])
    for n, name in enumerate("rkvz"):
        a["w_rwkv_" + name] = tiles(g["rwkv_w_in_2"][0, n])
    both = lambda w: tiles(np.concatenate([w[0], w[1]], 1))
    a["w_rwkv_lw"], a["w_rwkv_la"] = both(g["rwkv_w_lora1_2"][0]), both(g["rwkv_a_lora1_2"][0])
    second = [w[0].reshape(P, KD, P) for w in (g["rwkv_w_lora2_2"], g["rwkv_a_lora2_2"])]
    a["w_lora2"] = np.stack(second, 2).reshape(1, P, -1)
    a["w_rwkv_out"] = tiles(g["rwkv_w_out_2"][0])
    w = g["mla_w_in_2"][0]
    a["w_mla_q"] = tiles(w[:, :QR])
    a["w_mla_kv"] = tiles(w[:, QR:QR + KVR])
    rope = w[:, QR + KVR:QR + KVR + ROPE]
    a["w_mla_rope"] = tiles(np.concatenate([rope, rope], 1))
    a["w_mla_z"] = tiles(w[:, QR + KVR + ROPE:])
    uq = ktile(g["mla_w_uq_2"][0]).reshape(P, QR // P, MH, QK).transpose(2, 0, 1, 3).reshape(MH, P, -1)
    ukv = ktile(g["mla_w_ukv_2"][0]).reshape(P, KVR // P, MH, NOPE + VD).transpose(2, 0, 1, 3).reshape(MH, P, -1)
    a["w_mla_head"] = np.concatenate([uq, ukv], 2)
    a["w_mla_out"] = tiles(g["mla_w_out_2"][0])
    return a


FIRST_SEM, STAGE_SEMS = 140, 55


class Chip:

    def __init__(self, nc, dram, ctx):
        self.nc, self.dram, self.ctx = nc, dram, ctx
        self.sbuf = ctx.enter_context(nc.sbuf_tensor("sbuf", [P, A_END], F32))
        self.psum = ctx.enter_context(nc.psum_tensor("psum", [P, 8, 512], F32))
        self.stage_done, self.loads_issued = self.lasting("stage_done"), self.lasting("loads_issued")
        self.slot_landed = [self.lasting(f"slot_landed{u}") for u in range(2)]
        self.slot_used = [self.lasting(f"slot_used{u}") for u in range(2)]
        self.n_tiles = 0
        self.n_stages, self.n_sems = 0, [0, 0]

    def lasting(self, name):
        return self.ctx.enter_context(self.nc.semaphore(name))

    def begin_stage(self):
        self.n_stages += 1
        self.n_sems[self.n_stages % 2] = 0
        return self.n_stages - 1

    def sem(self, name):
        turn = self.n_stages % 2
        num = FIRST_SEM + turn * STAGE_SEMS + self.n_sems[turn]
        self.n_sems[turn] += 1
        assert self.n_sems[turn] <= STAGE_SEMS, name
        with self.nc.semaphore(name, num=num) as handle:
            return handle

    def clear_sems(self, pool, n):
        first = FIRST_SEM + (n + 1) % 2 * STAGE_SEMS
        pool.sem_clear(range(first, first + STAGE_SEMS))

    def view(self, at, *shape):
        n = int(np.prod(shape))
        v = self.sbuf[:, at:at + n]
        if len(shape) == 2:
            v = v.rearrange("p (a b) -> p a b", b=shape[1])
        if len(shape) == 3:
            v = v.rearrange("p (a b c) -> p a b c", b=shape[1], c=shape[2])
        return v

    def bank(self, b, n=512, at=0):
        return self.psum[:, b, at:at + n]

    def vec(self, name, col=0, n=None):
        off, w = VOFF[name]
        return self.sbuf[:, A_VEC + off + col:A_VEC + off + col + (w - col if n is None else n)]

    def vec_at(self, name, col):
        off, w = VOFF[name]
        return self.sbuf[:, A_VEC + off:A_VEC + off + w][:, bass.ds(col, 1)]

    def const(self, name):
        off, w = COFF[name]
        return self.sbuf[:, A_CONST + off:A_CONST + off + w]


def one(v, i):
    v = v[:, bass.ds(i, 1)]
    if len(v.shape) == 2:
        return v
    return v.rearrange("p o a -> p (o a)") if len(v.shape) == 3 else v.rearrange("p o a b -> p (o a) b")


def over(v, n):
    return v.unsqueeze(len(v.shape)).broadcast_to(list(v.shape) + [n])


def across(v, n):
    return v.unsqueeze(1).broadcast_to([v.shape[0], n] + list(v.shape[1:]))


class Weights:

    def __init__(self, chip, name, n, words):
        self.chip, self.dram, self.n, self.words = chip, chip.dram[name], n, words
        self.first = chip.n_tiles
        chip.n_tiles += n

    def slot(self, u):
        return (self.first + u) % 2

    def view(self, u, *shape):
        return self.chip.view(A_W + self.slot(u) * WSLOT, *shape)

    def load(self, sp):
        def tile(i, u, src):
            sp.wait_ge(self.chip.slot_used[self.slot(u)], i + (self.first + u) // 2 + 1)
            sp.dma_start(self.view(u, self.words), src).then_inc(self.chip.slot_landed[self.slot(u)], 16)

        if self.n == 1:
            return tile(0, 0, self.dram[0])
        with sp.Fori(0, self.n // 2) as i:
            for u in range(2):
                tile(i, u, self.dram[bass.ds(2 * i + u, 1)].rearrange("o p w -> (o p) w"))

    def landed(self, eng, i, u):
        eng.wait_ge(self.chip.slot_landed[self.slot(u)], 16 * i + 16 * ((self.first + u) // 2 + 1))

    def used(self, u):
        return self.chip.slot_used[self.slot(u)]

    def summed(self, eng, i, u):
        eng.wait_ge(self.chip.slot_used[self.slot(u)], i + (self.first + u) // 2 + 2)


def products(nc, out, pairs):
    last = None
    for n, (w, x) in enumerate(pairs):
        last = nc.tensor.matmul(out, w, x, start=(n == 0), stop=(n == len(pairs) - 1))
    return last


def pairs(eng, n, body):
    if n == 1:
        return body(0, 0)
    with eng.Fori(0, n // 2) as i:
        for u in range(2):
            body(i, u)


class Stage:
    def __init__(self, chip):
        self.chip, self.nc = chip, chip.nc
        self.index = chip.begin_stage()

    def sync(self, sp):
        pass

    def tensor(self, pe):
        pass

    def scalar(self, act):
        pass

    def vector(self, dve):
        pass

    def gpsimd(self, pool):
        pass


class Inputs(Stage):

    def __init__(self, chip):
        super().__init__(chip)
        self.here = chip.sem("inputs_here")

    def sync(self, sp):
        c, d = self.chip, self.chip.dram
        for at, name in ((A_VEC, "vec"), (A_CONST, "const"), (A_XL, "x_in"), (A_XC, "ctx1_in")):
            sp.dma_start(c.view(at, d[name].shape[1]), d[name]).then_inc(self.here, 16)

    def tensor(self, pe):
        pe.wait_ge(self.here, 64)
        for s in self.chip.slot_used:
            pe.sem_inc(s, 1)

    def scalar(self, act):
        act.wait_ge(self.here, 64)

    def vector(self, dve):
        dve.wait_ge(self.here, 64)

    def gpsimd(self, pool):
        pool.wait_ge(self.here, 64)


class NewContext(Stage):

    def __init__(self, chip):
        super().__init__(chip)
        self.here = chip.sem("context_here")

    def sync(self, sp):
        sp.wait_ge(self.chip.stage_done, 4 * self.index)
        sp.dma_start(self.chip.view(A_XC, KD * TC), self.chip.dram["ctx2_in"]).then_inc(self.here, 16)

    def tensor(self, pe):
        pe.wait_ge(self.here, 16)

    def scalar(self, act):
        act.wait_ge(self.here, 16)

    def vector(self, dve):
        dve.wait_ge(self.here, 16)

    def gpsimd(self, pool):
        pool.wait_ge(self.here, 16)


class Modulation(Stage):

    def __init__(self, chip, weights, n, conds, bias, out_at):
        super().__init__(chip)
        self.w = Weights(chip, weights, n, 4 * D)
        self.n, self.conds, self.bias = n, conds, bias
        self.out = chip.view(out_at, 4 * n, 2)
        self.cond = chip.view(A_SMALL, KD, 2)
        self.rows = chip.view(A_WORK, n, 512)[0:2]
        self.cond_ready, self.copied, self.turned = (chip.sem(weights + s) for s in ("_cond", "_copied", "_turned"))

    def sync(self, sp):
        self.w.load(sp)

    def scalar(self, act):
        a = self.nc.scalar
        for n, name in enumerate(self.conds):
            a.activation(self.cond[:, :, n], self.chip.vec(name), ACT.Silu).then_inc(self.cond_ready, 1)
        act.sem_inc(self.copied, 2)

        def body(i, u):
            self.w.summed(act, i, u)
            a.activation(one(self.rows, 2 * i + u), self.chip.bank(u)[0:2], ACT.Copy).then_inc(self.copied, 1)
        pairs(act, self.n, body)

    def tensor(self, pe):
        t = self.nc.tensor
        pe.wait_ge(self.cond_ready, 2)

        def body(i, u):
            self.w.landed(pe, i, u)
            pe.wait_ge(self.copied, 2 * i + u + 1)
            w = self.w.view(u, KD, 512)
            products(self.nc, self.chip.bank(u)[0:2], [(self.cond[:, k], w[:, k]) for k in range(KD)]).then_inc(self.w.used(u), 1)
        pairs(pe, self.n, body)
        pe.wait_ge(self.copied, self.n + 2)
        for m in range(4 * self.n):
            last = t.matmul(self.chip.bank(2, 2, 2 * m), self.rows[:, m // 4, P * (m % 4):P * (m % 4) + P],
                            self.chip.const("ident")[0:2, 0:2], start=True, stop=True)
        last.then_inc(self.turned, 1)

    def vector(self, dve):
        dve.wait_ge(self.turned, 1)
        self.nc.vector.tensor_tensor(self.out, self.chip.bank(2, 8 * self.n).rearrange("p (m c) -> p m c", c=2),
                                     over(self.chip.vec(self.bias), 2), ALU.add)


SIDE = A_END - 5 * D


class SideModulation:
    SLOTS = 3
    BLOCKS = 4 * 3 * KD
    HOSTS = [(((0, 1), (2, 0)), KX // 2), (((1,), (2,)), KS // 2), (((0, 1, 2, 0), (1, 2, 0, 1)), KD // 2)]

    def __init__(self, chip):
        self.chip, self.nc = chip, chip.nc
        self.slot = [chip.view(SIDE + b * D, D) for b in range(self.SLOTS)]
        self.rows = chip.view(SIDE + self.SLOTS * D, 2, D)
        self.products = chip.psum[:, 6:8].rearrange("p b w -> p (b w)")
        self.sums = chip.view(A_SIDE, self.SLOTS, 2)
        self.out = chip.view(A_MOD2, self.BLOCKS, 2)
        self.landed = [chip.lasting(f"side_landed{b}") for b in range(self.SLOTS)]
        self.used = [chip.lasting(f"side_used{b}") for b in range(self.SLOTS)]
        self.rows_in, self.rows_ready = chip.lasting("side_rows_in"), chip.lasting("side_rows_ready")

    def rows_of(self, pool):
        pool.dma_start(self.rows.rearrange("p c k -> p (c k)"), self.chip.dram["cond_rows2"]).then_inc(self.rows_in, 16)

    def silu(self, act, host):
        act.wait_ge(self.rows_in, 16 * host + 16)
        self.nc.scalar.activation(self.rows, self.rows, ACT.Silu).then_inc(self.rows_ready, 1)

    def start(self, dve, host):
        if host == 0:
            for s in self.used:
                dve.sem_inc(s, 1)
        dve.wait_ge(self.rows_ready, host + 1)

    def plan(self, host, i, u):
        uses, block = [0] * self.SLOTS, 0
        for steps, turns in self.HOSTS[:host]:
            for slots in steps:
                block += turns * len(slots)
                for b in slots:
                    uses[b] += turns
        steps = self.HOSTS[host][0]
        turn = steps[0] + steps[1]
        for n, b in enumerate(turn):
            if (n >= len(steps[0])) == (u == 1):
                yield b, i * turn.count(b) + (uses[b] + turn[:n].count(b)), i * len(turn) + (block + n)

    def load(self, pool, host, i, u):
        for b, uses, block in self.plan(host, i, u):
            src = self.chip.dram["w_mod2"][bass.ds(block, 1)].rearrange("o p k -> (o p) k")
            pool.wait_ge(self.used[b], uses + 1)
            pool.dma_start(self.slot[b], src).then_inc(self.landed[b], 16)

    def reduce(self, dve, host, i, u):
        v = self.nc.vector
        for b, uses, block in self.plan(host, i, u):
            dve.drain()
            dve.wait_ge(self.landed[b], uses * 16 + 16)
            for c in range(2):
                last = v.tensor_tensor_reduce(self.products, self.slot[b], self.rows[:, c], 1.0, 0.0, ALU.mult, ALU.add,
                                              self.sums[:, b, c:c + 1])
                if c == 0:
                    dve.drain()
            last.then_inc(self.used[b], 1)
            dve.drain()
            v.tensor_tensor(one(self.out, block), self.sums[:, b], self.chip.vec_at("ada_b", block).broadcast_to([P, 2]), ALU.add)


class Norm(Stage):

    def __init__(self, chip, name, jobs, work):
        super().__init__(chip)
        self.jobs, self.work = jobs, work
        self.squared, self.summed, self.rooted = (chip.sem(f"{name}_{s}") for s in ("squared", "summed", "rooted"))

    def places(self):
        at = self.work
        for n, job in enumerate(self.jobs):
            k, t = job["x"].shape[1:]
            yield job, n, self.chip.view(at, k, t), self.chip.view(at, t), self.chip.view(at + t, t), \
                self.chip.view(A_SMALL + 32 * n, k), k, t
            at += k * t

    def scalar(self, act):
        for job, n, squares, rms, inv, factor, k, t in self.places():
            self.nc.scalar.activation(squares, job["x"], ACT.Square).then_inc(self.squared, 1)
        for job, n, squares, rms, inv, factor, k, t in self.places():
            act.wait_ge(self.summed, n + 1)
            self.nc.scalar.activation(rms, self.chip.bank(n, t), ACT.Sqrt, scale=1.0 / (k * P),
                                      bias=EPS).then_inc(self.rooted, 1)

    def tensor(self, pe):
        for job, n, squares, rms, inv, factor, k, t in self.places():
            pe.wait_ge(self.squared, n + 1)
            products(self.nc, self.chip.bank(n, t), [(self.chip.const("ones"), squares[:, i]) for i in range(k)]
                     ).then_inc(self.summed, 1)

    def vector(self, dve):
        v = self.nc.vector
        for job, n, squares, rms, inv, factor, k, t in self.places():
            if job.get("scale") is None:
                v.tensor_copy(factor, job["gain"])
            elif job.get("gain") is None:
                v.tensor_scalar(factor, job["scale"], 1.0, None, ALU.add)
            else:
                v.scalar_tensor_tensor(factor, job["scale"], 1.0, job["gain"], ALU.add, ALU.mult)
        for job, n, squares, rms, inv, factor, k, t in self.places():
            dve.wait_ge(self.rooted, n + 1)
            v.reciprocal(inv, rms)
            dve.drain()
            v.tensor_tensor(job["out"], job["x"], across(inv, k), ALU.mult)
            dve.drain()
            for i in range(k):
                if job.get("shift") is None:
                    v.tensor_scalar(job["out"][:, i], job["out"][:, i], factor[:, i:i + 1], None, ALU.mult)
                else:
                    v.tensor_scalar(job["out"][:, i], job["out"][:, i], factor[:, i:i + 1], job["shift"][:, i:i + 1],
                                    ALU.mult, ALU.add)


PAD = T + 3
PL, PC = 1, TL + 2
XBC = A_WORK
DT = XBC + KX * T
LA = DT + NT * 64
SSDW = LA + NT * 64


def conv3(nc, dve, acc, raw, w, n):
    nc.vector.tensor_scalar(acc, raw[:, 0:n], w[0], None, ALU.mult)
    dve.drain()
    nc.vector.scalar_tensor_tensor(acc, raw[:, 1:n + 1], w[1], acc, ALU.mult, ALU.add)
    dve.drain()
    return nc.vector.scalar_tensor_tensor(acc, raw[:, 2:n + 2], w[2], acc, ALU.mult, ALU.add)


class Xbc(Stage):

    def __init__(self, chip, side):
        super().__init__(chip)
        self.side = side
        self.w = Weights(chip, "w_xbc", KX, D)
        self.h_lat, self.h_ctx = chip.view(A_HL, KD, TL), chip.view(A_HC, KD, TC)
        self.xbc = chip.view(XBC, KX, T)
        self.raw = [chip.view(SSDW + u * PAD, PAD) for u in range(2)]
        self.acc = [chip.view(SSDW + (2 + u) * PAD, PAD) for u in range(2)]
        self.padded, self.copied, self.convolved, self.activated = (
            chip.sem("xbc_" + s) for s in ("padded", "copied", "convolved", "activated"))

    def sync(self, sp):
        self.w.load(sp)

    def tensor(self, pe):
        with pe.Fori(0, KX // 2) as i:
            for u in range(2):
                self.w.landed(pe, i, u)
                pe.wait_ge(self.copied, 2 * i + u + 1)
                w = self.w.view(u, KD, P)
                products(self.nc, self.chip.bank(2 * u, TL), [(w[:, k], self.h_lat[:, k]) for k in range(KD)])
                products(self.nc, self.chip.bank(2 * u + 1, TC), [(w[:, k], self.h_ctx[:, k]) for k in range(KD)]
                         ).then_inc(self.w.used(u), 1)

    def gpsimd(self, pool):
        self.side.rows_of(pool)
        pairs(pool, KX, lambda i, u: self.side.load(pool, 0, i, u))

    def scalar(self, act):
        a = self.nc.scalar
        self.side.silu(act, 0)
        act.sem_inc(self.copied, 2)
        act.wait_ge(self.padded, 1)
        with act.Fori(0, KX // 2) as i:
            for u in range(2):
                self.w.summed(act, i, u)
                act.wait_ge(self.convolved, 2 * i + u + 1)
                a.activation(self.raw[u][:, PL:PL + TL], self.chip.bank(2 * u, TL), ACT.Copy)
                a.activation(self.raw[u][:, PC:PC + TC], self.chip.bank(2 * u + 1, TC), ACT.Copy
                             ).then_inc(self.copied, 1)
            for u in range(2):
                act.wait_ge(self.convolved, 2 * i + u + 3)
                j = 2 * i + u
                out, b = one(self.xbc, j), self.chip.vec_at("conv_b", j)
                a.activation(out[:, TC:T], self.acc[u][:, 0:TL], ACT.Silu, bias=b)
                a.activation(out[:, 0:TC], self.acc[u][:, PC - 1:PC - 1 + TC], ACT.Silu, bias=b
                             ).then_inc(self.activated, 1)

    def vector(self, dve):
        dve.sem_inc(self.convolved, 2)
        dve.sem_inc(self.activated, 2)
        for u in range(2):
            self.nc.vector.memset(self.raw[u], 0.0)
        dve.drain().then_inc(self.padded, 1)
        self.side.start(dve, 0)
        with dve.Fori(0, KX // 2) as i:
            for u in range(2):
                j = 2 * i + u
                dve.wait_ge(self.copied, j + 3)
                dve.wait_ge(self.activated, j + 1)
                conv3(self.nc, dve, self.acc[u][:, 0:T + 1], self.raw[u],
                      [self.chip.vec_at("conv_w", k * KX + j) for k in range(3)], T + 1).then_inc(self.convolved, 1)
                self.side.reduce(dve, 0, i, u)


class Dt(Stage):

    def __init__(self, chip):
        super().__init__(chip)
        self.w = Weights(chip, "w_dt", 1, KD * 64)
        self.h_lat, self.h_ctx = chip.view(A_HL, KD, TL), chip.view(A_HC, KD, TC)
        self.dt, self.la = chip.view(DT, NT * 64), chip.view(LA, NT * 64)
        self.y, self.s, self.s2, self.q = (chip.view(SSDW + n * NT * 64, NT * 64) for n in range(4))
        self.decay = chip.view(SSDW + 4 * NT * 64, 64)
        self.steps = [chip.sem(f"dt_{s}") for s in ("biased", "exp", "decay")]

    def sync(self, sp):
        self.w.load(sp)

    def tensor(self, pe):
        self.w.landed(pe, 0, 0)
        w = self.w.view(0, KD, 64)
        for t in range(NT):
            h, at = (self.h_ctx, t * P) if t < 2 else (self.h_lat, (t - 2) * P)
            last = products(self.nc, self.chip.bank(0, 64, 64 * t), [(h[:, k, at:at + P], w[:, k]) for k in range(KD)])
        last.then_inc(self.w.used(0), 1)

    def scalar(self, act):
        biased, expd, decay = self.steps
        self.nc.scalar.activation(self.decay, self.chip.vec("a_log"), ACT.Exp).then_inc(decay, 1)
        act.wait_ge(biased, 1)
        self.nc.scalar.activation(self.y, self.dt, ACT.Abs)
        act.drain()
        self.nc.scalar.activation(self.y, self.y, ACT.Exp, scale=-1.0).then_inc(expd, 1)

    def vector(self, dve):
        v = self.nc.vector
        biased, expd, decay = self.steps
        self.w.summed(dve, 0, 0)
        v.tensor_tensor(self.dt.rearrange("p (t h) -> p t h", h=64), self.chip.bank(0, NT * 64).rearrange("p (t h) -> p t h", h=64),
                        across(self.chip.vec("dt_bias"), NT), ALU.add).then_inc(biased, 1)
        dve.wait_ge(expd, 1)
        v.tensor_scalar(self.s, self.y, 2.0, None, ALU.add)
        dve.drain()
        v.reciprocal(self.s, self.s)
        dve.drain()
        v.tensor_tensor(self.s, self.s, self.y, ALU.mult)
        dve.drain()
        v.tensor_tensor(self.s2, self.s, self.s, ALU.mult)
        dve.drain()
        v.tensor_scalar(self.q, self.s2, 1.0 / 17, None, ALU.mult)
        for n in (15, 13, 11, 9, 7, 5, 3):
            dve.drain()
            v.scalar_tensor_tensor(self.q, self.q, 1.0 / n, self.s2, ALU.add, ALU.mult)
        dve.drain()
        v.scalar_tensor_tensor(self.q, self.q, 1.0, self.s, ALU.add, ALU.mult)
        v.tensor_scalar(self.dt, self.dt, 0.0, None, ALU.max)
        dve.drain()
        v.scalar_tensor_tensor(self.dt, self.q, 2.0, self.dt, ALU.mult, ALU.add)
        dve.wait_ge(decay, 1)
        dve.drain()
        v.scalar_tensor_tensor(self.la.rearrange("p (t h) -> p t h", h=64), self.dt.rearrange("p (t h) -> p t h", h=64),
                               -1.0, across(self.decay, NT), ALU.mult, ALU.mult)


HB = A_HL


def meet(eng, sem, i):
    eng.drain().then_inc(sem, 1)
    eng.wait_ge(sem, 4 * i + 4)


class SsdStates(Stage):
    STEPS = 5

    def __init__(self, chip):
        super().__init__(chip)
        self.xbc, self.dt, self.la = chip.view(XBC, KX, T), chip.view(DT, NT, 64), chip.view(LA, NT, 64)
        self.chunk = chip.view(HB, 20, P)
        self.xw = chip.view(HB + 20 * P, 4, 512)
        self.b_tok = chip.view(HB + 36 * P, 4, P)
        self.state = [chip.view(SSDW + d * D_SSD, 4, 512) for d in range(2)]
        self.weight = chip.view(A_SMALL, 32)
        self.decay = chip.view(A_SMALL + 32, 64)
        (self.met, self.staged, self.turned, self.decayed, self.weighted, self.evac, self.b_out,
         self.summed, self.updated, self.stored, self.zeroed) = (
            chip.sem("states_" + n) for n in "met staged turned decayed weighted evac b_out summed updated stored zeroed".split())

    def chunks(self, i, d, late):
        return i if d == 0 else i * -1 + (7 if late else 1)

    def passes(self, eng, body):
        for late, (a, b) in enumerate(((0, 2), (2, self.STEPS))):
            with eng.Fori(a, b) as i:
                for d in range(2):
                    body(i, d, self.chunks(i, d, late), 2 * i + d)

    def sync(self, sp):
        def body(i, d, c, n):
            sp.wait_ge(self.updated, 4 * n + 4)
            sp.dma_start(self.chip.dram["states"][bass.ds(n, 1)].rearrange("o p w -> (o p) w"),
                         self.state[d].rearrange("p g w -> p (g w)")).then_inc(self.stored, 16)
        self.passes(sp, body)
        sp.wait_ge(self.stored, 16 * 2 * self.STEPS + 16)

    def scalar(self, act):
        a = self.nc.scalar

        def body(i, d, c, n):
            meet(act, self.met, n)
            a.activation(self.chunk[:, 8:20], self.xbc[:, 8:20, bass.ds(c * P, P)], ACT.Copy).then_inc(self.staged, 1)
            act.wait_ge(self.decayed, n + 1)
            a.activation(self.decay, self.chip.bank(5, 64), ACT.Exp).then_inc(self.weighted, 1)
            act.wait_ge(self.turned, 5 * n + 5)
            a.activation(self.b_tok.rearrange("p g w -> p (g w)"), self.chip.bank(4), ACT.Copy).then_inc(self.b_out, 1)
        self.passes(act, body)

    def gpsimd(self, pool):
        def body(i, d, c, n):
            meet(pool, self.met, n)
            self.nc.gpsimd.tensor_copy(self.chunk[:, 0:8], self.xbc[:, 0:8, bass.ds(c * P, P)]).then_inc(self.staged, 1)
        self.passes(pool, body)

    def tensor(self, pe):
        t = self.nc.tensor
        ident = self.chip.const("ident")

        def body(i, d, c, n):
            meet(pe, self.met, n)
            la = one(self.la, c)[:, 32 * d:32 * d + 32]
            t.matmul(self.chip.bank(5, 32), self.chip.const("after" if d == 0 else "before"), la, start=True, stop=True)
            t.matmul(self.chip.bank(5, 32, 32), self.chip.const("ones"), la, start=True, stop=True).then_inc(self.decayed, 1)
            pe.wait_ge(self.staged, 2 * n + 2)
            for m in range(20):
                last = t.transpose(self.chip.bank(m // 4, P, P * (m % 4)), self.chunk[:, m], ident)
                if m % 4 == 3:
                    last.then_inc(self.turned, 1)
            pe.wait_ge(self.b_out, n + 1)
            for g in range(GROUPS):
                pe.wait_ge(self.evac, 4 * n + g + 1)
                t.matmul(self.chip.bank(g), self.b_tok[:, g], self.xw[:, g], start=True, stop=True).then_inc(self.summed, 1)
        self.passes(pe, body)

    def vector(self, dve):
        v = self.nc.vector
        for d in range(2):
            v.memset(self.state[d], 0.0)

        def body(i, d, c, n):
            meet(dve, self.met, n)
            dve.wait_ge(self.weighted, n + 1)
            v.tensor_tensor(self.weight, self.decay[:, 0:32], one(self.dt, c)[:, 32 * d:32 * d + 32], ALU.mult)
            dve.drain()
            for g in range(GROUPS):
                dve.wait_ge(self.turned, 5 * n + g + 1)
                v.tensor_tensor(self.xw[:, g].rearrange("p (h e) -> p h e", e=SSD_P),
                                self.chip.bank(g).rearrange("p (h e) -> p h e", e=SSD_P),
                                over(self.weight[:, 8 * g:8 * g + 8], SSD_P), ALU.mult).then_inc(self.evac, 1)
            dve.wait_ge(self.stored, 16 * n + 16)
            for g in range(GROUPS):
                s = self.state[d][:, g].rearrange("p (h e) -> p h e", e=SSD_P)
                v.tensor_tensor(s, s, over(self.decay[:, 32 + 8 * g:40 + 8 * g], SSD_P), ALU.mult)
                dve.drain()
                dve.wait_ge(self.summed, 4 * n + g + 1)
                v.tensor_tensor(self.state[d][:, g], self.state[d][:, g], self.chip.bank(g), ALU.add).then_inc(self.updated, 1)
        dve.sem_inc(self.stored, 16)
        self.passes(dve, body)


class SsdOutput(Stage):

    def __init__(self, chip):
        super().__init__(chip)
        self.xbc, self.dt, self.la = chip.view(XBC, KX, T), chip.view(DT, NT, 64), chip.view(LA, NT, 64)
        self.chunk = chip.view(HB, KX, P)
        self.x_dt = [chip.view(HB + 24 * P, D_SSD), chip.view(SSDW, D_SSD)]
        self.cb = [chip.view(HB + 40 * P + 512 * d, 4, P) for d in range(2)]
        self.state = [chip.view(SSDW + (1 + d) * D_SSD, D_SSD) for d in range(2)]
        at = SSDW + 3 * D_SSD
        self.c_dec = [chip.view(at + 512 * b, 4, P) for b in range(2)]
        self.m = [chip.view(at + 1024 + 512 * b, 4, P) for b in range(2)]
        self.la_here = chip.view(A_SMALL, 64)
        self.dt_here = chip.view(A_SMALL + 64, 64)
        self.cum = chip.view(A_SMALL + 128, 64)
        (self.met, self.staged, self.states_in, self.turned, self.scaled, self.bc, self.masked,
         self.cum_sum, self.cum_out, self.spread, self.grown, self.cut, self.exped, self.decayed_m,
         self.decayed_c, self.multiplied, self.evac) = (
            chip.sem("ssd_" + n) for n in (
                "met staged states_in turned scaled bc masked cum_sum cum_out spread grown cut exped "
                "decayed_m decayed_c multiplied evac").split())
        self.zero = chip.view(A_SMALL + 192, P)

    def y_bank(self, q, m):
        return self.chip.bank((6, 0)[q % 2] + m, P)

    def sync(self, sp):
        sp.wait_ge(self.chip.stage_done, 4 * self.index)
        with sp.Fori(0, 4) as i:
            sp.wait_ge(self.met, 4 * i + 4)
            for d in range(2):
                n = 2 * i + 2 if d == 0 else i * -2 + 9
                sp.dma_start(self.state[d], self.chip.dram["states"][bass.ds(n, 1)].rearrange("o p w -> (o p) w")
                             ).then_inc(self.states_in, 16)

    def gpsimd(self, pool):
        g = self.nc.gpsimd
        with pool.Fori(0, 4) as i:
            meet(pool, self.met, i)
            g.tensor_copy(self.la_here, one(self.la, i + 2))
            g.tensor_copy(self.dt_here, one(self.dt, i + 2))
            g.tensor_copy(self.chunk[:, 0:8], self.xbc[:, 0:8, bass.ds(i * P + 2 * P, P)]).then_inc(self.staged, 1)
            pool.wait_ge(self.masked, 2 * i + 2)
            for s in range(16):
                q, d = s // 2, s % 2
                pool.wait_ge(self.exped, 16 * i + s + 1)
                m = self.m[s % 2]
                g.tensor_tensor(m, m, across(self.cb[d][:, q // 2], 4), ALU.mult).then_inc(self.decayed_m, 1)

    def scalar(self, act):
        a = self.nc.scalar
        with act.Fori(0, 4) as i:
            meet(act, self.met, i)
            a.activation(self.chunk[:, 8:KX], self.xbc[:, 8:KX, bass.ds(i * P + 2 * P, P)], ACT.Copy).then_inc(self.staged, 1)
            act.wait_ge(self.cum_sum, i + 1)
            a.activation(self.cum, self.chip.bank(5, 64), ACT.Copy).then_inc(self.cum_out, 1)
            for s in range(16):
                act.wait_ge(self.cut, 16 * i + s + 1)
                if s >= 2:
                    act.wait_ge(self.multiplied, 16 * i + s - 1)
                a.activation(self.c_dec[s % 2].rearrange("p h l -> p (h l)"), self.chip.bank(4 + s % 2), ACT.Exp
                             ).then_inc(self.grown, 1)
                a.activation(self.m[s % 2], self.m[s % 2], ACT.Exp).then_inc(self.exped, 1)

    def tensor(self, pe):
        t = self.nc.tensor
        c = self.chip
        with pe.Fori(0, 4) as i:
            meet(pe, self.met, i)
            pe.wait_ge(self.staged, 2 * i + 2)
            for m in range(16):
                last = t.transpose(c.bank(m // 4, P, P * (m % 4)), self.chunk[:, m], c.const("ident"))
                if m % 4 == 3:
                    last.then_inc(self.turned, 1)
            for g in range(GROUPS):
                last = t.matmul(c.bank(4, P, P * g), self.chunk[:, 16 + g], self.chunk[:, 20 + g], start=True, stop=True)
            last.then_inc(self.bc, 1)
            t.matmul(c.bank(5, 32), c.const("upto"), self.la_here[:, 0:32], start=True, stop=True)
            t.matmul(c.bank(5, 32, 32), c.const("from"), self.la_here[:, 32:64], start=True, stop=True).then_inc(self.cum_sum, 1)
            pe.wait_ge(self.masked, 2 * i + 2)
            pe.wait_ge(self.cum_out, i + 1)

            def spread(s):
                q, d = s // 2, s % 2
                if s >= 2:
                    pe.wait_ge(self.grown, 16 * i + s - 1)
                for h in range(4):
                    col = 32 * d + 4 * q + h
                    last = t.matmul(c.bank(4 + s % 2, P, P * h), self.la_here[:, col:col + 1].broadcast_to([P, P]),
                                    c.const("upto" if d == 0 else "from"), start=True, stop=True)
                last.then_inc(self.spread, 1)

            spread(0)
            pe.wait_ge(self.states_in, 32 * i + 32)
            pe.wait_ge(self.scaled, 8 * i + 8)
            for s in range(16):
                q, d = s // 2, s % 2
                if s + 1 < 16:
                    spread(s + 1)
                pe.wait_ge(self.decayed_m, 16 * i + s + 1)
                pe.wait_ge(self.decayed_c, 16 * i + s + 1)
                if q >= 2 and d == 0:
                    pe.wait_ge(self.evac, 8 * i + q - 1)
                for h in range(4):
                    head = 4 * q + h
                    out = self.y_bank(q, h // 2)[64 * (h % 2):64 * (h % 2) + 64]
                    t.matmul(out, self.x_dt[d][:, 64 * head:64 * head + 64], self.m[s % 2][:, h], start=(d == 0), stop=False)
                    last = t.matmul(out, self.state[d][:, 64 * head:64 * head + 64], self.c_dec[s % 2][:, h],
                                    start=False, stop=(d == 1))
                last.then_inc(self.multiplied, 1)

    def vector(self, dve):
        v = self.nc.vector
        c = self.chip
        v.memset(self.zero, 0.0)
        with dve.Fori(0, 4) as i:
            meet(dve, self.met, i)
            dve.wait_ge(self.staged, 2 * i + 2)
            for g in range(GROUPS):
                dve.wait_ge(self.turned, 4 * i + g + 1)
                for d in range(2):
                    v.tensor_tensor(self.x_dt[d][:, 512 * g:512 * g + 512].rearrange("p (h e) -> p h e", e=SSD_P),
                                    c.bank(g).rearrange("p (h e) -> p h e", e=SSD_P),
                                    over(self.dt_here[:, 32 * d + 8 * g:32 * d + 8 * g + 8], SSD_P), ALU.mult
                                    ).then_inc(self.scaled, 1)
            dve.wait_ge(self.bc, i + 1)
            for d, mask in enumerate(("upto", "from")):
                v.tensor_tensor(self.cb[d], c.bank(4).rearrange("p (g l) -> p g l", l=P), across(c.const(mask), 4), ALU.mult
                                ).then_inc(self.masked, 1)
            dve.wait_ge(self.cum_out, i + 1)

            def out(q):
                dve.wait_ge(self.multiplied, 16 * i + 2 * q + 2)
                for m in range(2):
                    tile = 2 * q + m
                    last = v.scalar_tensor_tensor(self.xbc[:, tile, bass.ds(i * P + 2 * P, P)], self.chunk[:, tile],
                                                  c.vec("ssd_d", tile, 1), self.y_bank(q, m), ALU.mult, ALU.add)
                last.then_inc(self.evac, 1)

            for s in range(16):
                q, d = s // 2, s % 2
                dve.wait_ge(self.spread, 16 * i + s + 1)
                if s >= 2:
                    dve.wait_ge(self.multiplied, 16 * i + s - 1)
                for h in range(4):
                    col = 32 * d + 4 * q + h
                    last = v.scalar_tensor_tensor(self.m[s % 2][:, h], c.bank(4 + s % 2, P, P * h), self.cum[:, col:col + 1],
                                                  self.zero, ALU.subtract, ALU.min)
                last.then_inc(self.cut, 1)
                dve.wait_ge(self.grown, 16 * i + s + 1)
                v.tensor_tensor(self.c_dec[s % 2], self.c_dec[s % 2], across(self.chunk[:, 20 + q // 2], 4), ALU.mult
                                ).then_inc(self.decayed_c, 1)
                if d == 0 and q >= 1:
                    out(q - 1)
            out(7)


class GateZ(Stage):

    def __init__(self, chip, side):
        super().__init__(chip)
        self.side = side
        self.w = Weights(chip, "w_z", KS, D)
        self.h = chip.view(A_HL, KD, TL)
        self.y = chip.view(XBC, KX, T)
        self.z = [chip.view(SSDW + u * TL, TL) for u in range(2)]
        self.activated, self.used = chip.sem("z_activated"), chip.sem("z_used")

    def sync(self, sp):
        self.w.load(sp)

    def gpsimd(self, pool):
        self.side.rows_of(pool)
        pairs(pool, KS, lambda i, u: self.side.load(pool, 1, i, u))

    def tensor(self, pe):
        with pe.Fori(0, KS // 2) as i:
            for u in range(2):
                self.w.landed(pe, i, u)
                pe.wait_ge(self.activated, 2 * i + u + 1)
                w = self.w.view(u, KD, P)
                products(self.nc, self.chip.bank(u), [(w[:, k], self.h[:, k]) for k in range(KD)]).then_inc(self.w.used(u), 1)

    def scalar(self, act):
        self.side.silu(act, 1)
        act.sem_inc(self.activated, 2)
        with act.Fori(0, KS // 2) as i:
            for u in range(2):
                self.w.summed(act, i, u)
                act.wait_ge(self.used, 2 * i + u + 1)
                self.nc.scalar.activation(self.z[u], self.chip.bank(u), ACT.Silu).then_inc(self.activated, 1)

    def vector(self, dve):
        dve.sem_inc(self.used, 2)
        self.side.start(dve, 1)
        with dve.Fori(0, KS // 2) as i:
            for u in range(2):
                dve.wait_ge(self.activated, 2 * i + u + 3)
                y = one(self.y, 2 * i + u)[:, TC:T]
                self.nc.vector.tensor_tensor(y, y, self.z[u], ALU.mult).then_inc(self.used, 1)
                self.side.reduce(dve, 1, i, u)


ATT = A_WORK + KS * T
Y_ATT = ATT


class Attention(Stage):

    def __init__(self, chip):
        super().__init__(chip)
        self.w = Weights(chip, "w_qkv", KV, KD * 448)
        self.h_lat, self.h_ctx = chip.view(A_HL, KD, TL), chip.view(A_HC, KD, TC)
        self.y = chip.view(Y_ATT, KD, TL)
        at = ATT + KD * TL
        self.tables = chip.view(at, 2 * TL + P)
        self.cos, self.sin = chip.view(at, TL), chip.view(at + TL, TL)
        self.swap = chip.view(at + 2 * TL, P)
        at += 2 * TL + P
        self.mask = chip.view(at, 3 * P)
        at += 3 * P
        self.k = chip.view(at, T)
        at += T
        self.v = chip.view(at, NT, DH)
        at += NT * DH
        self.raw = [chip.view(at + n * TL, TL) for n in range(3)]
        at += 3 * TL
        self.q = [chip.view(at + n * TL, TL) for n in range(2)]
        at += 2 * TL
        self.s = chip.view(at, 4, 640)
        at += 4 * 640
        self.pt = chip.view(at, 5, 512)
        small = A_SMALL
        self.mx, self.neg, self.den, self.es, self.inv = (chip.view(small + 4 * n, 4) for n in range(5))
        (self.tables_in, self.projected, self.copied, self.swapped, self.rotated, self.values_out,
         self.scored, self.masked, self.peaked, self.exped, self.normed, self.turned, self.pt_out,
         self.summed, self.out, self.cosined, self.ctx_out) = (
            chip.sem("att_" + n) for n in (
                "tables_in projected copied swapped rotated values_out scored masked peaked exped normed "
                "turned pt_out summed out cosined ctx_out").split())

    @staticmethod
    def window(n):
        a, b = max(0, n - 1) * P, min(4, n + 2) * P
        return a, b - a

    def key_tiles(self, n):
        a, w = self.window(n)
        return [2 + a // P + m for m in range(w // P)] + [0, 1]

    PT_PER = sum([4, 5, 5, 4])

    def body(self, eng, run):
        with eng.Fori(0, KV // 2) as i:
            for u in range(2):
                run(i, u, 2 * i + u)

    def sync(self, sp):
        sp.wait_ge(self.chip.stage_done, 4 * self.index)
        sp.dma_start(self.tables, self.chip.dram["rope_att"]).then_inc(self.tables_in, 16)
        sp.dma_start(self.mask, self.chip.dram["win_mask"]).then_inc(self.tables_in, 16)
        self.w.load(sp)

    def tensor(self, pe):
        t, c = self.nc.tensor, self.chip
        pe.wait_ge(self.tables_in, 32)

        def run(i, u, g):
            w = self.w.view(u, KD, 448)
            self.w.landed(pe, i, u)
            pe.wait_ge(self.out, 4 * g + 4)
            products(self.nc, c.bank(0), [(w[:, k, 256:384], self.h_lat[:, k]) for k in range(KD)]).then_inc(self.projected, 1)
            for m in range(2):
                products(self.nc, c.bank(1 + m), [(w[:, k, P * m:P * m + P], self.h_lat[:, k]) for k in range(KD)]
                         ).then_inc(self.projected, 1)
            products(self.nc, c.bank(3, TC), [(w[:, k, 256:384], self.h_ctx[:, k]) for k in range(KD)]).then_inc(self.projected, 1)
            for m in range(NT):
                h, at = (self.h_ctx, m * P) if m < 2 else (self.h_lat, (m - 2) * P)
                last = products(self.nc, c.bank(4, DH, DH * m), [(h[:, k, at:at + P], w[:, k, 384:448]) for k in range(KD)])
            last.then_inc(self.w.used(u), 1)
            for n in range(3):
                pe.wait_ge(self.copied, 3 * g + n + 1)
                t.matmul(c.bank(5 + n), self.swap, self.raw[n], start=True, stop=True).then_inc(self.swapped, 1)
            pe.wait_ge(self.rotated, 4 * g + 4)
            pe.wait_ge(self.values_out, g + 1)
            for n in range(4):
                a, width = self.window(n)
                for h in range(4):
                    half = slice(64 * (h % 2), 64 * (h % 2) + 64)
                    if n > 0 or h >= 2:
                        pe.wait_ge(self.masked, 16 * g + 4 * n + h - 1)
                        pe.wait_ge(self.ctx_out, 16 * g + 4 * n + h - 1)
                    q = self.q[h // 2][half, P * n:P * n + P]
                    t.matmul(c.bank(2 * (h % 2), width), q, self.k[half, TC + a:TC + a + width], start=True, stop=True)
                    t.matmul(c.bank(2 * (h % 2) + 1, TC), q, self.k[half, 0:TC], start=True, stop=True).then_inc(self.scored, 1)
                pe.wait_ge(self.normed, 4 * g + n + 1)
                done = sum([4, 5, 5, 4][:n])
                for j, tile in enumerate(self.key_tiles(n)):
                    x = done + j
                    if x >= 2:
                        pe.wait_ge(self.pt_out, self.PT_PER * g + x - 1)
                    for h in range(4):
                        last = t.transpose(c.bank(4 + x % 2, P, P * h), self.s[:, h, P * j:P * j + P], c.const("ident"))
                    last.then_inc(self.turned, 1)
                if n > 0:
                    pe.wait_ge(self.out, 4 * g + n + 4)
                for j, tile in enumerate(self.key_tiles(n)):
                    pe.wait_ge(self.pt_out, self.PT_PER * g + done + j + 1)
                    p = self.pt[:, j].rearrange("p (m e q) -> p m e q", e=2, q=P)
                    for e in range(2):
                        last = t.matmul(c.bank(6, 2 * P)[64 * e:64 * e + 64], self.v[:, tile], p[:, :, e],
                                        start=(j == 0), stop=(j == len(self.key_tiles(n)) - 1))
                last.then_inc(self.summed, 1)

        self.body(pe, run)

    def scalar(self, act):
        a, c = self.nc.scalar, self.chip

        def run(i, u, g):
            for n in range(3):
                act.wait_ge(self.projected, 4 * g + n + 1)
                a.activation(self.raw[n], c.bank(n), ACT.Copy).then_inc(self.copied, 1)
            act.wait_ge(self.projected, 4 * g + 4)
            a.activation(self.k[:, 0:TC], c.bank(3, TC), ACT.Copy).then_inc(self.rotated, 1)
            self.w.summed(act, i, u)
            a.activation(self.v.rearrange("p t e -> p (t e)"), c.bank(4, NT * DH), ACT.Copy).then_inc(self.values_out, 1)
            for n in range(4):
                start, width = self.window(n)
                for h in range(4):
                    act.wait_ge(self.scored, 16 * g + 4 * n + h + 1)
                    a.activation(self.s[:, h, width:width + TC], c.bank(2 * (h % 2) + 1, TC), ACT.Copy).then_inc(self.ctx_out, 1)
                act.wait_ge(self.peaked, 4 * g + n + 1)
                for h in range(4):
                    s = self.s[:, h, 0:width + TC]
                    a.activation(s, s, ACT.Exp, bias=self.neg[:, h:h + 1], scale=DH ** -0.5, accum_out=self.den[:, h:h + 1])
                a.activation(self.es, self.es, ACT.Exp).then_inc(self.exped, 1)
                done = sum([4, 5, 5, 4][:n])
                for j in range(0, len(self.key_tiles(n)), 2):
                    act.wait_ge(self.turned, self.PT_PER * g + done + j + 1)
                    if j:
                        act.wait_ge(self.pt_out, self.PT_PER * g + done + j)
                    a.activation(self.pt[:, j], c.bank(4 + (done + j) % 2), ACT.Copy).then_inc(self.pt_out, 1)

        self.body(act, run)

    def gpsimd(self, pool):
        g_ = self.nc.gpsimd
        pool.wait_ge(self.tables_in, 32)

        def run(i, u, g):
            for n in range(3):
                pool.wait_ge(self.copied, 3 * g + n + 1)
                pool.wait_ge(self.swapped, 3 * g + n + 1)
                g_.tensor_tensor(self.raw[n], self.raw[n], self.cos, ALU.mult).then_inc(self.cosined, 1)

        self.body(pool, run)

    def vector(self, dve):
        v, c = self.nc.vector, self.chip
        dve.wait_ge(self.tables_in, 32)
        dve.sem_inc(self.out, 4)

        def run(i, u, g):
            for n in range(3):
                to = self.k[:, TC:T] if n == 0 else self.q[n - 1]
                dve.wait_ge(self.swapped, 3 * g + n + 1)
                v.tensor_tensor(to, c.bank(5 + n), self.sin, ALU.mult)
                dve.drain()
                dve.wait_ge(self.cosined, 3 * g + n + 1)
                v.tensor_tensor(to, to, self.raw[n], ALU.add).then_inc(self.rotated, 1)
            for n in range(4):
                start, width = self.window(n)
                m0 = P if n == 0 else 0
                for h in range(4):
                    dve.wait_ge(self.scored, 16 * g + 4 * n + h + 1)
                    v.tensor_tensor(self.s[:, h, 0:width], c.bank(2 * (h % 2), width), self.mask[:, m0:m0 + width], ALU.add
                                    ).then_inc(self.masked, 1)
                    dve.wait_ge(self.masked, 16 * g + 4 * n + h + 1)
                    dve.wait_ge(self.ctx_out, 16 * g + 4 * n + h + 1)
                    v.tensor_reduce(self.mx[:, h:h + 1], self.s[:, h, 0:width + TC], AX.X, ALU.max)
                sink = c.vec("sink")[:, bass.ds(4 * g, 4)]
                dve.drain()
                v.scalar_tensor_tensor(self.mx, self.mx, DH ** -0.5, sink, ALU.mult, ALU.max)
                dve.drain()
                v.tensor_scalar(self.neg, self.mx, -1.0, None, ALU.mult)
                v.tensor_tensor(self.es, sink, self.mx, ALU.subtract).then_inc(self.peaked, 1)
                dve.wait_ge(self.exped, 4 * g + n + 1)
                v.tensor_tensor(self.den, self.den, self.es, ALU.add)
                dve.drain()
                v.reciprocal(self.inv, self.den)
                dve.drain()
                for h in range(4):
                    s = self.s[:, h, 0:width + TC]
                    last = v.tensor_scalar(s, s, self.inv[:, h:h + 1], None, ALU.mult)
                last.then_inc(self.normed, 1)
                done = sum([4, 5, 5, 4][:n])
                for j in range(1, len(self.key_tiles(n)), 2):
                    dve.wait_ge(self.turned, self.PT_PER * g + done + j + 1)
                    dve.wait_ge(self.pt_out, self.PT_PER * g + done + j)
                    v.tensor_copy(self.pt[:, j], c.bank(4 + (done + j) % 2)).then_inc(self.pt_out, 1)
                dve.wait_ge(self.summed, 4 * g + n + 1)
                v.tensor_copy(self.y[:, bass.ds(2 * g, 2), P * n:P * n + P], c.bank(6, 2 * P).rearrange("p (m q) -> p m q", q=P)
                              ).then_inc(self.out, 1)

        self.body(dve, run)


class Merge(Stage):

    def __init__(self, chip):
        super().__init__(chip)
        self.w = Weights(chip, "w_merge", KD, 40 * P)
        self.h = chip.view(A_HL, KD, TL)
        self.y_ssd, self.y_att = chip.view(XBC, KX, T), chip.view(Y_ATT, KD, TL)
        at = ATT + KD * TL
        self.out = chip.view(at, KD, TL)
        at += KD * TL
        self.gates = [[chip.view(at + (2 * u + n) * TL, TL) for n in range(2)] for u in range(2)]
        self.gated, self.merged = chip.sem("merge_gated"), chip.sem("merge_merged")
        self.gate_sums = chip.sem("merge_gate_sums")

    def sync(self, sp):
        self.w.load(sp)

    def tensor(self, pe):
        with pe.Fori(0, KD // 2) as i:
            for u in range(2):
                self.w.landed(pe, i, u)
                pe.wait_ge(self.merged, 2 * i + u + 1)
                w = self.w.view(u, 40, P)
                bank = [self.chip.bank(4 * u + n) for n in range(4)]
                products(self.nc, bank[0], [(w[:, k], self.h[:, k]) for k in range(KD)])
                products(self.nc, bank[1], [(w[:, 24 + k], self.h[:, k]) for k in range(KD)]).then_inc(self.gate_sums, 1)
                products(self.nc, bank[2], [(w[:, 8 + k], self.y_ssd[:, k, TC:T]) for k in range(KS)])
                products(self.nc, bank[3], [(w[:, 32 + k], self.y_att[:, k]) for k in range(KD)]).then_inc(self.w.used(u), 1)

    def scalar(self, act):
        with act.Fori(0, KD // 2) as i:
            for u in range(2):
                act.wait_ge(self.gate_sums, 2 * i + u + 1)
                act.wait_ge(self.merged, 2 * i + u + 1)
                for n in range(2):
                    last = self.nc.scalar.activation(self.gates[u][n], self.chip.bank(4 * u + n), ACT.Sigmoid)
                last.then_inc(self.gated, 1)

    def vector(self, dve):
        v = self.nc.vector
        dve.sem_inc(self.merged, 2)
        with dve.Fori(0, KD // 2) as i:
            for u in range(2):
                dve.wait_ge(self.gated, 2 * i + u + 1)
                self.w.summed(dve, i, u)
                for n in range(2):
                    v.tensor_tensor(self.gates[u][n], self.gates[u][n], self.chip.bank(4 * u + 2 + n), ALU.mult)
                dve.drain()
                v.tensor_tensor(one(self.out, 2 * i + u), self.gates[u][0], self.gates[u][1], ALU.add).then_inc(self.merged, 1)


class Residual(Stage):

    def __init__(self, chip, name, kt, y, gate, y_ctx=None, gate_ctx=None, side=None):
        super().__init__(chip)
        self.w = Weights(chip, name, KD, kt * P)
        self.kt, self.side = kt, side
        self.parts = [(chip.view(A_XL, KD, TL), y, gate, TL)]
        if y_ctx is not None:
            self.parts.append((chip.view(A_XC, KD, TC), y_ctx, gate_ctx, TC))
        self.added = chip.sem(name + "_added")

    def sync(self, sp):
        self.w.load(sp)

    def gpsimd(self, pool):
        if self.side:
            self.side.rows_of(pool)
            pairs(pool, KD, lambda i, u: self.side.load(pool, 2, i, u))

    def scalar(self, act):
        if self.side:
            self.side.silu(act, 2)

    def tensor(self, pe):
        with pe.Fori(0, KD // 2) as i:
            for u in range(2):
                self.w.landed(pe, i, u)
                pe.wait_ge(self.added, 2 * i + u + 1)
                w = self.w.view(u, self.kt, P)
                for n, (x, y, gate, t) in enumerate(self.parts):
                    last = products(self.nc, self.chip.bank(2 * u + n, t), [(w[:, k], y(k)) for k in range(self.kt)])
                last.then_inc(self.w.used(u), 1)

    def vector(self, dve):
        dve.sem_inc(self.added, 2)
        if self.side:
            self.side.start(dve, 2)
        with dve.Fori(0, KD // 2) as i:
            for u in range(2):
                self.w.summed(dve, i, u)
                j = 2 * i + u
                for n, (x, y, gate, t) in enumerate(self.parts):
                    last = self.nc.vector.scalar_tensor_tensor(one(x, j), self.chip.bank(2 * u + n, t), gate[:, bass.ds(j, 1)],
                                                               one(x, j), ALU.mult, ALU.add)
                last.then_inc(self.added, 1)
                if self.side:
                    self.side.reduce(dve, 2, i, u)


FFN_G = A_WORK
FPAD = TL + 2


class FfnUp(Stage):

    def __init__(self, chip):
        super().__init__(chip)
        self.w = Weights(chip, "w_up", KF, 2 * D)
        self.h = chip.view(A_HL, KD, TL)
        self.g = chip.view(FFN_G, KF, TL)
        at = FFN_G + KF * TL
        self.raw = [[chip.view(at + (2 * u + n) * FPAD, FPAD) for n in range(2)] for u in range(2)]
        at += 4 * FPAD
        self.acc = [[chip.view(at + (2 * u + n) * TL, TL) for n in range(2)] for u in range(2)]
        self.padded, self.copied, self.convolved, self.activated, self.gated = (
            chip.sem("ffn_" + s) for s in ("padded", "copied", "convolved", "activated", "gated"))

    def sync(self, sp):
        self.w.load(sp)

    def tensor(self, pe):
        with pe.Fori(0, KF // 2) as i:
            for u in range(2):
                self.w.landed(pe, i, u)
                pe.wait_ge(self.copied, 2 * i + u + 1)
                w = self.w.view(u, 2, KD, P)
                for n in range(2):
                    last = products(self.nc, self.chip.bank(2 * u + n), [(w[:, n, k], self.h[:, k]) for k in range(KD)])
                last.then_inc(self.w.used(u), 1)

    def scalar(self, act):
        a = self.nc.scalar
        act.sem_inc(self.copied, 2)
        act.wait_ge(self.padded, 1)
        with act.Fori(0, KF // 2) as i:
            for u in range(2):
                self.w.summed(act, i, u)
                act.wait_ge(self.convolved, 2 * i + u + 1)
                for n in range(2):
                    last = a.activation(self.raw[u][n][:, 1:1 + TL], self.chip.bank(2 * u + n), ACT.Copy)
                last.then_inc(self.copied, 1)
            for u in range(2):
                act.wait_ge(self.convolved, 2 * i + u + 3)
                a.activation(self.acc[u][0], self.acc[u][0], ACT.Silu, bias=self.chip.vec_at("ffn_b", 2 * i + u)
                             ).then_inc(self.activated, 1)

    def vector(self, dve):
        v = self.nc.vector
        dve.sem_inc(self.convolved, 2)
        dve.sem_inc(self.gated, 2)
        for u in range(2):
            for n in range(2):
                v.memset(self.raw[u][n], 0.0)
        dve.drain().then_inc(self.padded, 1)
        with dve.Fori(0, KF // 2) as i:
            for u in range(2):
                j = 2 * i + u
                dve.wait_ge(self.copied, j + 3)
                dve.wait_ge(self.gated, j + 1)
                for n in range(2):
                    last = conv3(self.nc, dve, self.acc[u][n], self.raw[u][n],
                                 [self.chip.vec_at("ffn_w", 2 * KF * k + KF * n + j) for k in range(3)], TL)
                last.then_inc(self.convolved, 1)
            for u in range(2):
                j = 2 * i + u
                dve.wait_ge(self.activated, j + 1)
                dve.wait_ge(self.convolved, j + 3)
                v.scalar_tensor_tensor(one(self.g, j), self.acc[u][1], self.chip.vec_at("ffn_b", j + KF), self.acc[u][0],
                                       ALU.add, ALU.mult).then_inc(self.gated, 1)


class Store(Stage):

    def __init__(self, chip):
        super().__init__(chip)
        self.stored = chip.sem("stored")

    def sync(self, sp):
        sp.wait_ge(self.chip.stage_done, 4 * self.index)
        sp.dma_start(self.chip.dram["out"], self.chip.view(A_XL, KD * TL)).then_inc(self.stored, 16)
        sp.wait_ge(self.stored, 16)


def block1(chip):
    mod = chip.view(A_MOD1, 48, 2)
    x_lat, x_ctx = chip.view(A_XL, KD, TL), chip.view(A_XC, KD, TC)
    h_lat, h_ctx = chip.view(A_HL, KD, TL), chip.view(A_HC, KD, TC)
    part = lambda n, who: mod[:, 8 * n:8 * n + 8, who]
    g1, g2 = chip.vec("norm1_g"), chip.vec("norm2_g")
    job_lat = dict(x=x_lat, out=h_lat, gain=g1, scale=part(1, 0), shift=part(0, 0))
    job_ctx = dict(x=x_ctx, out=h_ctx, gain=g1, scale=part(1, 1), shift=part(0, 1))
    y = chip.view(XBC, KX, T)[:, 0:KS, TC:T]
    merged = chip.view(ATT + KD * TL, KD, TL)
    g = chip.view(FFN_G, KF, TL)
    side = SideModulation(chip)
    return [
        Inputs(chip),
        Modulation(chip, "w_mod1", 12, ("c", "c_ctx"), "b_mod", A_MOD1),
        Norm(chip, "norm_in", [job_lat, job_ctx], A_WORK),
        Xbc(chip, side), Dt(chip), SsdStates(chip), SsdOutput(chip),
        Norm(chip, "norm_again", [job_lat, job_ctx], SSDW),
        GateZ(chip, side),
        Norm(chip, "norm_ssd", [dict(x=y, out=y, gain=chip.vec("ssd_g"))], SSDW),
        Attention(chip), Merge(chip),
        Residual(chip, "w_out1", KD, lambda k: merged[:, k], part(2, 0)),
        Norm(chip, "norm_ffn", [dict(x=x_lat, out=h_lat, gain=g2, scale=part(4, 0), shift=part(3, 0))], A_WORK),
        FfnUp(chip),
        Residual(chip, "w_down", KF, lambda k: g[:, k], part(5, 0), side=side),
        Norm(chip, "norm_out", [dict(x=x_lat, out=x_lat, gain=chip.vec("final_g"))], A_WORK),
    ]


SGU_V = A_WORK


class SguValues(Stage):

    def __init__(self, chip, layer, nt):
        super().__init__(chip)
        self.nt = nt
        self.w = Weights(chip, f"w_sgu_v{layer}", 4, 4 * D)
        self.h_lat, self.h_ctx = chip.view(A_HL, KD, TL), chip.view(A_HC, KD, TC)
        self.v = chip.view(SGU_V, KG, nt, P)
        self.junk = chip.view(SGU_V + KG * T, 4, P)
        self.sums = chip.view(A_SMALL, 4, nt)
        self.activated, self.summed = chip.sem(f"sgu{layer}_v"), chip.sem(f"sgu{layer}_v_summed")

    def sync(self, sp):
        self.w.load(sp)

    def tensor(self, pe):
        def body(i, u):
            self.w.landed(pe, i, u)
            w = self.w.view(u, KD, 512)
            for t in range(self.nt):
                h, at = (self.h_lat, t * P) if t < 4 else (self.h_ctx, (t - 4) * P)
                x = u * self.nt + t
                pe.wait_ge(self.activated, 2 * self.nt * i + x + 1)
                last = products(self.nc, self.chip.bank(x % 4), [(h[:, k, at:at + P], w[:, k]) for k in range(KD)])
                if t < self.nt - 1:
                    last.then_inc(self.summed, 1)
            last.then_inc(self.w.used(u), 1)
        pairs(pe, 4, body)

    def scalar(self, act):
        act.sem_inc(self.activated, 4)

        def body(i, u):
            for t in range(self.nt):
                x = u * self.nt + t
                if t < self.nt - 1:
                    act.wait_ge(self.summed, (self.nt - 1) * (2 * i + u) + t + 1)
                else:
                    self.w.summed(act, i, u)
                self.nc.scalar.activation(self.v[:, bass.ds(8 * i + 4 * u, 4), t], self.chip.bank(x % 4).rearrange("p (m f) -> p m f", f=P),
                                          ACT.Gelu_apprx_tanh).then_inc(self.activated, 1)
        pairs(act, 4, body)

    def vector(self, dve):
        def body(i, u):
            for t in range(self.nt):
                v = self.v[:, bass.ds(8 * i + 4 * u, 4), t]
                dve.drain()
                dve.wait_ge(self.activated, 2 * self.nt * i + u * self.nt + t + 5)
                self.nc.vector.tensor_tensor(self.junk, v, v, ALU.mult)
                dve.drain()
                self.nc.vector.tensor_reduce(one(self.sums, 2 * i + u)[:, t:t + 1], self.junk.rearrange("p m f -> p (m f)"), AX.X, ALU.add)
        pairs(dve, 4, body)


class SguMix(Stage):

    def __init__(self, chip, layer, j, nt):
        super().__init__(chip)
        self.nt, self.j, self.layer = nt, j, layer
        t = nt * P
        self.w = Weights(chip, f"w_sgu_uz{layer}", KG, 17 * P)
        self.h = [(chip.view(A_HL, KD, TL), TL, 0), (chip.view(A_HC, KD, TC), TC, TL)][:2 if nt == 6 else 1]
        self.v = chip.view(SGU_V, KG, nt, P)
        self.s = chip.view(SGU_V, KG, t)
        at = SGU_V + KG * T
        self.staged_v = [chip.view(at + u * T, nt, P) for u in range(2)]
        self.u = [chip.view(at + (2 + u) * T, t) for u in range(2)]
        self.z = [chip.view(at + (4 + u) * T, t) for u in range(2)]
        self.tmp = [chip.view(at + (6 + u) * T, t) for u in range(2)]
        self.bs = chip.view(at + 8 * T, SGU_G, P)
        self.sums = chip.view(A_SMALL, 4, nt)
        self.total, self.inv = chip.view(A_SMALL + 32, nt), chip.view(A_SMALL + 40, nt)
        (self.bs_in, self.totalled, self.rooted, self.inverted, self.staged, self.mixed, self.u_done,
         self.activated, self.gated) = (
            chip.sem(f"sgu{layer}_{n}") for n in "bs_in totalled rooted inverted staged mixed u_done activated gated".split())

    def banks(self, u):
        return [(self.chip.bank(n + 3 * u), self.chip.bank(*c)) for n, c in enumerate(((7, TC), (6, TC), (6, TC, TC)))]

    def sync(self, sp):
        sp.wait_ge(self.chip.stage_done, 4 * self.index)
        sp.dma_start(self.bs.rearrange("p g q -> p (g q)"), self.chip.dram[f"sgu_bs{self.layer}"]).then_inc(self.bs_in, 16)
        self.w.load(sp)

    def gpsimd(self, pool):
        pool.wait_ge(self.inverted, 1)

        def body(i, u):
            pool.wait_ge(self.gated, 2 * i + u + 1)
            self.nc.gpsimd.tensor_tensor(self.staged_v[u], one(self.v, 2 * i + u), over(self.inv, P), ALU.mult
                                         ).then_inc(self.staged, 1)
        pairs(pool, KG, body)

    def tensor(self, pe):
        def body(i, u):
            j = 2 * i + u
            self.w.landed(pe, i, u)
            w = self.w.view(u, 17, P)
            mix, ub, zb = self.banks(u)
            pe.wait_ge(self.gated, j + 1)
            pe.wait_ge(self.staged, j + 1)
            for t in range(4):
                self.nc.tensor.matmul(mix[0][:, t * P:t * P + P], self.staged_v[u][:, t], w[:, 16], start=True, stop=True)
            for n, b in ((0, ub), (8, zb)):
                products(self.nc, b[0], [(w[:, n + k], self.h[0][0][:, k]) for k in range(KD)]).then_inc(self.u_done, 1)
            if self.nt > 4:
                pe.wait_ge(self.gated, j + 2)
                for t in range(4, self.nt):
                    self.nc.tensor.matmul(mix[1][:, (t - 4) * P:(t - 3) * P], self.staged_v[u][:, t], w[:, 16], start=True, stop=True)
                for n, b in ((0, ub), (8, zb)):
                    products(self.nc, b[1], [(w[:, n + k], self.h[1][0][:, k]) for k in range(KD)])
            pe.drain().then_inc(self.w.used(u), 1)
        pairs(pe, KG, body)

    def scalar(self, act):
        a = self.nc.scalar
        act.wait_ge(self.totalled, 1)
        a.activation(self.total, self.total, ACT.Sqrt, scale=1.0 / SGU_W, bias=EPS).then_inc(self.rooted, 1)

        def body(i, u):
            mix, ub, zb = self.banks(u)
            self.w.summed(act, i, u)
            act.wait_ge(self.gated, 2 * i + u + 1)
            for n, (_, t, at) in enumerate(self.h):
                a.activation(self.u[u][:, at:at + t], ub[n], ACT.Gelu_apprx_tanh)
            for n, (_, t, at) in enumerate(self.h):
                last = a.activation(self.z[u][:, at:at + t], zb[n], ACT.Silu)
            last.then_inc(self.activated, 1)
        pairs(act, KG, body)

    def vector(self, dve):
        v = self.nc.vector
        v.tensor_reduce(self.total, self.sums.rearrange("p c t -> p t c"), AX.X, ALU.add).then_inc(self.totalled, 1)
        dve.wait_ge(self.rooted, 1)
        v.reciprocal(self.inv, self.total).then_inc(self.inverted, 1)
        dve.wait_ge(self.bs_in, 16)
        dve.sem_inc(self.gated, 2)

        def body(i, u):
            mix, ub, zb = self.banks(u)
            self.w.summed(dve, i, u)
            dve.wait_ge(self.gated, 2 * i + u + 1)
            for n, (_, t, at) in enumerate(self.h):
                c = t // P
                v.scalar_tensor_tensor(self.tmp[u][:, at:at + t].rearrange("p (c q) -> p c q", q=P), mix[n].rearrange("p (c q) -> p c q", q=P),
                                       self.chip.vec_at("sgu_gain", KG * self.j + 2 * i + u),
                                       across(one(self.bs, i), c), ALU.mult, ALU.add)
            dve.drain()
            dve.wait_ge(self.activated, 2 * i + u + 1)
            v.tensor_tensor(self.tmp[u], self.tmp[u], self.u[u], ALU.mult)
            dve.drain()
            v.tensor_tensor(one(self.s, 2 * i + u), self.tmp[u], self.z[u], ALU.mult).then_inc(self.gated, 1)
        pairs(dve, KG, body)


def modulated(chip, layer, n):
    m = chip.view(A_MOD2, 96, 2)
    return [m[:, 24 * layer + 8 * n:24 * layer + 8 * n + 8, who] for who in range(2)]


def norm2(chip, layer, ctx):
    lat = dict(x=chip.view(A_XL, KD, TL), out=chip.view(A_HL, KD, TL), shift=modulated(chip, layer, 0)[0], scale=modulated(chip, layer, 1)[0])
    con = dict(x=chip.view(A_XC, KD, TC), out=chip.view(A_HC, KD, TC), shift=modulated(chip, layer, 0)[1], scale=modulated(chip, layer, 1)[1])
    return Norm(chip, f"norm_layer{layer}", [lat, con] if ctx else [lat], A_WORK)


def sgu_layer(chip, layer, j, nt):
    s = chip.view(SGU_V, KG, nt * P)
    gate = modulated(chip, layer, 2)
    ctx = (lambda k: s[:, k, TL:T], gate[1]) if nt == 6 else (None, None)
    return [norm2(chip, layer, nt == 6), SguValues(chip, layer, nt), SguMix(chip, layer, j, nt),
            Residual(chip, f"w_sgu_out{layer}", KG, lambda k: s[:, k, 0:TL], gate[0], *ctx)]


class Project(Stage):

    def __init__(self, chip, name, n, parts, out):
        super().__init__(chip)
        self.w = Weights(chip, name, n, D)
        self.n, self.parts, self.out = n, parts, out
        self.copied = chip.sem(name + "_copied")

    def sync(self, sp):
        self.w.load(sp)

    def tensor(self, pe):
        def body(i, u):
            self.w.landed(pe, i, u)
            pe.wait_ge(self.copied, 2 * i + u + 1)
            w = self.w.view(u, KD, P)
            for n, (x, t, at) in enumerate(self.parts):
                last = products(self.nc, self.chip.bank(2 * u + n, t), [(w[:, k], x[:, k]) for k in range(KD)])
            last.then_inc(self.w.used(u), 1)
        pairs(pe, self.n, body)

    def scalar(self, act):
        act.sem_inc(self.copied, 2)

        def body(i, u):
            self.w.summed(act, i, u)
            out = one(self.out, 2 * i + u) if self.n > 1 else self.out[:, 0]
            for n, (x, t, at) in enumerate(self.parts):
                last = self.nc.scalar.activation(out[:, at:at + t], self.chip.bank(2 * u + n, t), ACT.Copy)
            last.then_inc(self.copied, 1)
        pairs(act, self.n, body)


CQ = A_WORK
CKV = CQ + 6 * TL
KROPE = CKV + 2 * T
O_MLA = KROPE + T
MLAW = O_MLA + MH * TL


class Mla(Stage):
    WORDS = 6 * QK + 2 * (NOPE + VD)

    def __init__(self, chip):
        super().__init__(chip)
        self.w = Weights(chip, "w_mla_head", MH, self.WORDS)
        self.cq, self.ckv = chip.view(CQ, 6, TL), chip.view(CKV, 2, T)
        self.k_rope = chip.view(KROPE, T)
        self.o = chip.view(O_MLA, MH, TL)
        at = MLAW
        self.tables = chip.view(at, 2 * TL + P)
        self.cos, self.sin, self.swap = chip.view(at, TL)[0:64], chip.view(at + TL, TL)[0:64], chip.view(at + 2 * TL, P)[0:64]
        at += 2 * TL + P
        self.sq_rope = chip.view(at, T)[0:64]
        at += T
        spare = [A_W + u * WSLOT + self.WORDS for u in range(2)]
        assert max(4 * T, 4 * TL) <= WSLOT - self.WORDS
        q_at, k_at = (at, spare[1]), (at + 3 * TL, spare[0])
        self.qn = [chip.view(x, TL) for x in q_at]
        self.qr = [chip.view(x + TL, TL)[0:64] for x in q_at]
        self.q_rot = [chip.view(x + 2 * TL, TL)[0:64] for x in q_at]
        self.kn = [chip.view(x, T) for x in k_at]
        self.kr = [chip.view(x + T, T)[0:64] for x in k_at]
        self.v = [chip.view(x + 2 * T, NT, VD) for x in k_at]
        self.iq, self.ik = chip.view(spare[1] + 3 * TL, TL), chip.view(spare[0] + 3 * T, T)
        at += 3 * TL + 3 * T
        self.sq_qn, self.sq_qr, self.sq_kn = chip.view(at, TL), chip.view(at + TL, TL)[0:64], chip.view(at + 2 * TL, T)
        at += 2 * TL + T
        self.p = [chip.view(at, T), chip.view(at + T, T)]
        at += 2 * T
        self.pt = chip.view(at, NT, TL)
        at += NT * TL
        assert at <= A_END, at
        self.mx, self.neg, self.den, self.inv = (chip.view(A_SMALL + 4 * n, 4) for n in range(4))
        (self.tables_in, self.shared, self.raw, self.squared, self.ssq, self.rooted, self.q_ready, self.turned,
         self.values_out, self.scored, self.peaked, self.exped, self.normed, self.p_turned, self.pt_out, self.summed,
         self.out, self.shared_turned) = (
            chip.sem("mla_" + n) for n in (
                "tables_in shared raw squared ssq rooted q_ready turned values_out scored peaked exped normed "
                "p_turned pt_out summed out shared_turned").split())

    def s_bank(self, n):
        return self.wide(2 * (n % 2))

    def wide(self, b):
        return self.chip.psum[:, b:b + 2].rearrange("p b w -> p (b w)")[:, 0:T]

    def sync(self, sp):
        sp.wait_ge(self.chip.stage_done, 4 * self.index)
        sp.dma_start(self.tables, self.chip.dram["rope_mla"]).then_inc(self.tables_in, 16)
        self.w.load(sp)

    def heads(self, eng, prepare, attend):
        prepare(0, 0, 0)
        with eng.Fori(0, MH // 2 - 1) as i:
            for u in range(2):
                attend(2 * i + u, u, lambda: prepare(i + u, 1 - u, 2 * i + u + 1))
        attend(MH - 2, 0, lambda: prepare(MH // 2 - 1, 1, MH - 1))
        attend(MH - 1, 1, None)

    def tensor(self, pe):
        t, c = self.nc.tensor, self.chip
        pe.wait_ge(self.tables_in, 16)
        pe.wait_ge(self.shared, 1)
        t.matmul(c.bank(7), self.swap, self.k_rope[0:64, 0:TL], start=True, stop=True).then_inc(self.shared_turned, 1)
        ones = c.const("ones")

        def prepare(i, u, h):
            self.w.landed(pe, i, u)
            words = self.w.view(u, self.WORDS)
            wq = words[:, 0:6 * QK].rearrange("p (k m) -> p k m", m=QK)
            wkv = words[:, 6 * QK:].rearrange("p (k m) -> p k m", m=NOPE + VD)
            products(self.nc, c.bank(0), [(wq[:, k, 0:NOPE], self.cq[:, k]) for k in range(6)])
            products(self.nc, c.bank(1)[0:64], [(wq[:, k, NOPE:QK], self.cq[:, k]) for k in range(6)]).then_inc(self.raw, 1)
            for b, a, n in ((2, 0, TL), (3, TL, TC)):
                last = products(self.nc, c.bank(b, n), [(wkv[:, k, 0:NOPE], self.ckv[:, k, a:a + n]) for k in range(2)])
            last.then_inc(self.raw, 1)
            pe.wait_ge(self.squared, 2 * h + 1)
            pe.wait_ge(self.out, h + 1)
            t.matmul(c.bank(6), ones, self.sq_qn, start=True, stop=False)
            t.matmul(c.bank(6), ones[0:64], self.sq_qr, start=False, stop=True).then_inc(self.ssq, 1)
            for m in range(NT):
                last = products(self.nc, c.bank(4 + m // 4, VD, VD * (m % 4)),
                                [(self.ckv[:, k, P * m:P * m + P], wkv[:, k, NOPE:]) for k in range(2)])
            last.then_inc(self.w.used(u), 1)
            pe.wait_ge(self.squared, 2 * h + 2)
            pe.wait_ge(self.values_out, h + 1)
            for b, a, n in ((4, 0, TL), (5, TL, TC)):
                t.matmul(c.bank(b, n), ones, self.sq_kn[:, a:a + n], start=True, stop=False)
                last = t.matmul(c.bank(b, n), ones[0:64], self.sq_rope[:, a:a + n], start=False, stop=True)
            last.then_inc(self.ssq, 1)
            if isinstance(h, int) and h == 0:
                swap(h, u)

        def swap(h, u):
            pe.wait_ge(self.q_ready, 3 * h + 4)
            t.matmul(c.bank(7), self.swap, self.qr[u], start=True, stop=True).then_inc(self.turned, 1)

        def attend(h, u, ahead):
            if ahead:
                ahead()
            pe.wait_ge(self.q_ready, 3 * h + 6)
            pe.wait_ge(self.rooted, 2 * h + (4 if ahead else 2))
            for n in range(4):
                if n >= 2:
                    pe.wait_ge(self.exped, 4 * h + n - 1)
                q = slice(P * n, P * n + P)
                s = self.s_bank(n)
                for a, w, rot in ((0, TL, self.q_rot[u]), (TL, TC, self.qr[u])):
                    t.matmul(s[:, a:a + w], self.qn[u][:, q], self.kn[u][:, a:a + w], start=True, stop=False)
                    last = t.matmul(s[:, a:a + w], rot[:, q], self.kr[u][:, a:a + w], start=False, stop=True)
                last.then_inc(self.scored, 1)
                if n >= 1:
                    self.turn(pe, h, n - 1)
                if n == 2 and ahead:
                    swap(h + 1, 1 - u)
            self.turn(pe, h, 3)
            pe.wait_ge(self.pt_out, 4 * h + 4)
            products(self.nc, c.bank(6), [(self.v[u][:, m], self.pt[:, m]) for m in range(NT)]).then_inc(self.summed, 1)

        self.heads(pe, prepare, attend)

    def turn(self, pe, h, n):
        pe.wait_ge(self.normed, 4 * h + n + 1)
        if n >= 1:
            pe.wait_ge(self.pt_out, 4 * h + n)
        for m in range(NT):
            last = self.nc.tensor.transpose(self.chip.bank(4 + m // 4, P, P * (m % 4)), self.p[n % 2][:, P * m:P * m + P], self.chip.const("ident"))
        last.then_inc(self.p_turned, 1)

    def scalar(self, act):
        a, c = self.nc.scalar, self.chip

        def prepare(i, u, h):
            act.wait_ge(self.raw, 2 * h + 1)
            act.wait_ge(self.q_ready, 3 * h + 1)
            a.activation(self.sq_qn, c.bank(0), ACT.Square)
            a.activation(self.sq_qr, c.bank(1)[0:64], ACT.Square).then_inc(self.squared, 1)
            a.activation(self.qn[u], c.bank(0), ACT.Copy)
            a.activation(self.qr[u], c.bank(1)[0:64], ACT.Copy)
            act.wait_ge(self.raw, 2 * h + 2)
            act.wait_ge(self.q_ready, 3 * h + 2)
            a.activation(self.sq_kn, self.wide(2), ACT.Square).then_inc(self.squared, 1)
            a.activation(self.kn[u], self.wide(2), ACT.Copy)
            self.w.summed(act, i, u)
            a.activation(self.v[u].rearrange("p t e -> p (t e)"), self.wide(4), ACT.Copy).then_inc(self.values_out, 1)
            act.wait_ge(self.ssq, 2 * h + 1)
            a.activation(self.sq_qn, c.bank(6), ACT.Sqrt, scale=1.0 / QK, bias=EPS).then_inc(self.rooted, 1)
            act.wait_ge(self.ssq, 2 * h + 2)
            a.activation(self.sq_kn, self.wide(4), ACT.Sqrt, scale=1.0 / QK, bias=EPS).then_inc(self.rooted, 1)

        def attend(h, u, ahead):
            if ahead:
                ahead()
            for n in range(4):
                act.wait_ge(self.peaked, 4 * h + n + 1)
                if n >= 2:
                    act.wait_ge(self.p_turned, 4 * h + n - 1)
                a.activation(self.p[n % 2], self.s_bank(n), ACT.Exp, bias=self.neg[:, n:n + 1], scale=QK ** -0.5,
                             accum_out=self.den[:, n:n + 1]).then_inc(self.exped, 1)
                if n >= 1:
                    self.out_turned(act, h, n - 1)
            self.out_turned(act, h, 3)

        self.heads(act, prepare, attend)

    def out_turned(self, act, h, n):
        act.wait_ge(self.p_turned, 4 * h + n + 1)
        self.nc.scalar.activation(self.pt[:, :, P * n:P * n + P], self.wide(4).rearrange("p (m q) -> p m q", q=P), ACT.Copy
                                  ).then_inc(self.pt_out, 1)

    def vector(self, dve):
        v, c = self.nc.vector, self.chip
        dve.wait_ge(self.tables_in, 16)
        dve.sem_inc(self.out, 2)
        dve.sem_inc(self.q_ready, 3)
        kr = self.k_rope[0:64]
        v.tensor_tensor(self.sq_rope, kr, kr, ALU.mult)
        dve.drain()
        v.tensor_scalar(kr, kr, c.vec("gk_rope")[0:64], None, ALU.mult).then_inc(self.shared, 1)
        dve.wait_ge(self.shared_turned, 1)
        v.tensor_tensor(self.q_rot[0], c.bank(7)[0:64], self.sin, ALU.mult)
        v.tensor_tensor(kr[:, 0:TL], kr[:, 0:TL], self.cos, ALU.mult)
        dve.drain()
        v.tensor_tensor(kr[:, 0:TL], kr[:, 0:TL], self.q_rot[0], ALU.add)
        dve.drain()

        def queries(h, u):
            dve.drain()
            dve.wait_ge(self.rooted, 2 * h + 1)
            v.reciprocal(self.iq, self.sq_qn)
            dve.drain()
            v.scalar_tensor_tensor(self.qr[u], self.qr[u], c.vec("gq_rope")[0:64], self.iq[0:64], ALU.mult, ALU.mult
                                   ).then_inc(self.q_ready, 1)
            v.scalar_tensor_tensor(self.qn[u], self.qn[u], c.vec("gq_nope"), self.iq, ALU.mult, ALU.mult)

        def key_norms(h, u):
            dve.wait_ge(self.rooted, 2 * h + 2)
            v.reciprocal(self.ik, self.sq_kn)
            dve.drain()

        def keys(h, u):
            v.scalar_tensor_tensor(self.kn[u], self.kn[u], c.vec("gk_nope"), self.ik, ALU.mult, ALU.mult)
            v.tensor_tensor(self.kr[u], kr, self.ik[0:64], ALU.mult).then_inc(self.q_ready, 1)

        def rotate(h, u):
            dve.wait_ge(self.turned, h + 1)
            v.tensor_tensor(self.q_rot[u], c.bank(7)[0:64], self.sin, ALU.mult)
            v.tensor_tensor(self.iq[0:64], self.qr[u], self.cos, ALU.mult)
            dve.drain()
            v.tensor_tensor(self.q_rot[u], self.q_rot[u], self.iq[0:64], ALU.add).then_inc(self.q_ready, 1)

        parts = (queries, key_norms, keys, rotate)

        def prepare(i, u, h):
            for part in parts:
                part(h, u)

        def attend(h, u, ahead):
            for n in range(4):
                if ahead:
                    parts[n](h + 1, 1 - u)
                dve.wait_ge(self.scored, 4 * h + n + 1)
                v.tensor_reduce(self.mx[:, n:n + 1], self.s_bank(n), AX.X, ALU.max)
                dve.drain()
                v.tensor_scalar(self.neg[:, n:n + 1], self.mx[:, n:n + 1], -QK ** -0.5, None, ALU.mult).then_inc(self.peaked, 1)
                self.normalise(dve, h, n)
            dve.wait_ge(self.summed, h + 1)
            v.tensor_copy(one(self.o, h), c.bank(6)).then_inc(self.out, 1)

        self.heads(dve, prepare, attend)

    def normalise(self, dve, h, n):
        v = self.nc.vector
        dve.wait_ge(self.exped, 4 * h + n + 1)
        v.reciprocal(self.inv[:, n:n + 1], self.den[:, n:n + 1])
        dve.drain()
        v.tensor_scalar(self.p[n % 2], self.p[n % 2], self.inv[:, n:n + 1], None, ALU.mult).then_inc(self.normed, 1)


class GateO(Stage):

    def __init__(self, chip):
        super().__init__(chip)
        self.w = Weights(chip, "w_mla_z", MH, D)
        self.h = chip.view(A_HL, KD, TL)
        self.y = chip.view(O_MLA, MH, TL)
        self.z = [chip.view(MLAW + u * TL, TL) for u in range(2)]
        self.activated, self.used = chip.sem("mla_z_activated"), chip.sem("mla_z_used")

    def sync(self, sp):
        self.w.load(sp)

    def tensor(self, pe):
        def body(i, u):
            self.w.landed(pe, i, u)
            pe.wait_ge(self.activated, 2 * i + u + 1)
            w = self.w.view(u, KD, P)
            products(self.nc, self.chip.bank(u), [(w[:, k], self.h[:, k]) for k in range(KD)]).then_inc(self.w.used(u), 1)
        pairs(pe, MH, body)

    def scalar(self, act):
        act.sem_inc(self.activated, 2)

        def body(i, u):
            self.w.summed(act, i, u)
            act.wait_ge(self.used, 2 * i + u + 1)
            self.nc.scalar.activation(self.z[u], self.chip.bank(u), ACT.Silu).then_inc(self.activated, 1)
        pairs(act, MH, body)

    def vector(self, dve):
        dve.sem_inc(self.used, 2)

        def body(i, u):
            dve.wait_ge(self.activated, 2 * i + u + 3)
            y = one(self.y, 2 * i + u)
            self.nc.vector.tensor_tensor(y, y, self.z[u], ALU.mult).then_inc(self.used, 1)
        pairs(dve, MH, body)


def mla_layer(chip, layer):
    h_lat, h_ctx = chip.view(A_HL, KD, TL), chip.view(A_HC, KD, TC)
    both = [(h_lat, TL, 0), (h_ctx, TC, TL)]
    cq, ckv = chip.view(CQ, 6, TL), chip.view(CKV, 2, T)
    o = chip.view(O_MLA, MH, TL)
    kvn = chip.vec("kv_norm")
    return [norm2(chip, layer, True),
            Project(chip, "w_mla_q", 6, both[:1], cq), Project(chip, "w_mla_kv", 2, both, ckv),
            Project(chip, "w_mla_rope", 1, both, chip.view(KROPE, 1, T)),
            Norm(chip, "norm_rank", [dict(x=cq, out=cq, gain=chip.vec("q_norm")), dict(x=ckv[:, :, 0:TL], out=ckv[:, :, 0:TL], gain=kvn),
                                     dict(x=ckv[:, :, TL:T], out=ckv[:, :, TL:T], gain=kvn)], MLAW),
            Mla(chip), GateO(chip),
            Residual(chip, "w_mla_out", MH, lambda k: o[:, k], modulated(chip, layer, 2)[0])]


MIDS = A_WORK
RWKV = MIDS + 2 * T
TERMS = 5
BATCH = 4
BATCHES = NC // BATCH
DECAYS = A_SMALL
LOG_DECAY = float(np.exp(-0.5))


class RwkvFeatures(Stage):
    ORDER = (4, 5, 0, 1, 2, 3)

    def __init__(self, chip):
        super().__init__(chip)
        names = {4: "w_rwkv_lw", 5: "w_rwkv_la", 0: "w_rwkv_r", 1: "w_rwkv_k", 2: "w_rwkv_v", 3: "w_rwkv_z"}
        self.w = {c: Weights(chip, names[c], 1 if c > 3 else KD, D) for c in self.ORDER}
        self.parts = [(chip.view(A_HC, KD, TC), 0, TC), (chip.view(A_HL, KD, TL), TC, TL)]
        at = RWKV
        self.xx = chip.view(at, KD, T)
        self.xs = [chip.view(at + (1 + u) * KD * T, KD, T) for u in range(2)]
        at += 3 * KD * T
        self.out = [chip.view(at + u * T, T) for u in range(2)]
        self.mids = chip.view(MIDS, 2, T)
        self.mixed, self.multiplied, self.copied, self.out_free = (
            chip.sem("rwkv_" + s) for s in ("mixed", "multiplied", "copied", "out_free"))
        self.stored = chip.lasting("rwkv_stored")

    def wide(self, u):
        return self.chip.psum[:, 2 * u:2 * u + 2].rearrange("p b w -> p (b w)")[:, 0:T]

    def sync(self, sp):
        for c in self.ORDER:
            self.w[c].load(sp)

    def before(self, n):
        return sum(self.w[c].n for c in self.ORDER[:n])

    def vector(self, dve):
        v = self.nc.vector
        for h, at, n in self.parts:
            xx = self.xx[:, :, at:at + n]
            v.tensor_tensor(xx[:, :, 1:n - 1], h[:, :, 0:n - 2], h[:, :, 2:n], ALU.add)
            v.tensor_copy(xx[:, :, 0:1], h[:, :, 1:2])
            v.tensor_copy(xx[:, :, n - 1:n], h[:, :, n - 2:n - 1])
        dve.drain()
        for h, at, n in self.parts:
            xx = self.xx[:, :, at:at + n]
            v.scalar_tensor_tensor(xx, xx, 0.5, h, ALU.mult, ALU.subtract)
        dve.drain()
        for n, c in enumerate(self.ORDER):
            if n >= 2:
                dve.wait_ge(self.multiplied, n - 1)
            for k in range(KD):
                for h, at, w in self.parts:
                    last = v.scalar_tensor_tensor(self.xs[n % 2][:, k, at:at + w], self.xx[:, k, at:at + w],
                                                  self.chip.vec("mu", 8 * c + k, 1), h[:, k], ALU.mult, ALU.add)
            last.then_inc(self.mixed, 1)

    def tensor(self, pe):
        for n, c in enumerate(self.ORDER):
            pe.wait_ge(self.mixed, n + 1)
            xs, weights = self.xs[n % 2], self.w[c]

            def body(i, u):
                weights.landed(pe, i, u)
                pe.wait_ge(self.copied, self.before(n) + 2 * i + u + 1)
                w = weights.view(u, KD, P)
                b = (self.before(n) + u) % 2
                for at, width in ((0, TL), (TL, TC)):
                    last = products(self.nc, self.wide(b)[:, at:at + width], [(w[:, k], xs[:, k, at:at + width]) for k in range(KD)])
                last.then_inc(weights.used(u), 1)
            pairs(pe, weights.n, body)
            pe.drain().then_inc(self.multiplied, 1)

    def scalar(self, act):
        a = self.nc.scalar
        act.sem_inc(self.copied, 2)
        act.sem_inc(self.out_free, 2)
        for n, c in enumerate(self.ORDER):
            func = {3: ACT.Silu, 4: ACT.Tanh}.get(c, ACT.Copy)

            def body(i, u):
                self.w[c].summed(act, i, u)
                b = (self.before(n) + u) % 2
                if c > 3:
                    out = self.mids[:, c - 4]
                else:
                    act.wait_ge(self.out_free, self.before(n) - 2 + 2 * i + u + 1)
                    out = self.out[b]
                a.activation(out, self.wide(b), func).then_inc(self.copied, 1)
            pairs(act, self.w[c].n, body)

    def gpsimd(self, pool):
        for n, c in enumerate(self.ORDER):
            if c > 3:
                continue

            def body(i, u):
                pool.wait_ge(self.copied, self.before(n) + 2 * i + u + 3)
                self.nc.gpsimd.dma_start(self.chip.dram["rkvz"][bass.ds(i * 8 + (4 * u + c), 1)].rearrange("o p w -> (o p) w"),
                                         self.out[(self.before(n) + u) % 2]).then_inc(self.stored, 16)
                pool.wait_ge(self.stored, 16 * (self.before(n) - 2) + 32 * i + 16 * u + 16)
                pool.sem_inc(self.out_free, 1)
            pairs(pool, KD, body)


class RwkvTerms(Stage):

    def __init__(self, chip):
        super().__init__(chip)
        self.w = Weights(chip, "w_lora2", 1, KD * 2 * P)
        self.mids = chip.view(MIDS, 2, T)
        at = RWKV
        self.starts, at = chip.view(at, T), at + T
        self.slice, at = chip.view(at, 2, P), at + 2 * P
        self.x = [chip.view(at + u * 4 * T, 4, T) for u in range(2)]
        at += 8 * T
        self.out, at = [chip.view(at + d * TERMS * T, NC, TERMS, CH) for d in range(2)], at + 2 * TERMS * T
        row = lambda n: chip.view(at + n * T, T)
        self.sg, self.a = [row(0), row(1)], [row(2), row(3)]
        self.kk_raw, self.norm, self.kk = row(4), row(5), row(6)
        self.ci, self.ce = [row(7), row(8)], [row(9), row(10)]
        self.kka, self.kd = [row(11), row(12)], [row(13), row(14)]
        assert at + 15 * T <= A_W + 2 * WSLOT + 28164, at
        self.decays = chip.view(DECAYS, KD, 2, NC)
        self.one_minus_ka = chip.view(DECAYS + KD * 2 * NC, KD)
        self.loaded = [chip.sem(f"terms_loaded{u}") for u in range(2)]
        (self.starts_in, self.scaled, self.sliced, self.lora, self.activated, self.raw_done, self.squared,
         self.norm_sum, self.rooted, self.scanned, self.kk_done, self.directed, self.exped, self.weighted,
         self.bonus_sum, self.done, self.stored) = (
            chip.sem("terms_" + n) for n in (
                "starts_in scaled sliced lora activated raw_done squared norm_sum rooted scanned kk_done "
                "directed exped weighted bonus_sum done stored").split())

    def wide(self, q):
        return self.chip.psum[:, 2 * q:2 * q + 2].rearrange("p b w -> p (b w)")[:, 0:T]

    def each(self, eng, body):
        with eng.Fori(0, KD // 2) as i:
            for u in range(2):
                body(2 * i + u, u, i)

    def sync(self, sp):
        d = self.chip.dram
        sp.wait_ge(self.chip.stage_done, 4 * self.index)
        sp.dma_start(self.starts, d["scan_const"][:, 0:T]).then_inc(self.starts_in, 16)
        self.w.load(sp)

        def load(m, u):
            src = (d["rkvz"][bass.ds(4 * m, 4)] if not isinstance(m, int) else d["rkvz"][4 * m:4 * m + 4]).rearrange("c p w -> p c w")
            if not isinstance(m, int):
                sp.wait_ge(self.stored, 80 * m)
            sp.dma_start(self.x[u], src).then_inc(self.loaded[u], 16)

        def store(m, u, i):
            to = d["terms"][bass.ds(3 * m, 3)] if not isinstance(m, int) else d["terms"][3 * m:3 * m + 3]
            bonus = d["bonus"][bass.ds(m, 1)].rearrange("o p w -> (o p) w") if not isinstance(m, int) else d["bonus"][m]
            width = BATCH * TERMS * CH
            flat = [o.rearrange("p c n e -> p (c n e)").rearrange("p (b w) -> p b w", w=width) for o in self.out]
            sp.wait_ge(self.done, m + 2)
            sp.wait_ge(self.loaded[u], 16 * i + 16)
            sp.dma_start(to[:, :, 0].rearrange("b p w -> p b w"), flat[0]).then_inc(self.stored, 16)
            for b, chunks in enumerate((0, 2, 1)):
                sp.dma_start(to[b, :, 1], flat[1][:, chunks]).then_inc(self.stored, 16)
            sp.dma_start(bonus, self.x[u][:, 1]).then_inc(self.stored, 16)

        load(0, 0)
        load(1, 1)
        with sp.Fori(0, KD // 2 - 1) as i:
            for u in range(2):
                store(2 * i + u, u, i)
                load(2 * i + u + 2, u)
        for u in range(2):
            store(KD - 2 + u, u, KD // 2 - 1)

    def gpsimd(self, pool):
        g = self.nc.gpsimd
        self.w.landed(pool, 0, 0)
        pool.sem_inc(self.lora, 4)
        pool.sem_inc(self.directed, 2)
        lora2 = self.w.view(0, KD, 2 * P)

        def body(m, u, i):
            k = self.x[u][:, 1]
            pool.drain()
            pool.wait_ge(self.lora, 4 * m + 4)
            g.tensor_copy(self.slice.rearrange("p q e -> p (q e)"), one(lora2, m)).then_inc(self.sliced, 1)
            pool.wait_ge(self.loaded[u], 16 * i + 16)
            pool.wait_ge(self.scaled, 2 * m + 1)
            for d in range(2):
                g.tensor_tensor(self.kd[d], self.kd[d], k, ALU.mult)
            pool.drain()
            pool.wait_ge(self.kk_done, m + 1)
            for d in range(2):
                g.tensor_tensor(self.kka[d], self.kk, self.a[d], ALU.mult).then_inc(self.directed, 1)
            g.tensor_tensor(self.norm, self.kd[0], self.kd[1], ALU.add)
            pool.drain()
            pool.wait_ge(self.scaled, 2 * m + 2)
            g.tensor_tensor(self.norm, self.norm, self.kk_raw, ALU.mult).then_inc(self.weighted, 1)
        self.each(pool, body)
        pool.wait_ge(self.stored, 80 * KD + 80)

    def tensor(self, pe):
        t = self.nc.tensor
        pe.sem_inc(self.done, 1)

        def halves(out, w, x):
            for at, width in ((0, TL), (TL, TC)):
                last = t.matmul(out[:, at:at + width], w, x[:, at:at + width], start=True, stop=True)
            return last

        def body(m, u, i):
            pe.wait_ge(self.done, m + 1)
            pe.wait_ge(self.sliced, m + 1)
            for q in range(2):
                for d in range(2):
                    hs = slice(LORA * d, LORA * d + LORA)
                    halves(self.wide(2 * q + d), self.slice[hs, q], self.mids[hs, q]).then_inc(self.lora, 1)
            pe.wait_ge(self.squared, m + 1)
            pe.wait_ge(self.activated, 4 * m + 4)
            halves(self.wide(0), self.chip.const("pair_ones"), self.norm).then_inc(self.norm_sum, 1)
            pe.wait_ge(self.weighted, m + 1)
            halves(self.wide(1), self.chip.const("pair_ones"), self.norm).then_inc(self.bonus_sum, 1)
        self.w.landed(pe, 0, 0)
        self.each(pe, body)
        pe.drain().then_inc(self.w.used(0), 1)

    def scalar(self, act):
        a = self.nc.scalar
        act.sem_inc(self.stored, 80)
        a.activation(self.one_minus_ka, self.chip.vec("k_a"), ACT.Copy, scale=-1.0, bias=1.0)
        act.drain()

        def body(m, u, i):
            for q, (out, bias) in enumerate(((self.sg, "w0"), (self.a, "a0"))):
                for d in range(2):
                    act.wait_ge(self.lora, 4 * m + 2 * q + d + 5)
                    a.activation(out[d], self.wide(2 * q + d), ACT.Sigmoid, bias=self.chip.vec_at(bias, m + 8 * d)).then_inc(self.activated, 1)
            act.wait_ge(self.raw_done, m + 1)
            a.activation(self.norm, self.kk_raw, ACT.Square).then_inc(self.squared, 1)
            act.wait_ge(self.activated, 4 * m + 4)
            act.wait_ge(self.directed, 2 * m + 2)
            for d in range(2):
                last = a.activation(self.kd[d], self.a[d], ACT.Identity, scale=self.chip.vec_at("k_a", m), bias=self.one_minus_ka[:, bass.ds(m, 1)])
            last.then_inc(self.scaled, 1)
            act.wait_ge(self.norm_sum, m + 1)
            a.activation(self.norm, self.wide(0), ACT.Sqrt, bias=1e-12).then_inc(self.rooted, 1)
            act.wait_ge(self.kk_done, m + 1)
            a.activation(self.kk_raw, self.x[u][:, 0], ACT.Identity, scale=self.chip.vec_at("r_k", m)).then_inc(self.scaled, 1)
            act.wait_ge(self.stored, 80 * m + 80)
            by_chunk = lambda x: x.rearrange("p (c e) -> p c e", e=CH)
            for d in range(2):
                act.wait_ge(self.scanned, 2 * m + d + 1)
                ci, ce = by_chunk(self.ci[d]), by_chunk(self.ce[d])
                a.activation(self.out[d][:, :, 0], ce, ACT.Exp, scale=-LOG_DECAY)
                a.activation(self.out[d][:, :, 1], ci, ACT.Exp, scale=-LOG_DECAY)
                a.activation(self.out[d][:, :, 2], ci, ACT.Exp, scale=LOG_DECAY)
                whole = ci[:, :, CH - 1] if d == 0 else ci[:, :, 0]
                a.activation(one(self.decays, m)[:, d], whole, ACT.Exp, scale=-LOG_DECAY).then_inc(self.exped, 1)
            for d in range(2):
                a.activation(self.out[d][:, :, 4], by_chunk(self.x[u][:, 2]), ACT.Copy)
            act.drain().then_inc(self.exped, 1)
        self.each(act, body)

    def vector(self, dve):
        v = self.nc.vector
        dve.wait_ge(self.starts_in, 16)

        def body(m, u, i):
            r, k, val = (self.x[u][:, n] for n in range(3))
            by_chunk = lambda x: x.rearrange("p (c e) -> p c e", e=CH)
            dve.wait_ge(self.loaded[u], 16 * i + 16)
            v.tensor_scalar(self.kk_raw, k, self.chip.vec_at("k_k", m), None, ALU.mult).then_inc(self.raw_done, 1)
            for d in range(2):
                dve.wait_ge(self.activated, 4 * m + d + 1)
                v.tensor_tensor_scan(self.ci[d], self.starts, self.sg[d], 0.0, ALU.mult, ALU.add)
                dve.drain()
                if d == 0:
                    v.tensor_tensor(self.ce[d], self.ci[d], self.sg[d], ALU.subtract).then_inc(self.scanned, 1)
                else:
                    ci = by_chunk(self.ci[d])
                    v.tensor_tensor(by_chunk(self.ce[d]), ci[:, :, CH - 1:CH].broadcast_to([P, NC, CH]), ci, ALU.subtract)
                    dve.drain()
                    v.tensor_tensor(self.ci[d], self.ce[d], self.sg[d], ALU.add).then_inc(self.scanned, 1)
            dve.wait_ge(self.rooted, m + 1)
            v.reciprocal(self.kk, self.norm)
            dve.drain()
            v.tensor_tensor(self.kk, self.kk, self.kk_raw, ALU.mult).then_inc(self.kk_done, 1)
            dve.drain()
            for d in range(2):
                dve.wait_ge(self.exped, 3 * m + d + 1)
                dve.wait_ge(self.directed, 2 * m + d + 3)
                o = self.out[d]
                v.tensor_tensor(o[:, :, 3], o[:, :, 2], by_chunk(self.kd[d]), ALU.mult)
                v.tensor_tensor(o[:, :, 0], o[:, :, 0], by_chunk(self.kk), ALU.mult)
                v.tensor_tensor(o[:, :, 1], o[:, :, 1], by_chunk(r), ALU.mult)
                dve.drain()
                v.tensor_tensor(o[:, :, 2], o[:, :, 2], by_chunk(self.kka[d]), ALU.mult)
            dve.wait_ge(self.exped, 3 * m + 3)
            dve.wait_ge(self.bonus_sum, m + 1)
            v.tensor_tensor(k, self.wide(1), val, ALU.mult)
            dve.drain().then_inc(self.done, 1)
        self.each(dve, body)


Y_RWKV = A_HL
SCAN_MASKS = [("lo", CH), ("up", CH), ("lo_diag", CH), ("up_diag", CH), ("lo1", CH), ("up1", CH)] + \
    [(f"level{s}", CH) for s in (2, 4, 8, 16, 32)] + [("ident64", CH)]
LEVELS = (2, 4, 8, 16, 32)


class RwkvScan(Stage):

    def __init__(self, chip):
        super().__init__(chip)
        at = A_WORK
        self.masks_at, at = at, at + len(SCAN_MASKS) * CH
        self.terms, at = chip.view(at, BATCHES, 2 * BATCH * TERMS * CH), at + BATCHES * 2 * BATCH * TERMS * CH
        single = lambda i: [chip.view(at + (2 * i + d) * BATCH * CH, BATCH, 1, CH) for d in range(2)]
        self.t, self.tt, self.z, self.v, self.qa, self.nh = (single(i) for i in range(6))
        at += 12 * BATCH * CH
        double = lambda i: [chip.view(at + (2 * i + d) * BATCH * 2 * CH, BATCH, 2, CH) for d in range(2)]
        self.p_lg, self.mb_b, self.mg_g = (double(i) for i in range(3))
        at += 6 * BATCH * 2 * CH
        self.spread_at = at
        wide = lambda i: [chip.view(at + (2 * i + d) * BATCH * P, BATCH, P) for d in range(2)]
        self.p_sp, self.b_sp, self.g_sp, self.vin_sp, self.lbt_sp, self.tt_sp, self.z_sp, self.v_sp = (wide(i) for i in range(8))
        self.w1_sp, self.w2_sp, self.a_sp = (wide(i) for i in range(8, 11))
        self.h_sp = self.z_sp
        at += 22 * BATCH * P
        self.state_sp = [chip.view(at + d * P, 1, P) for d in range(2)]
        at += 2 * P
        self.spread_words = at - self.spread_at
        self.state = [chip.view(at + d * CH, CH) for d in range(2)]
        at += 2 * CH
        assert at <= A_END, at
        self.y = chip.view(Y_RWKV, KD * NC, CH)
        self.decays = chip.view(DECAYS, KD * 2 * NC)
        (self.masks_in, self.zeroed, self.landed, self.ready, self.taken) = (
            chip.sem("scan_" + n) for n in "masks_in zeroed landed ready taken".split())
        (self.sources_spread, self.sums, self.evacuated, self.tokens_out, self.t_ready, self.tt_ready,
         self.tt_spread, self.z_sums, self.z_masked, self.z_spread, self.t_sums, self.tt_sums,
         self.v_sums, self.v_out, self.w_sums, self.w_out, self.corrected, self.a_ready,
         self.state_ready, self.state_sums, self.y_added) = (
            [chip.sem(f"scan{d}_{n}") for d in range(2)] for n in (
                "sources_spread sums evacuated tokens_out t_ready tt_ready tt_spread z_sums z_masked "
                "z_spread t_sums tt_sums v_sums v_out w_sums w_out corrected a_ready state_ready "
                "state_sums y_added").split())

    def mask(self, name):
        i = [n for n, _ in SCAN_MASKS].index(name)
        return across(self.chip.view(self.masks_at + i * CH, CH), BATCH)

    def spread(self, emit, to, of):
        for h in range(2):
            hs = slice(CH * h, CH * h + CH)
            last = emit(to[hs, :, CH * h:CH * h + CH], of[hs])
        return last

    def passes(self, eng, body, start=lambda m: None):
        with eng.Fori(0, KD) as m:
            start(m)
            body(3 * m, m, 0, (0, 0))
            with eng.Fori(0, 2) as j:
                body(3 * m + j + 1, m, j + 1, (j * 4 + 4, j * -4 + 8))

    def source(self, pos, d):
        x = self.terms[:, 0] if isinstance(pos, int) else one(self.terms, pos)
        return x.rearrange("p (d c n e) -> p d c n e", d=2, n=TERMS, e=CH)[:, d]

    def bank(self, d, b):
        return self.chip.bank(4 * d + b)

    def slots(self, d, b, n):
        return self.chip.bank(4 * d + b, BATCH * n * CH).rearrange("p (c n e) -> p c n e", n=n, e=CH)

    def step(self, s, d):
        return s if d == 0 else BATCH - 1 - s

    def sync(self, sp):
        d = self.chip.dram
        sp.wait_ge(self.chip.stage_done, 4 * self.index)
        sp.dma_start(self.chip.view(self.masks_at, len(SCAN_MASKS) * CH), d["scan_const"][:, T:]).then_inc(self.masks_in, 16)
        with sp.Fori(0, KD) as m:
            for b in range(BATCHES):
                sp.wait_ge(self.taken, 3 * m + b + 1)
                sp.dma_start(self.terms[:, b], d["terms"][bass.ds(3 * m + b, 1)].rearrange("o p d w -> (o p) (d w)")
                             ).then_inc(self.landed, 16)
                sp.wait_ge(self.landed, 48 * m + 16 * b + 16)
                sp.sem_inc(self.ready, 1)

    def gpsimd(self, pool):
        g = self.nc.gpsimd
        g.memset(self.chip.view(self.spread_at, self.spread_words), 0.0)
        g.memset(self.y, 0.0)
        pool.drain().then_inc(self.zeroed, 1)

        def body(n, m, pos, chunk):
            pool.wait_ge(self.ready, n + 1)
            for d in range(2):
                x = self.source(pos, d)
                pool.wait_ge(self.v_sums[d], n + 1)
                for to, term in ((self.b_sp, 2), (self.p_sp, 0), (self.g_sp, 3), (self.vin_sp, 4)):
                    last = g.tensor_tensor(to[d].rearrange("p c (h e) -> p c h e", e=CH), x[:, :, term].unsqueeze(2).broadcast_to([P, BATCH, 2, CH]),
                                           across(self.chip.const("pair_ones").rearrange("p (h e) -> p h e", e=CH), BATCH), ALU.mult)
                last.then_inc(self.sources_spread[d], 1)
        self.passes(pool, body)

    def tensor(self, pe):
        t = self.nc.tensor
        pe.wait_ge(self.masks_in, 16)
        for d in range(2):
            pe.sem_inc(self.v_sums[d], 1)
        ident = self.chip.view(self.masks_at + (len(SCAN_MASKS) - 1) * CH, CH)

        def each(out, lhs, rhs):
            for s in range(BATCH):
                last = t.matmul(out(s), lhs[:, s], rhs(s), start=True, stop=True)
            return last

        def body(n, m, pos, chunk):
            pe.wait_ge(self.ready, n + 1)
            for d in range(2):
                x = self.source(pos, d)
                two = lambda b: lambda s: self.bank(d, b)[:, 2 * CH * s:2 * CH * s + 2 * CH]
                one_ = lambda b, at: lambda s: self.bank(d, b)[:, at + CH * s:at + CH * s + CH]
                pe.wait_ge(self.y_added[d], n + 1)
                pe.wait_ge(self.sources_spread[d], n + 1)
                each(two(1), self.b_sp[d], lambda s: x[:, s, 0:2].rearrange("p n e -> p (n e)")).then_inc(self.sums[d], 1)
                each(two(0), self.p_sp[d], lambda s: x[:, s, 2:4].rearrange("p n e -> p (n e)")).then_inc(self.sums[d], 1)
                each(one_(2, 0), self.g_sp[d], lambda s: x[:, s, 1])
                each(one_(2, BATCH * CH), self.p_sp[d], lambda s: ident).then_inc(self.sums[d], 1)
                each(one_(3, 0), self.b_sp[d], lambda s: ident)
                each(one_(3, BATCH * CH), self.g_sp[d], lambda s: ident).then_inc(self.sums[d], 1)
            for l in range(len(LEVELS)):
                last_level = l == len(LEVELS) - 1
                for d in range(2):
                    if l == 0:
                        pe.wait_ge(self.evacuated[d], n + 1)
                    pe.wait_ge(self.t_ready[d], 5 * n + l + 1)
                    each(one_of(self.bank(d, 0)), self.lbt_sp[d], lambda s: self.t[d][:, s, 0]).then_inc(self.z_sums[d], 1)
                    if l == 0:
                        pe.wait_ge(self.tokens_out[d], n + 1)
                        each(one_of(self.bank(d, 3)), self.vin_sp[d], lambda s: ident).then_inc(self.v_sums[d], 1)
                for d in range(2):
                    pe.wait_ge(self.tt_spread[d], 6 * n + l + 1)
                    pe.wait_ge(self.z_masked[d], 5 * n + l + 1)
                    if not last_level:
                        each(one_of(self.bank(d, 1)), self.tt_sp[d], lambda s: self.z[d][:, s, 0]).then_inc(self.t_sums[d], 1)
                    pe.wait_ge(self.z_spread[d], 5 * n + l + 1)
                    each(one_of(self.bank(d, 2)), self.z_sp[d], lambda s: self.tt[d][:, s, 0]).then_inc(self.tt_sums[d], 1)
            pair_of = lambda b: lambda s: b[:, 2 * CH * s:2 * CH * s + 2 * CH]
            flat = lambda x: lambda s: x[:, s].rearrange("p n e -> p (n e)")
            for d in range(2):
                pe.wait_ge(self.v_out[d], n + 1)
                pe.wait_ge(self.tt_spread[d], 6 * n + 6)
                each(pair_of(self.bank(d, 3)), self.tt_sp[d], flat(self.p_lg[d])).then_inc(self.w_sums[d], 1)
            for d in range(2):
                pe.wait_ge(self.w_out[d], n + 1)
                each(pair_of(self.bank(d, 0)), self.w1_sp[d], flat(self.mb_b[d])).then_inc(self.corrected[d], 1)
                each(pair_of(self.bank(d, 1)), self.w2_sp[d], flat(self.mb_b[d])).then_inc(self.corrected[d], 1)
            for s in range(BATCH):
                for d in range(2):
                    c = self.step(s, d)
                    if s == 0:
                        pe.wait_ge(self.a_ready[d], n + 1)
                    pe.wait_ge(self.state_ready[d], 13 * m + 4 * pos + s + 1)
                    y, new = one_of(self.bank(d, 3))(c), self.bank(d, 2)[:, 0:CH]
                    t.matmul(y, self.v_sp[d][:, c], self.nh[d][:, c, 0], start=True, stop=False)
                    t.matmul(y, self.state_sp[d][:, 0], self.qa[d][:, c, 0], start=False, stop=True)
                    t.matmul(new, self.h_sp[d][:, c], self.v[d][:, c, 0], start=True, stop=False)
                    t.matmul(new, self.a_sp[d][:, c], self.state[d], start=False, stop=True).then_inc(self.state_sums[d], 1)
        one_of = lambda b: lambda s: b[:, CH * s:CH * s + CH]
        self.passes(pe, body)

    def scalar(self, act):
        a = self.nc.scalar
        act.wait_ge(self.zeroed, 1)
        copy = lambda to, of: a.activation(to, of, ACT.Copy)
        half = lambda d, b, x: self.bank(d, b)[:, BATCH * CH * x:BATCH * CH * x + BATCH * CH].rearrange("p (c e) -> p c e", e=CH)

        def body(n, m, pos, chunk):
            for d in range(2):
                act.wait_ge(self.tt_ready[d], 6 * n + 1)
                self.spread(copy, self.tt_sp[d], self.tt[d][:, :, 0]).then_inc(self.tt_spread[d], 1)
                act.wait_ge(self.sums[d], 4 * n + 4)
                copy(self.mb_b[d][:, :, 1], half(d, 3, 0))
                copy(self.mg_g[d][:, :, 1], half(d, 3, 1)).then_inc(self.tokens_out[d], 1)
            for l in range(len(LEVELS)):
                if l == 0:
                    for d in range(2):
                        act.wait_ge(self.v_sums[d], n + 2)
                        copy(self.v[d][:, :, 0], half(d, 3, 0))
                        self.spread(copy, self.v_sp[d], half(d, 3, 0)).then_inc(self.v_out[d], 1)
                for d in range(2):
                    act.wait_ge(self.tt_ready[d], 6 * n + l + 2)
                    self.spread(copy, self.tt_sp[d], self.tt[d][:, :, 0]).then_inc(self.tt_spread[d], 1)
            act.wait_ge(self.w_sums[1], n + 1)
            w = self.slots(1, 3, 2)
            self.spread(copy, self.w1_sp[1], w[:, :, 0])
            self.spread(copy, self.w2_sp[1], w[:, :, 1]).then_inc(self.w_out[1], 1)
        self.passes(act, body)

    def vector(self, dve):
        v = self.nc.vector
        dve.wait_ge(self.masks_in, 16)
        dve.wait_ge(self.zeroed, 1)
        dve.sem_inc(self.taken, 3)
        for d in range(2):
            dve.sem_inc(self.y_added[d], 1)
        after, before = ("lo", "up"), ("up", "lo")
        add, mult, sub = ALU.add, ALU.mult, ALU.subtract

        def start(m):
            for d in range(2):
                v.memset(self.state[d], 0.0)
                v.memset(self.state_sp[d], 0.0)
                dve.drain().then_inc(self.state_ready[d], 1)

        def body(n, m, pos, chunk):
            for d in range(2):
                dve.wait_ge(self.sums[d], 4 * n + 1)
                lbt, lb = self.slots(d, 1, 2), self.slots(d, 0, 2)
                v.tensor_tensor(self.tt[d][:, :, 0], lbt[:, :, 0], self.mask(before[d] + "1"), mult)
                for h in range(2):
                    hs = slice(CH * h, CH * h + CH)
                    v.tensor_tensor(self.lbt_sp[d][hs, :, CH * h:CH * h + CH], lbt[hs, :, 0], self.mask(before[d])[hs], mult)
                dve.drain()
                v.tensor_tensor(self.tt[d][:, :, 0], self.tt[d][:, :, 0], self.mask("ident64"), add).then_inc(self.tt_ready[d], 1)
                dve.wait_ge(self.sums[d], 4 * n + 2)
                v.tensor_tensor(self.t[d][:, :, 0], lb[:, :, 0], self.mask(after[d] + "1"), mult)
                v.tensor_tensor(self.mb_b[d][:, :, 0], lbt[:, :, 1], self.mask(before[d] + "_diag"), mult)
                dve.drain()
                v.tensor_tensor(self.t[d][:, :, 0], self.t[d][:, :, 0], self.mask("ident64"), add).then_inc(self.t_ready[d], 1)
                v.tensor_tensor(self.p_lg[d][:, :, 1], lb[:, :, 1], self.mask(after[d]), mult)
                dve.wait_ge(self.sums[d], 4 * n + 3)
                third = self.bank(d, 2).rearrange("p (n c e) -> p n c e", n=2, e=CH)
                v.tensor_tensor(self.mg_g[d][:, :, 0], third[:, 0], self.mask(before[d] + "_diag"), mult)
                v.tensor_copy(self.p_lg[d][:, :, 0], third[:, 1])
                dve.drain().then_inc(self.evacuated[d], 1)
            for l, level in enumerate(LEVELS):
                for d in range(2):
                    dve.wait_ge(self.z_sums[d], 5 * n + l + 1)
                    v.tensor_tensor(self.z[d][:, :, 0], self.slots(d, 0, 1)[:, :, 0], self.mask(f"level{level}"), mult).then_inc(self.z_masked[d], 1)
                    dve.drain()
                    self.spread(v.tensor_copy, self.z_sp[d], self.z[d][:, :, 0]).then_inc(self.z_spread[d], 1)
                for d in range(2):
                    if level != LEVELS[-1]:
                        dve.wait_ge(self.t_sums[d], 4 * n + l + 1)
                        v.tensor_tensor(self.t[d], self.t[d], self.slots(d, 1, 1), add).then_inc(self.t_ready[d], 1)
                    dve.wait_ge(self.tt_sums[d], 5 * n + l + 1)
                    v.tensor_tensor(self.tt[d], self.tt[d], self.slots(d, 2, 1), add).then_inc(self.tt_ready[d], 1)
            dve.wait_ge(self.w_sums[0], n + 1)
            w = self.slots(0, 3, 2)
            self.spread(v.tensor_copy, self.w1_sp[0], w[:, :, 0])
            self.spread(v.tensor_copy, self.w2_sp[0], w[:, :, 1]).then_inc(self.w_out[0], 1)
            for d in range(2):
                x = self.source(pos, d)
                ident = self.mask("ident64")
                minus = lambda to, a, b: v.tensor_tensor(to, a, b, sub)
                both = lambda to, a, b: self.spread(lambda t_, i: minus(t_, i[0], i[1]), to, Halves(a, b))
                dve.wait_ge(self.corrected[d], 2 * n + 1)
                c1, c2 = self.slots(d, 0, 2), self.slots(d, 1, 2)
                minus(self.qa[d][:, :, 0], x[:, :, 1], c1[:, :, 0])
                both(self.a_sp[d], ident, c1[:, :, 1])
                dve.wait_ge(self.corrected[d], 2 * n + 2)
                minus(self.nh[d][:, :, 0], self.mg_g[d][:, :, 0], c2[:, :, 0])
                both(self.h_sp[d], self.mg_g[d][:, :, 1], c2[:, :, 1])
                dve.drain().then_inc(self.a_ready[d], 1)
            dve.sem_inc(self.taken, 1)
            for s in range(BATCH):
                for d in range(2):
                    dve.wait_ge(self.state_sums[d], 4 * n + s + 1)
                    at = m * (2 * NC) + NC * d + self.step(s, d) + chunk[d]
                    v.tensor_scalar(self.state[d], self.bank(d, 2)[:, 0:CH], self.decays[:, bass.ds(at, 1)], None, mult)
                    dve.drain()
                    self.spread(v.tensor_copy, self.state_sp[d], self.state[d].unsqueeze(1)).then_inc(self.state_ready[d], 1)
            for d in range(2):
                y = self.y[:, bass.ds(m * NC + chunk[d], BATCH)]
                v.tensor_tensor(y, y, self.slots(d, 3, 1)[:, :, 0], add).then_inc(self.y_added[d], 1)
                dve.drain()
        self.passes(dve, body, start)


class Halves:

    def __init__(self, *views):
        self.views = views

    def __getitem__(self, hs):
        return [v[hs] for v in self.views]


class RwkvOutput(Stage):

    def __init__(self, chip):
        super().__init__(chip)
        self.y = chip.view(Y_RWKV, KD, T)
        at = RWKV
        self.bonus = [chip.view(at + u * T, T) for u in range(2)]
        self.z = [chip.view(at + (2 + u) * T, T) for u in range(2)]
        self.squares, self.inv = chip.view(at + 4 * T, T), chip.view(at + 5 * T, T)
        self.loaded = [chip.sem(f"rwkv_out_loaded{u}") for u in range(2)]
        (self.mean_sum, self.centred, self.squared, self.var_sum, self.rooted, self.done) = (
            chip.sem("rwkv_out_" + n) for n in "mean_sum centred squared var_sum rooted done".split())

    def wide(self, q):
        return self.chip.psum[:, 2 * q:2 * q + 2].rearrange("p b w -> p (b w)")[:, 0:T]

    def each(self, eng, body):
        with eng.Fori(0, KD // 2) as i:
            for u in range(2):
                body(2 * i + u, u, i)

    def sync(self, sp):
        sp.wait_ge(self.chip.stage_done, 4 * self.index)

        def body(m, u, i):
            sp.wait_ge(self.done, m + 1)
            for to, of in ((self.bonus[u], self.chip.dram["bonus"][bass.ds(m, 1)]), (self.z[u], self.chip.dram["rkvz"][bass.ds(4 * m + 3, 1)])):
                sp.dma_start(to, of.rearrange("o p w -> (o p) w")).then_inc(self.loaded[u], 16)
        self.each(sp, body)

    def tensor(self, pe):
        def sums(out, x):
            for at, width in ((0, TL), (TL, TC)):
                last = self.nc.tensor.matmul(out[:, at:at + width], self.chip.const("pair_ones"), x[:, at:at + width], start=True, stop=True)
            return last

        def body(m, u, i):
            pe.wait_ge(self.done, m + 2)
            sums(self.wide(0), one(self.y, m)).then_inc(self.mean_sum, 1)
            pe.wait_ge(self.squared, m + 1)
            sums(self.wide(1), self.squares).then_inc(self.var_sum, 1)
        self.each(pe, body)

    def scalar(self, act):
        a = self.nc.scalar

        def body(m, u, i):
            act.wait_ge(self.centred, m + 1)
            a.activation(self.squares, one(self.y, m), ACT.Square).then_inc(self.squared, 1)
            act.wait_ge(self.var_sum, m + 1)
            a.activation(self.squares, self.wide(1), ACT.Sqrt, scale=1.0 / RW, bias=64e-5).then_inc(self.rooted, 1)
        self.each(act, body)

    def vector(self, dve):
        v = self.nc.vector
        dve.sem_inc(self.done, 2)

        def body(m, u, i):
            y = one(self.y, m)
            dve.wait_ge(self.mean_sum, m + 1)
            v.scalar_tensor_tensor(y, self.wide(0), -1.0 / RW, y, ALU.mult, ALU.add).then_inc(self.centred, 1)
            dve.wait_ge(self.rooted, m + 1)
            v.reciprocal(self.inv, self.squares)
            dve.drain()
            v.tensor_tensor(y, y, self.inv, ALU.mult)
            dve.drain()
            v.tensor_scalar(y, y, self.chip.vec_at("ln_gain", m), self.chip.vec_at("ln_bias", m), ALU.mult, ALU.add)
            dve.drain()
            dve.wait_ge(self.loaded[u], 32 * i + 32)
            v.tensor_tensor(y, y, self.bonus[u], ALU.add)
            dve.drain()
            v.tensor_tensor(y, y, self.z[u], ALU.mult).then_inc(self.done, 1)
        self.each(dve, body)


def rwkv_layer(chip, layer):
    y = chip.view(Y_RWKV, KD, T)
    gate = modulated(chip, layer, 2)
    return [norm2(chip, layer, True), RwkvFeatures(chip), RwkvTerms(chip), RwkvScan(chip), RwkvOutput(chip),
            Residual(chip, "w_rwkv_out", KD, lambda k: y[:, k, TC:T], gate[0], lambda k: y[:, k, 0:TC], gate[1])]


def program(nc, dram, stages_of=None):
    with ExitStack() as ctx:
        chip = Chip(nc, dram, ctx)
        stages = (stages_of or all_stages)(chip)
        assert [stage.index for stage in stages] == list(range(len(stages)))
        block = ctx.enter_context(nc.Block())

        def walk(eng, run, between=lambda n: None):
            for n, stage in enumerate(stages):
                if n > 0:
                    eng.wait_ge(chip.stage_done, 4 * n)
                    between(n)
                    eng.drain()
                run(stage)
                eng.drain().then_inc(chip.stage_done, 1)

        @block.sync
        def _(sp):
            for stage in stages:
                stage.sync(sp)
                sp.sem_inc(chip.loads_issued, 1)

        @block.tensor
        def _(pe):
            walk(pe, lambda stage: stage.tensor(pe))

        @block.scalar
        def _(act):
            walk(act, lambda stage: stage.scalar(act))

        @block.vector
        def _(dve):
            walk(dve, lambda stage: stage.vector(dve))

        @block.gpsimd
        def _(pool):
            def clear(n):
                pool.wait_ge(chip.loads_issued, n)
                chip.clear_sems(pool, n - 1)

            walk(pool, lambda stage: stage.gpsimd(pool), clear)


SCRATCH = {"states": (2 * SsdStates.STEPS, P, D_SSD), "rkvz": (4 * KD, P, T), "bonus": (KD, P, T),
           "terms": (KD * BATCHES, P, 2, BATCH * TERMS * CH)}


def layers(chip):
    return block1(chip) + [
        NewContext(chip),
        *sgu_layer(chip, 0, 0, 6), *rwkv_layer(chip, 1), *mla_layer(chip, 2), *sgu_layer(chip, 3, 1, 4)]


def all_stages(chip):
    return layers(chip) + [Store(chip)]


def kernel(**inputs):
    import concourse.bacc as bacc
    from concourse.bass_utils import run_bass_kernel_spmd

    nc = bacc.Bacc("TRN2", target_bir_lowering=False, num_devices=1)
    arrays = {n: np.ascontiguousarray(a, dtype=np.float32) for n, a in prepare(inputs).items()}
    dram = {n: nc.dram_tensor(n, a.shape, F32, kind="ExternalInput").ap() for n, a in arrays.items()}
    for n, shape in SCRATCH.items():
        dram[n] = nc.dram_tensor(n, shape, F32, kind="Internal").ap()
    dram["out"] = nc.dram_tensor("out", (P, KD * TL), F32, kind="ExternalOutput").ap()
    program(nc, dram)
    got = run_bass_kernel_spmd(nc, [arrays], core_ids=[0]).results[0]["out"]
    return np.asarray(got).reshape(P, KD, TL).transpose(2, 1, 0).reshape(1, TL, D)
```

```python
from contextlib import ExitStack

import concourse.bass as bass
import numpy as np
from concourse import mybir
from concourse.alu_op_type import AluOpType as ALU

F32 = mybir.dt.float32
ACT = mybir.ActivationFunctionType
AX = mybir.AxisListType

P = 128
D = 1024
KD = D // P
TL, TC = 512, 256
T = TL + TC
NT = T // P
EPS = 1e-6

D_SSD, SSD_HEADS, SSD_P, GROUPS, STATE = 2048, 32, 64, 4, 128
D_BC = GROUPS * STATE
D_XBC = D_SSD + 2 * D_BC
KX, KS = D_XBC // P, D_SSD // P
HEADS, KV, DH = 16, 4, 64
D_Q, D_KV = HEADS * DH, KV * DH
D_FF = 2816
KF = D_FF // P
Z0, XBC0 = 0, D_SSD
DT0 = XBC0 + D_XBC
Q0 = DT0 + 2 * SSD_HEADS
K0 = Q0 + D_Q
V0 = K0 + D_KV
G0 = V0 + D_KV
SGU_W, SGU_G = 2048, 8
KG = SGU_W // P
RH, RW = 16, 64
CH = 64
NC = T // CH
LORA = 64
MH, NOPE, ROPE, VD = 16, 128, 64, 128
QK = NOPE + ROPE
QR, KVR = 768, 256
GRID_W, ROPE_BASE = 64, 10000.0

VEC = [("c", 8), ("c_ctx", 8),
       ("b_mod", 48), ("ada_b", 96), ("norm1_g", 8), ("norm2_g", 8), ("conv_w", 3 * KX), ("conv_b", KX),
       ("ssd_d", KS), ("ssd_g", KS), ("ffn_w", 6 * KF), ("ffn_b", 2 * KF), ("final_g", 8),
       ("dt_bias", 64), ("a_log", 64), ("sink", HEADS),
       ("sgu_gain", 2 * KG), ("mu", 48), ("w0", 16), ("a0", 16), ("k_k", 8), ("k_a", 8), ("r_k", 8),
       ("ln_gain", 8), ("ln_bias", 8), ("q_norm", 6), ("kv_norm", 2),
       ("gq_nope", 1), ("gq_rope", 1), ("gk_nope", 1), ("gk_rope", 1)]
VOFF, _n = {}, 0
for _name, _w in VEC:
    VOFF[_name] = (_n, _w)
    _n += _w
NVEC = _n
CONST = [("ident", P), ("ones", P), ("upto", P), ("from", P), ("after", P), ("before", P), ("pair_ones", P)]
COFF, _n = {}, 0
for _name, _w in CONST:
    COFF[_name] = (_n, _w)
    _n += _w
NCONST = _n

WSLOT = 5120
A_VEC = 0
A_CONST = A_VEC + NVEC
A_MOD1 = A_CONST + NCONST
A_MOD2 = A_MOD1 + 96
A_SIDE = A_MOD2 + 192
A_SMALL = A_SIDE + 6
A_XL = A_SMALL + 512
A_XC = A_XL + KD * TL
A_HL = A_XC + KD * TC
A_HC = A_HL + KD * TL
A_W = A_HC + KD * TC
A_WORK = A_W + 2 * WSLOT
A_END = 53200


def constants():
    i = np.arange(P)
    k, m = i[:, None], i[None, :]
    c = {"ident": k == m, "ones": k >= 0 * m, "upto": k <= m, "from": k >= m, "after": k > m, "before": k < m,
         "pair_ones": (k // RW) == (m // RW)}
    return np.ascontiguousarray(np.concatenate([np.broadcast_to(c[n], (P, P)) for n, _ in CONST], 1).astype(np.float32))


def rope_tables():
    t = np.arange(TL)
    row, col = (t // GRID_W).astype(np.float32), (t % GRID_W).astype(np.float32)
    inv = (ROPE_BASE ** (-np.arange(0, 32, 2, dtype=np.float32) / np.float32(32))).astype(np.float32)
    a = np.zeros((64, TL), np.float32)
    swap = np.zeros((P, P), np.float32)
    for f in range(64):
        a[f] = (row if f < 32 else col) * inv[f % 16]
        half, lo = f % 32, f % 32 < 16
        for h in (0, 64):
            swap[h + (f + 16 if lo else f - 16), h + f] = -1.0 if lo else 1.0
    att = np.stack([np.tile(np.cos(a), (2, 1)), np.tile(np.sin(a), (2, 1))], 1)
    b = np.zeros((P, TL), np.float32)
    mswap = np.zeros((P, P), np.float32)
    for f in range(64):
        i = f % 32
        b[f] = (row if i < 16 else col) * inv[i % 16]
        mswap[(f + 32 if f < 32 else f - 32), f] = -1.0 if f < 32 else 1.0
    mla = np.stack([np.cos(b), np.sin(b)], 1)
    pack = lambda x, s: np.ascontiguousarray(np.concatenate([x.reshape(P, -1), s], 1).astype(np.float32))
    return pack(att, swap), pack(mla, mswap)


def window_mask():
    q, k = np.arange(P)[:, None], np.arange(3 * P)[None, :] - P
    return np.where(np.abs(q - k) <= P, 0.0, -1e30).astype(np.float32)


def tiles(w):
    k, m = w.shape
    return w.reshape(k // P, P, m // P, P).transpose(2, 1, 0, 3).reshape(m // P, P, -1)


def columns(v):
    return v.reshape(-1, P).T


def feature_major(x):
    t, f = x.shape
    return x.reshape(t, f // P, P).transpose(2, 1, 0).reshape(P, -1)


def prepare(inp):
    g = {n: np.asarray(v) for n, v in inp.items()}
    rows = lambda v: np.broadcast_to(v.reshape(1, -1), (P, v.size))
    half = lambda v: np.concatenate([v, v]).reshape(P, 1)
    w_in = g["w_in"][0]
    vec = {
        "c": columns(g["c"][0]), "c_ctx": columns(g["c_ctx"]),
        "b_mod": columns(g["b_mod"][0]), "ada_b": columns(g["ada_b_2"].reshape(-1)),
        "norm1_g": columns(g["norm1_g"][0]), "norm2_g": columns(g["norm2_g"][0]),
        "conv_w": columns(g["ssd_conv_w"][0].reshape(-1)), "conv_b": columns(g["ssd_conv_b"][0]),
        "ssd_d": columns(np.repeat(g["ssd_d"][0], SSD_P)), "ssd_g": columns(g["ssd_norm_g"][0]),
        "ffn_w": columns(g["ffn_conv_w"][0].reshape(-1)), "ffn_b": columns(g["ffn_conv_b"][0]),
        "final_g": columns(g["final_g"]),
        "dt_bias": rows(g["ssd_dt_bias"][0]), "a_log": rows(g["ssd_a_log"][0]), "sink": rows(g["att_sink"][0]),
        "sgu_gain": columns(g["sgu_gain_2"].reshape(-1)), "mu": columns(g["rwkv_mu_2"][0].reshape(-1)),
        "w0": columns(g["rwkv_w0_2"][0].reshape(-1)), "a0": columns(g["rwkv_a0_2"][0].reshape(-1)),
        "k_k": columns(g["rwkv_k_k_2"][0]), "k_a": columns(g["rwkv_k_a_2"][0]), "r_k": columns(g["rwkv_r_k_2"][0].reshape(-1)),
        "ln_gain": columns(g["rwkv_ln_gain_2"][0]), "ln_bias": columns(g["rwkv_ln_bias_2"][0]),
        "q_norm": columns(g["mla_q_norm_2"][0]), "kv_norm": columns(g["mla_kv_norm_2"][0]),
        "gq_nope": g["mla_qk_gain_q_2"][0, :NOPE].reshape(P, 1), "gq_rope": half(g["mla_qk_gain_q_2"][0, NOPE:]),
        "gk_nope": g["mla_qk_gain_k_2"][0, :NOPE].reshape(P, 1), "gk_rope": half(g["mla_qk_gain_k_2"][0, NOPE:]),
    }
    a = {"vec": np.concatenate([vec[n] for n, _ in VEC], 1), "const": constants()}
    a["rope_att"], a["rope_mla"] = rope_tables()
    a["win_mask"] = window_mask()
    a["x_in"] = feature_major(g["x"][0])
    a["ctx1_in"] = feature_major(g["ctx"][0])
    a["ctx2_in"] = feature_major(g["ctx_2"][0])
    four = lambda w: tiles(w).reshape(-1, 4, P, w.shape[0] // P, P).transpose(0, 2, 3, 1, 4).reshape(-1, P, w.shape[0] * 4)
    a["w_mod1"] = four(g["w_mod"][0])
    a["w_mod2"] = np.concatenate([w.T.reshape(-1, P, D) for w in g["ada_w_2"]])
    a["cond_rows2"] = np.concatenate([rows(g["c_2"][0]), rows(g["c_ctx_2"])], 1)
    a["w_xbc"] = tiles(w_in[:, XBC0:DT0])
    ktile = lambda w: w.reshape(w.shape[0] // P, P, -1).transpose(1, 0, 2)
    a["w_dt"] = ktile(w_in[:, DT0:Q0]).reshape(1, P, -1)
    a["w_z"] = tiles(w_in[:, Z0:XBC0])
    qkv = []
    for h in range(KV):
        q = w_in[:, Q0 + h * 256:Q0 + (h + 1) * 256]
        k = w_in[:, K0 + h * DH:K0 + (h + 1) * DH]
        v = w_in[:, V0 + h * DH:V0 + (h + 1) * DH]
        qkv.append(ktile(np.concatenate([q, k, k, v], 1)).reshape(P, -1))
    a["w_qkv"] = np.stack(qkv)
    a["w_merge"] = np.concatenate([tiles(w_in[:, G0:G0 + D]), tiles(g["w_o_ssd"][0]),
                                   tiles(w_in[:, G0 + D:G0 + 2 * D]), tiles(g["w_o_att"][0])], 2)
    a["w_out1"] = tiles(g["w_out"][0])
    up = tiles(g["w_up"][0])
    a["w_up"] = np.concatenate([up[:KF], up[KF:]], 2)
    a["w_down"] = tiles(g["w_down"][0])
    return prepare2(g, a, ktile)


def scan_constants():
    i = np.arange(CH)
    r, c = i[:, None], i[None, :]
    two = lambda a: np.concatenate([a, a], 0).astype(np.float32)
    lo, up = r > c, r < c
    off = lambda s: (r // (2 * s) == c // (2 * s)) & (r // s != c // s)
    starts = np.broadcast_to(np.arange(T) % CH != 0, (P, T)).astype(np.float32)
    masks = [lo, up, r >= c, r <= c, -1.0 * (lo & off(1)), -1.0 * (up & off(1))] + [-1.0 * off(s) for s in (2, 4, 8, 16, 32)] + [r == c]
    return np.ascontiguousarray(np.concatenate([starts] + [two(x) for x in masks], 1))


def prepare2(g, a, ktile):
    a["scan_const"] = scan_constants()
    for j, layer in enumerate((0, 3)):
        w = g["sgu_w_in_2"][j]
        u, v, z = w[:, :SGU_W], w[:, SGU_W:2 * SGU_W], w[:, 2 * SGU_W:]
        a[f"w_sgu_v{layer}"] = np.stack([ktile(v[:, 512 * n:512 * n + 512]).reshape(P, -1) for n in range(4)])
        ws = np.repeat(g["sgu_w_s_2"][j].transpose(0, 2, 1), KG // SGU_G, 0)
        a[f"w_sgu_uz{layer}"] = np.concatenate([tiles(u), tiles(z), ws], 2)
        a[f"sgu_bs{layer}"] = np.broadcast_to(g["sgu_b_s_2"][j].reshape(1, -1), (P, SGU_G * P))
        a[f"w_sgu_out{layer}"] = tiles(g["sgu_w_out_2"][j])
    for n, name in enumerate("rkvz"):
        a["w_rwkv_" + name] = tiles(g["rwkv_w_in_2"][0, n])
    both = lambda w: tiles(np.concatenate([w[0], w[1]], 1))
    a["w_rwkv_lw"], a["w_rwkv_la"] = both(g["rwkv_w_lora1_2"][0]), both(g["rwkv_a_lora1_2"][0])
    second = [w[0].reshape(P, KD, P) for w in (g["rwkv_w_lora2_2"], g["rwkv_a_lora2_2"])]
    a["w_lora2"] = np.stack(second, 2).reshape(1, P, -1)
    a["w_rwkv_out"] = tiles(g["rwkv_w_out_2"][0])
    w = g["mla_w_in_2"][0]
    a["w_mla_q"] = tiles(w[:, :QR])
    a["w_mla_kv"] = tiles(w[:, QR:QR + KVR])
    rope = w[:, QR + KVR:QR + KVR + ROPE]
    a["w_mla_rope"] = tiles(np.concatenate([rope, rope], 1))
    a["w_mla_z"] = tiles(w[:, QR + KVR + ROPE:])
    uq = ktile(g["mla_w_uq_2"][0]).reshape(P, QR // P, MH, QK).transpose(2, 0, 1, 3).reshape(MH, P, -1)
    ukv = ktile(g["mla_w_ukv_2"][0]).reshape(P, KVR // P, MH, NOPE + VD).transpose(2, 0, 1, 3).reshape(MH, P, -1)
    a["w_mla_head"] = np.concatenate([uq, ukv], 2)
    a["w_mla_out"] = tiles(g["mla_w_out_2"][0])
    return a


FIRST_SEM, STAGE_SEMS = 140, 55


class Chip:

    def __init__(self, nc, dram, ctx):
        self.nc, self.dram, self.ctx = nc, dram, ctx
        self.sbuf = ctx.enter_context(nc.sbuf_tensor("sbuf", [P, A_END], F32))
        self.psum = ctx.enter_context(nc.psum_tensor("psum", [P, 8, 512], F32))
        self.stage_done, self.loads_issued = self.lasting("stage_done"), self.lasting("loads_issued")
        self.slot_landed = [self.lasting(f"slot_landed{u}") for u in range(2)]
        self.slot_used = [self.lasting(f"slot_used{u}") for u in range(2)]
        self.n_tiles = 0
        self.n_stages, self.n_sems = 0, [0, 0]

    def lasting(self, name):
        return self.ctx.enter_context(self.nc.semaphore(name))

    def begin_stage(self):
        self.n_stages += 1
        self.n_sems[self.n_stages % 2] = 0
        return self.n_stages - 1

    def sem(self, name):
        turn = self.n_stages % 2
        num = FIRST_SEM + turn * STAGE_SEMS + self.n_sems[turn]
        self.n_sems[turn] += 1
        assert self.n_sems[turn] <= STAGE_SEMS, name
        with self.nc.semaphore(name, num=num) as handle:
            return handle

    def clear_sems(self, pool, n):
        first = FIRST_SEM + (n + 1) % 2 * STAGE_SEMS
        pool.sem_clear(range(first, first + STAGE_SEMS))

    def view(self, at, *shape):
        n = int(np.prod(shape))
        v = self.sbuf[:, at:at + n]
        if len(shape) == 2:
            v = v.rearrange("p (a b) -> p a b", b=shape[1])
        if len(shape) == 3:
            v = v.rearrange("p (a b c) -> p a b c", b=shape[1], c=shape[2])
        return v

    def bank(self, b, n=512, at=0):
        return self.psum[:, b, at:at + n]

    def vec(self, name, col=0, n=None):
        off, w = VOFF[name]
        return self.sbuf[:, A_VEC + off + col:A_VEC + off + col + (w - col if n is None else n)]

    def vec_at(self, name, col):
        off, w = VOFF[name]
        return self.sbuf[:, A_VEC + off:A_VEC + off + w][:, bass.ds(col, 1)]

    def const(self, name):
        off, w = COFF[name]
        return self.sbuf[:, A_CONST + off:A_CONST + off + w]


def one(v, i):
    v = v[:, bass.ds(i, 1)]
    if len(v.shape) == 2:
        return v
    return v.rearrange("p o a -> p (o a)") if len(v.shape) == 3 else v.rearrange("p o a b -> p (o a) b")


def over(v, n):
    return v.unsqueeze(len(v.shape)).broadcast_to(list(v.shape) + [n])


def across(v, n):
    return v.unsqueeze(1).broadcast_to([v.shape[0], n] + list(v.shape[1:]))


class Weights:

    def __init__(self, chip, name, n, words):
        self.chip, self.dram, self.n, self.words = chip, chip.dram[name], n, words
        self.first = chip.n_tiles
        chip.n_tiles += n

    def slot(self, u):
        return (self.first + u) % 2

    def view(self, u, *shape):
        return self.chip.view(A_W + self.slot(u) * WSLOT, *shape)

    def load(self, sp):
        def tile(i, u, src):
            sp.wait_ge(self.chip.slot_used[self.slot(u)], i + (self.first + u) // 2 + 1)
            sp.dma_start(self.view(u, self.words), src).then_inc(self.chip.slot_landed[self.slot(u)], 16)

        if self.n == 1:
            return tile(0, 0, self.dram[0])
        with sp.Fori(0, self.n // 2) as i:
            for u in range(2):
                tile(i, u, self.dram[bass.ds(2 * i + u, 1)].rearrange("o p w -> (o p) w"))

    def landed(self, eng, i, u):
        eng.wait_ge(self.chip.slot_landed[self.slot(u)], 16 * i + 16 * ((self.first + u) // 2 + 1))

    def used(self, u):
        return self.chip.slot_used[self.slot(u)]

    def summed(self, eng, i, u):
        eng.wait_ge(self.chip.slot_used[self.slot(u)], i + (self.first + u) // 2 + 2)


def products(nc, out, pairs):
    last = None
    for n, (w, x) in enumerate(pairs):
        last = nc.tensor.matmul(out, w, x, start=(n == 0), stop=(n == len(pairs) - 1))
    return last


def pairs(eng, n, body):
    if n == 1:
        return body(0, 0)
    with eng.Fori(0, n // 2) as i:
        for u in range(2):
            body(i, u)


class Stage:
    def __init__(self, chip):
        self.chip, self.nc = chip, chip.nc
        self.index = chip.begin_stage()

    def sync(self, sp):
        pass

    def tensor(self, pe):
        pass

    def scalar(self, act):
        pass

    def vector(self, dve):
        pass

    def gpsimd(self, pool):
        pass


class Inputs(Stage):

    def __init__(self, chip):
        super().__init__(chip)
        self.here = chip.sem("inputs_here")

    def sync(self, sp):
        c, d = self.chip, self.chip.dram
        for at, name in ((A_VEC, "vec"), (A_CONST, "const"), (A_XL, "x_in"), (A_XC, "ctx1_in")):
            sp.dma_start(c.view(at, d[name].shape[1]), d[name]).then_inc(self.here, 16)

    def tensor(self, pe):
        pe.wait_ge(self.here, 64)
        for s in self.chip.slot_used:
            pe.sem_inc(s, 1)

    def scalar(self, act):
        act.wait_ge(self.here, 64)

    def vector(self, dve):
        dve.wait_ge(self.here, 64)

    def gpsimd(self, pool):
        pool.wait_ge(self.here, 64)


class LoadContext(Stage):

    def __init__(self, chip):
        super().__init__(chip)
        self.here = chip.lasting("context_here")

    def sync(self, sp):
        sp.wait_ge(self.chip.stage_done, 4 * self.index)
        sp.dma_start(self.chip.view(A_XC, KD * TC), self.chip.dram["ctx2_in"]).then_inc(self.here, 16)


class NewContext(Stage):

    def __init__(self, chip, load):
        super().__init__(chip)
        self.here = load.here

    def tensor(self, pe):
        pe.wait_ge(self.here, 16)

    def scalar(self, act):
        act.wait_ge(self.here, 16)

    def vector(self, dve):
        dve.wait_ge(self.here, 16)

    def gpsimd(self, pool):
        pool.wait_ge(self.here, 16)


class Modulation(Stage):

    def __init__(self, chip, weights, n, conds, bias, out_at):
        super().__init__(chip)
        self.w = Weights(chip, weights, n, 4 * D)
        self.n, self.conds, self.bias = n, conds, bias
        self.out = chip.view(out_at, 4 * n, 2)
        self.cond = chip.view(A_SMALL, KD, 2)
        self.rows = chip.view(A_WORK, n, 512)[0:2]
        self.cond_ready, self.copied, self.turned = (chip.sem(weights + s) for s in ("_cond", "_copied", "_turned"))

    def sync(self, sp):
        self.w.load(sp)

    def scalar(self, act):
        a = self.nc.scalar
        for n, name in enumerate(self.conds):
            a.activation(self.cond[:, :, n], self.chip.vec(name), ACT.Silu).then_inc(self.cond_ready, 1)
        act.sem_inc(self.copied, 2)

        def body(i, u):
            self.w.summed(act, i, u)
            a.activation(one(self.rows, 2 * i + u), self.chip.bank(u)[0:2], ACT.Copy).then_inc(self.copied, 1)
        pairs(act, self.n, body)

    def tensor(self, pe):
        t = self.nc.tensor
        pe.wait_ge(self.cond_ready, 2)

        def body(i, u):
            self.w.landed(pe, i, u)
            pe.wait_ge(self.copied, 2 * i + u + 1)
            w = self.w.view(u, KD, 512)
            products(self.nc, self.chip.bank(u)[0:2], [(self.cond[:, k], w[:, k]) for k in range(KD)]).then_inc(self.w.used(u), 1)
        pairs(pe, self.n, body)
        pe.wait_ge(self.copied, self.n + 2)
        for m in range(4 * self.n):
            last = t.matmul(self.chip.bank(2, 2, 2 * m), self.rows[:, m // 4, P * (m % 4):P * (m % 4) + P],
                            self.chip.const("ident")[0:2, 0:2], start=True, stop=True)
        last.then_inc(self.turned, 1)

    def vector(self, dve):
        dve.wait_ge(self.turned, 1)
        self.nc.vector.tensor_tensor(self.out, self.chip.bank(2, 8 * self.n).rearrange("p (m c) -> p m c", c=2),
                                     over(self.chip.vec(self.bias), 2), ALU.add)


SIDE = A_END - 5 * D


class SideModulation:
    SLOTS = 3
    BLOCKS = 4 * 3 * KD
    HOSTS = [(((0, 1), (2, 0)), KX // 2), (((1,), (2,)), KS // 2), (((0, 1, 2, 0), (1, 2, 0, 1)), KD // 2)]

    def __init__(self, chip):
        self.chip, self.nc = chip, chip.nc
        self.slot = [chip.view(SIDE + b * D, D) for b in range(self.SLOTS)]
        self.rows = chip.view(SIDE + self.SLOTS * D, 2, D)
        self.products = chip.psum[:, 6:8].rearrange("p b w -> p (b w)")
        self.sums = chip.view(A_SIDE, self.SLOTS, 2)
        self.out = chip.view(A_MOD2, self.BLOCKS, 2)
        self.landed = [chip.lasting(f"side_landed{b}") for b in range(self.SLOTS)]
        self.used = [chip.lasting(f"side_used{b}") for b in range(self.SLOTS)]
        self.rows_in, self.rows_ready = chip.lasting("side_rows_in"), chip.lasting("side_rows_ready")

    def rows_of(self, pool):
        pool.dma_start(self.rows.rearrange("p c k -> p (c k)"), self.chip.dram["cond_rows2"]).then_inc(self.rows_in, 16)

    def silu(self, act, host):
        act.wait_ge(self.rows_in, 16 * host + 16)
        self.nc.scalar.activation(self.rows, self.rows, ACT.Silu).then_inc(self.rows_ready, 1)

    def start(self, dve, host):
        if host == 0:
            for s in self.used:
                dve.sem_inc(s, 1)
        dve.wait_ge(self.rows_ready, host + 1)

    def plan(self, host, i, u):
        uses, block = [0] * self.SLOTS, 0
        for steps, turns in self.HOSTS[:host]:
            for slots in steps:
                block += turns * len(slots)
                for b in slots:
                    uses[b] += turns
        steps = self.HOSTS[host][0]
        turn = steps[0] + steps[1]
        for n, b in enumerate(turn):
            if (n >= len(steps[0])) == (u == 1):
                yield b, i * turn.count(b) + (uses[b] + turn[:n].count(b)), i * len(turn) + (block + n)

    def load(self, pool, host, i, u):
        for b, uses, block in self.plan(host, i, u):
            src = self.chip.dram["w_mod2"][bass.ds(block, 1)].rearrange("o p k -> (o p) k")
            pool.wait_ge(self.used[b], uses + 1)
            pool.dma_start(self.slot[b], src).then_inc(self.landed[b], 16)

    def reduce(self, dve, host, i, u):
        v = self.nc.vector
        for b, uses, block in self.plan(host, i, u):
            dve.drain()
            dve.wait_ge(self.landed[b], uses * 16 + 16)
            for c in range(2):
                last = v.tensor_tensor_reduce(self.products, self.slot[b], self.rows[:, c], 1.0, 0.0, ALU.mult, ALU.add,
                                              self.sums[:, b, c:c + 1])
                if c == 0:
                    dve.drain()
            last.then_inc(self.used[b], 1)
            dve.drain()
            v.tensor_tensor(one(self.out, block), self.sums[:, b], self.chip.vec_at("ada_b", block).broadcast_to([P, 2]), ALU.add)


class Norm(Stage):

    def __init__(self, chip, name, jobs, work):
        super().__init__(chip)
        self.jobs, self.work = jobs, work
        self.squared, self.summed, self.rooted, self.scaled = (
            chip.sem(f"{name}_{s}") for s in ("squared", "summed", "rooted", "scaled"))

    def places(self):
        at = self.work
        for n, job in enumerate(self.jobs):
            k, t = job["x"].shape[1:]
            yield job, n, self.chip.view(at, k, t), self.chip.view(at, t), self.chip.view(at + t, t), \
                self.chip.view(A_SMALL + 32 * n, k), k, t
            at += k * t

    def scalar(self, act):
        a = self.nc.scalar
        for job, n, squares, rms, inv, factor, k, t in self.places():
            for i in range(k):
                a.activation(squares[:, i], job["x"][:, i], ACT.Square).then_inc(self.squared, 1)
        for job, n, squares, rms, inv, factor, k, t in self.places():
            act.wait_ge(self.summed, n + 1)
            a.activation(rms, self.chip.bank(n, t), ACT.Sqrt, scale=1.0 / (k * P), bias=EPS).then_inc(self.rooted, 1)
        done = 0
        for job, n, squares, rms, inv, factor, k, t in self.places():
            if job.get("shift") is not None:
                for i in range(k):
                    act.wait_ge(self.scaled, done + i + 1)
                    a.activation(job["out"][:, i], job["out"][:, i], ACT.Identity, bias=job["shift"][:, i:i + 1])
            done += k

    def tensor(self, pe):
        done = 0
        for job, n, squares, rms, inv, factor, k, t in self.places():
            for i in range(k):
                pe.wait_ge(self.squared, done + i + 1)
                last = self.nc.tensor.matmul(self.chip.bank(n, t), self.chip.const("ones"), squares[:, i], start=(i == 0), stop=(i == k - 1))
            last.then_inc(self.summed, 1)
            done += k

    def vector(self, dve):
        v = self.nc.vector
        for job, n, squares, rms, inv, factor, k, t in self.places():
            if job.get("scale") is None:
                v.tensor_copy(factor, job["gain"])
            elif job.get("gain") is None:
                v.tensor_scalar(factor, job["scale"], 1.0, None, ALU.add)
            else:
                v.scalar_tensor_tensor(factor, job["scale"], 1.0, job["gain"], ALU.add, ALU.mult)
        for job, n, squares, rms, inv, factor, k, t in self.places():
            dve.wait_ge(self.rooted, n + 1)
            v.reciprocal(inv, rms)
            dve.drain()
            for i in range(k):
                v.scalar_tensor_tensor(job["out"][:, i], job["x"][:, i], factor[:, i:i + 1], inv, ALU.mult, ALU.mult).then_inc(self.scaled, 1)


PAD = T + 3
PL, PC = 1, TL + 2
XBC = A_WORK
DT = XBC + KX * T
LA = DT + NT * 64
SSDW = LA + NT * 64


def conv3(nc, dve, acc, raw, w, n):
    nc.vector.tensor_scalar(acc, raw[:, 0:n], w[0], None, ALU.mult)
    dve.drain()
    nc.vector.scalar_tensor_tensor(acc, raw[:, 1:n + 1], w[1], acc, ALU.mult, ALU.add)
    dve.drain()
    return nc.vector.scalar_tensor_tensor(acc, raw[:, 2:n + 2], w[2], acc, ALU.mult, ALU.add)


class Xbc(Stage):

    def __init__(self, chip, side):
        super().__init__(chip)
        self.side = side
        self.w = Weights(chip, "w_xbc", KX, D)
        self.h_lat, self.h_ctx = chip.view(A_HL, KD, TL), chip.view(A_HC, KD, TC)
        self.xbc = chip.view(XBC, KX, T)
        self.raw = [chip.view(SSDW + u * PAD, PAD) for u in range(2)]
        self.acc = [chip.view(SSDW + (2 + u) * PAD, PAD) for u in range(2)]
        self.padded, self.copied, self.convolved, self.activated = (
            chip.sem("xbc_" + s) for s in ("padded", "copied", "convolved", "activated"))

    def sync(self, sp):
        self.w.load(sp)

    def tensor(self, pe):
        with pe.Fori(0, KX // 2) as i:
            for u in range(2):
                self.w.landed(pe, i, u)
                pe.wait_ge(self.copied, 2 * i + u + 1)
                w = self.w.view(u, KD, P)
                products(self.nc, self.chip.bank(2 * u, TL), [(w[:, k], self.h_lat[:, k]) for k in range(KD)])
                products(self.nc, self.chip.bank(2 * u + 1, TC), [(w[:, k], self.h_ctx[:, k]) for k in range(KD)]
                         ).then_inc(self.w.used(u), 1)

    def gpsimd(self, pool):
        self.side.rows_of(pool)
        pairs(pool, KX, lambda i, u: self.side.load(pool, 0, i, u))

    def scalar(self, act):
        a = self.nc.scalar
        self.side.silu(act, 0)
        act.sem_inc(self.copied, 2)
        act.wait_ge(self.padded, 1)
        with act.Fori(0, KX // 2) as i:
            for u in range(2):
                self.w.summed(act, i, u)
                act.wait_ge(self.convolved, 2 * i + u + 1)
                a.activation(self.raw[u][:, PL:PL + TL], self.chip.bank(2 * u, TL), ACT.Copy)
                a.activation(self.raw[u][:, PC:PC + TC], self.chip.bank(2 * u + 1, TC), ACT.Copy
                             ).then_inc(self.copied, 1)
            for u in range(2):
                act.wait_ge(self.convolved, 2 * i + u + 3)
                j = 2 * i + u
                out, b = one(self.xbc, j), self.chip.vec_at("conv_b", j)
                a.activation(out[:, TC:T], self.acc[u][:, 0:TL], ACT.Silu, bias=b)
                a.activation(out[:, 0:TC], self.acc[u][:, PC - 1:PC - 1 + TC], ACT.Silu, bias=b
                             ).then_inc(self.activated, 1)

    def vector(self, dve):
        dve.sem_inc(self.convolved, 2)
        dve.sem_inc(self.activated, 2)
        for u in range(2):
            self.nc.vector.memset(self.raw[u], 0.0)
        dve.drain().then_inc(self.padded, 1)
        self.side.start(dve, 0)
        with dve.Fori(0, KX // 2) as i:
            for u in range(2):
                j = 2 * i + u
                dve.wait_ge(self.copied, j + 3)
                dve.wait_ge(self.activated, j + 1)
                conv3(self.nc, dve, self.acc[u][:, 0:T + 1], self.raw[u],
                      [self.chip.vec_at("conv_w", k * KX + j) for k in range(3)], T + 1).then_inc(self.convolved, 1)
                self.side.reduce(dve, 0, i, u)


class Dt(Stage):

    def __init__(self, chip):
        super().__init__(chip)
        self.w = Weights(chip, "w_dt", 1, KD * 64)
        self.h_lat, self.h_ctx = chip.view(A_HL, KD, TL), chip.view(A_HC, KD, TC)
        self.dt, self.la = chip.view(DT, NT * 64), chip.view(LA, NT * 64)
        self.y, self.s, self.s2, self.q = (chip.view(SSDW + n * NT * 64, NT * 64) for n in range(4))
        self.decay = chip.view(SSDW + 4 * NT * 64, 64)
        self.steps = [chip.sem(f"dt_{s}") for s in ("biased", "exp", "decay")]

    def sync(self, sp):
        self.w.load(sp)

    def tensor(self, pe):
        self.w.landed(pe, 0, 0)
        w = self.w.view(0, KD, 64)
        for t in range(NT):
            h, at = (self.h_ctx, t * P) if t < 2 else (self.h_lat, (t - 2) * P)
            last = products(self.nc, self.chip.bank(0, 64, 64 * t), [(h[:, k, at:at + P], w[:, k]) for k in range(KD)])
        last.then_inc(self.w.used(0), 1)

    def scalar(self, act):
        biased, expd, decay = self.steps
        self.nc.scalar.activation(self.decay, self.chip.vec("a_log"), ACT.Exp).then_inc(decay, 1)
        act.wait_ge(biased, 1)
        self.nc.scalar.activation(self.y, self.dt, ACT.Abs)
        act.drain()
        self.nc.scalar.activation(self.y, self.y, ACT.Exp, scale=-1.0).then_inc(expd, 1)

    def vector(self, dve):
        v = self.nc.vector
        biased, expd, decay = self.steps
        self.w.summed(dve, 0, 0)
        v.tensor_tensor(self.dt.rearrange("p (t h) -> p t h", h=64), self.chip.bank(0, NT * 64).rearrange("p (t h) -> p t h", h=64),
                        across(self.chip.vec("dt_bias"), NT), ALU.add).then_inc(biased, 1)
        dve.wait_ge(expd, 1)
        v.tensor_scalar(self.s, self.y, 2.0, None, ALU.add)
        dve.drain()
        v.reciprocal(self.s, self.s)
        dve.drain()
        v.tensor_tensor(self.s, self.s, self.y, ALU.mult)
        dve.drain()
        v.tensor_tensor(self.s2, self.s, self.s, ALU.mult)
        dve.drain()
        v.tensor_scalar(self.q, self.s2, 1.0 / 17, None, ALU.mult)
        for n in (15, 13, 11, 9, 7, 5, 3):
            dve.drain()
            v.scalar_tensor_tensor(self.q, self.q, 1.0 / n, self.s2, ALU.add, ALU.mult)
        dve.drain()
        v.scalar_tensor_tensor(self.q, self.q, 1.0, self.s, ALU.add, ALU.mult)
        v.tensor_scalar(self.dt, self.dt, 0.0, None, ALU.max)
        dve.drain()
        v.scalar_tensor_tensor(self.dt, self.q, 2.0, self.dt, ALU.mult, ALU.add)
        dve.wait_ge(decay, 1)
        dve.drain()
        v.scalar_tensor_tensor(self.la.rearrange("p (t h) -> p t h", h=64), self.dt.rearrange("p (t h) -> p t h", h=64),
                               -1.0, across(self.decay, NT), ALU.mult, ALU.mult)


HB = A_HL


def meet(eng, sem, i):
    eng.drain().then_inc(sem, 1)
    eng.wait_ge(sem, 4 * i + 4)


class SsdStates(Stage):
    STEPS = 5

    def __init__(self, chip):
        super().__init__(chip)
        self.xbc, self.dt, self.la = chip.view(XBC, KX, T), chip.view(DT, NT, 64), chip.view(LA, NT, 64)
        self.chunk = chip.view(HB, 20, P)
        self.xw = chip.view(HB + 20 * P, 4, 512)
        self.b_tok = chip.view(HB + 36 * P, 4, P)
        self.state = [chip.view(SSDW + d * D_SSD, 4, 512) for d in range(2)]
        self.weight = chip.view(A_SMALL, 32)
        self.decay = chip.view(A_SMALL + 32, 64)
        (self.met, self.staged, self.x_staged, self.turned, self.decayed, self.weighted, self.evac, self.b_out,
         self.shrunk, self.summed, self.updated, self.stored) = (
            chip.sem("states_" + n) for n in (
                "met staged x_staged turned decayed weighted evac b_out shrunk summed updated stored").split())

    def chunks(self, i, d, late):
        return i if d == 0 else i * -1 + (7 if late else 1)

    def passes(self, eng, body):
        for late, (a, b) in enumerate(((0, 2), (2, self.STEPS))):
            with eng.Fori(a, b) as i:
                for d in range(2):
                    body(i, d, self.chunks(i, d, late), 2 * i + d)

    def sync(self, sp):
        def body(i, d, c, n):
            sp.wait_ge(self.updated, 4 * n + 4)
            sp.dma_start(self.chip.dram["states"][bass.ds(n, 1)].rearrange("o p w -> (o p) w"),
                         self.state[d].rearrange("p g w -> p (g w)")).then_inc(self.stored, 16)
        self.passes(sp, body)
        sp.wait_ge(self.stored, 16 * 2 * self.STEPS + 16)

    def scalar(self, act):
        a = self.nc.scalar

        def body(i, d, c, n):
            meet(act, self.met, n)
            a.activation(self.chunk[:, 8:20], self.xbc[:, 8:20, bass.ds(c * P, P)], ACT.Copy).then_inc(self.staged, 1)
            act.wait_ge(self.decayed, n + 1)
            a.activation(self.decay, self.chip.bank(5, 64), ACT.Exp).then_inc(self.weighted, 1)
            act.wait_ge(self.turned, 5 * n + 5)
            a.activation(self.b_tok.rearrange("p g w -> p (g w)"), self.chip.bank(4), ACT.Copy).then_inc(self.b_out, 1)
        self.passes(act, body)

    def gpsimd(self, pool):
        def body(i, d, c, n):
            meet(pool, self.met, n)
            pool.wait_ge(self.weighted, n + 1)
            pool.wait_ge(self.stored, 16 * n + 16)
            for g in range(GROUPS):
                s = self.state[d][:, g].rearrange("p (h e) -> p h e", e=SSD_P)
                self.nc.gpsimd.tensor_tensor(s, s, over(self.decay[:, 32 + 8 * g:40 + 8 * g], SSD_P), ALU.mult).then_inc(self.shrunk, 1)
        self.passes(pool, body)

    def tensor(self, pe):
        t = self.nc.tensor
        ident = self.chip.const("ident")

        def body(i, d, c, n):
            meet(pe, self.met, n)
            la = one(self.la, c)[:, 32 * d:32 * d + 32]
            t.matmul(self.chip.bank(5, 32), self.chip.const("after" if d == 0 else "before"), la, start=True, stop=True)
            t.matmul(self.chip.bank(5, 32, 32), self.chip.const("ones"), la, start=True, stop=True).then_inc(self.decayed, 1)
            pe.wait_ge(self.x_staged, n + 1)
            for m in range(20):
                if m == 8:
                    pe.wait_ge(self.staged, n + 1)
                last = t.transpose(self.chip.bank(m // 4, P, P * (m % 4)), self.chunk[:, m], ident)
                if m % 4 == 3:
                    last.then_inc(self.turned, 1)
            pe.wait_ge(self.b_out, n + 1)
            for g in range(GROUPS):
                pe.wait_ge(self.evac, 4 * n + g + 1)
                t.matmul(self.chip.bank(g), self.b_tok[:, g], self.xw[:, g], start=True, stop=True).then_inc(self.summed, 1)
        self.passes(pe, body)

    def vector(self, dve):
        v = self.nc.vector
        for d in range(2):
            v.memset(self.state[d], 0.0)

        def body(i, d, c, n):
            meet(dve, self.met, n)
            v.tensor_copy(self.chunk[:, 0:8], self.xbc[:, 0:8, bass.ds(c * P, P)]).then_inc(self.x_staged, 1)
            dve.wait_ge(self.weighted, n + 1)
            v.tensor_tensor(self.weight, self.decay[:, 0:32], one(self.dt, c)[:, 32 * d:32 * d + 32], ALU.mult)
            dve.drain()
            for g in range(GROUPS):
                dve.wait_ge(self.turned, 5 * n + g + 1)
                v.tensor_tensor(self.xw[:, g].rearrange("p (h e) -> p h e", e=SSD_P),
                                self.chip.bank(g).rearrange("p (h e) -> p h e", e=SSD_P),
                                over(self.weight[:, 8 * g:8 * g + 8], SSD_P), ALU.mult).then_inc(self.evac, 1)
            for g in range(GROUPS):
                dve.wait_ge(self.shrunk, 4 * n + g + 1)
                dve.wait_ge(self.summed, 4 * n + g + 1)
                v.tensor_tensor(self.state[d][:, g], self.state[d][:, g], self.chip.bank(g), ALU.add).then_inc(self.updated, 1)
        dve.sem_inc(self.stored, 16)
        self.passes(dve, body)


class SsdOutput(Stage):

    def __init__(self, chip):
        super().__init__(chip)
        self.xbc, self.dt, self.la = chip.view(XBC, KX, T), chip.view(DT, NT, 64), chip.view(LA, NT, 64)
        self.chunk = chip.view(HB, KX, P)
        self.x_dt = [chip.view(HB + 24 * P, D_SSD), chip.view(SSDW, D_SSD)]
        self.cb = [chip.view(HB + 40 * P + 512 * d, 4, P) for d in range(2)]
        self.state = [chip.view(SSDW + (1 + d) * D_SSD, D_SSD) for d in range(2)]
        at = SSDW + 3 * D_SSD
        self.c_dec = [chip.view(at + 512 * b, 4, P) for b in range(4)]
        self.m = [chip.view(A_W + D + 512 * b, 4, P) for b in range(4)]
        self.la_here = chip.view(A_SMALL, 64)
        self.dt_here = chip.view(A_SMALL + 64, 64)
        self.cum = chip.view(A_SMALL + 128, 64)
        (self.met, self.staged, self.x_staged, self.states_in, self.turned, self.scaled, self.bc, self.masked,
         self.cum_sum, self.cum_out, self.spread, self.grown, self.cut, self.exped, self.decayed_m,
         self.decayed_c, self.multiplied, self.evac) = (
            chip.sem("ssd_" + n) for n in (
                "met staged x_staged states_in turned scaled bc masked cum_sum cum_out spread grown cut exped "
                "decayed_m decayed_c multiplied evac").split())
        self.zero = chip.view(A_SMALL + 192, P)

    def y_bank(self, q, m):
        return self.chip.bank((6, 0)[q % 2] + m, P)

    def spread_bank(self, s, *part):
        return self.chip.bank((4, 5, 2, 3)[s % 4], *part)

    def sync(self, sp):
        sp.wait_ge(self.chip.stage_done, 4 * self.index)
        with sp.Fori(0, 4) as i:
            sp.wait_ge(self.met, 4 * i + 4)
            for d in range(2):
                n = 2 * i + 2 if d == 0 else i * -2 + 9
                sp.dma_start(self.state[d], self.chip.dram["states"][bass.ds(n, 1)].rearrange("o p w -> (o p) w")
                             ).then_inc(self.states_in, 16)

    def gpsimd(self, pool):
        g = self.nc.gpsimd
        with pool.Fori(0, 4) as i:
            meet(pool, self.met, i)
            g.tensor_copy(self.la_here, one(self.la, i + 2))
            g.tensor_copy(self.dt_here, one(self.dt, i + 2)).then_inc(self.staged, 1)
            pool.wait_ge(self.masked, 2 * i + 2)
            for s in range(16):
                q, d = s // 2, s % 2
                pool.wait_ge(self.exped, 16 * i + s + 1)
                m = self.m[s % 4]
                g.tensor_tensor(m, m, across(self.cb[d][:, q // 2], 4), ALU.mult).then_inc(self.decayed_m, 1)

    def scalar(self, act):
        a = self.nc.scalar
        with act.Fori(0, 4) as i:
            meet(act, self.met, i)
            a.activation(self.chunk[:, 8:KX], self.xbc[:, 8:KX, bass.ds(i * P + 2 * P, P)], ACT.Copy).then_inc(self.staged, 1)
            act.wait_ge(self.cum_sum, i + 1)
            a.activation(self.cum, self.chip.bank(5, 64), ACT.Copy).then_inc(self.cum_out, 1)
            for s in range(16):
                act.wait_ge(self.cut, 16 * i + s + 1)
                if s >= 4:
                    act.wait_ge(self.multiplied, 16 * i + s - 3)
                a.activation(self.c_dec[s % 4].rearrange("p h l -> p (h l)"), self.spread_bank(s), ACT.Exp
                             ).then_inc(self.grown, 1)
                a.activation(self.m[s % 4], self.m[s % 4], ACT.Exp).then_inc(self.exped, 1)

    def tensor(self, pe):
        t = self.nc.tensor
        c = self.chip
        with pe.Fori(0, 4) as i:
            meet(pe, self.met, i)
            pe.wait_ge(self.x_staged, i + 1)
            for m in range(16):
                if m == 8:
                    pe.wait_ge(self.staged, 2 * i + 2)
                last = t.transpose(c.bank(m // 4, P, P * (m % 4)), self.chunk[:, m], c.const("ident"))
                if m % 4 == 3:
                    last.then_inc(self.turned, 1)
            for g in range(GROUPS):
                last = t.matmul(c.bank(4, P, P * g), self.chunk[:, 16 + g], self.chunk[:, 20 + g], start=True, stop=True)
            last.then_inc(self.bc, 1)
            t.matmul(c.bank(5, 32), c.const("upto"), self.la_here[:, 0:32], start=True, stop=True)
            t.matmul(c.bank(5, 32, 32), c.const("from"), self.la_here[:, 32:64], start=True, stop=True).then_inc(self.cum_sum, 1)
            pe.wait_ge(self.masked, 2 * i + 2)
            pe.wait_ge(self.cum_out, i + 1)

            def spread(s):
                q, d = s // 2, s % 2
                if s >= 4:
                    pe.wait_ge(self.grown, 16 * i + s - 3)
                for h in range(4):
                    col = 32 * d + 4 * q + h
                    last = t.matmul(self.spread_bank(s, P, P * h), self.la_here[:, col:col + 1].broadcast_to([P, P]),
                                    c.const("upto" if d == 0 else "from"), start=True, stop=True)
                last.then_inc(self.spread, 1)

            spread(0)
            spread(1)
            pe.wait_ge(self.scaled, 8 * i + 8)
            spread(2)
            pe.wait_ge(self.states_in, 32 * i + 32)
            for s in range(16):
                q, d = s // 2, s % 2
                if s + 3 < 16:
                    spread(s + 3)
                pe.wait_ge(self.decayed_m, 16 * i + s + 1)
                pe.wait_ge(self.decayed_c, 16 * i + s + 1)
                if q >= 2 and d == 0:
                    pe.wait_ge(self.evac, 8 * i + q - 1)
                for h in range(4):
                    head = 4 * q + h
                    out = self.y_bank(q, h // 2)[64 * (h % 2):64 * (h % 2) + 64]
                    t.matmul(out, self.x_dt[d][:, 64 * head:64 * head + 64], self.m[s % 4][:, h], start=(d == 0), stop=False)
                    last = t.matmul(out, self.state[d][:, 64 * head:64 * head + 64], self.c_dec[s % 4][:, h],
                                    start=False, stop=(d == 1))
                last.then_inc(self.multiplied, 1)

    def vector(self, dve):
        v = self.nc.vector
        c = self.chip
        v.memset(self.zero, 0.0)
        with dve.Fori(0, 4) as i:
            meet(dve, self.met, i)
            v.tensor_copy(self.chunk[:, 0:8], self.xbc[:, 0:8, bass.ds(i * P + 2 * P, P)]).then_inc(self.x_staged, 1)
            dve.wait_ge(self.staged, 2 * i + 2)
            for g in range(GROUPS):
                dve.wait_ge(self.turned, 4 * i + g + 1)
                for d in range(2):
                    v.tensor_tensor(self.x_dt[d][:, 512 * g:512 * g + 512].rearrange("p (h e) -> p h e", e=SSD_P),
                                    c.bank(g).rearrange("p (h e) -> p h e", e=SSD_P),
                                    over(self.dt_here[:, 32 * d + 8 * g:32 * d + 8 * g + 8], SSD_P), ALU.mult
                                    ).then_inc(self.scaled, 1)
            dve.wait_ge(self.bc, i + 1)
            for d, mask in enumerate(("upto", "from")):
                v.tensor_tensor(self.cb[d], c.bank(4).rearrange("p (g l) -> p g l", l=P), across(c.const(mask), 4), ALU.mult
                                ).then_inc(self.masked, 1)
            dve.wait_ge(self.cum_out, i + 1)

            def out(q):
                dve.wait_ge(self.multiplied, 16 * i + 2 * q + 2)
                for m in range(2):
                    tile = 2 * q + m
                    last = v.scalar_tensor_tensor(self.xbc[:, tile, bass.ds(i * P + 2 * P, P)], self.chunk[:, tile],
                                                  c.vec("ssd_d", tile, 1), self.y_bank(q, m), ALU.mult, ALU.add)
                last.then_inc(self.evac, 1)

            def cut(s):
                q, d = s // 2, s % 2
                dve.wait_ge(self.spread, 16 * i + s + 1)
                if s >= 4:
                    dve.wait_ge(self.multiplied, 16 * i + s - 3)
                for h in range(4):
                    col = 32 * d + 4 * q + h
                    last = v.scalar_tensor_tensor(self.m[s % 4][:, h], self.spread_bank(s, P, P * h), self.cum[:, col:col + 1],
                                                  self.zero, ALU.subtract, ALU.min)
                last.then_inc(self.cut, 1)

            cut(0)
            for s in range(16):
                if s + 1 < 16:
                    cut(s + 1)
                dve.wait_ge(self.grown, 16 * i + s + 1)
                v.tensor_tensor(self.c_dec[s % 4], self.c_dec[s % 4], across(self.chunk[:, 20 + s // 4], 4), ALU.mult
                                ).then_inc(self.decayed_c, 1)
                if s >= 5 and s % 2:
                    out((s - 5) // 2)
            out(6)
            out(7)


class GateZ(Stage):

    def __init__(self, chip, side):
        super().__init__(chip)
        self.side = side
        self.w = Weights(chip, "w_z", KS, D)
        self.h = chip.view(A_HL, KD, TL)
        self.y = chip.view(XBC, KX, T)
        self.z = [chip.view(SSDW + u * TL, TL) for u in range(2)]
        self.activated, self.used = chip.sem("z_activated"), chip.sem("z_used")

    def sync(self, sp):
        self.w.load(sp)

    def gpsimd(self, pool):
        self.side.rows_of(pool)
        pairs(pool, KS, lambda i, u: self.side.load(pool, 1, i, u))

    def tensor(self, pe):
        with pe.Fori(0, KS // 2) as i:
            for u in range(2):
                self.w.landed(pe, i, u)
                pe.wait_ge(self.activated, 2 * i + u + 1)
                w = self.w.view(u, KD, P)
                products(self.nc, self.chip.bank(u), [(w[:, k], self.h[:, k]) for k in range(KD)]).then_inc(self.w.used(u), 1)

    def scalar(self, act):
        self.side.silu(act, 1)
        act.sem_inc(self.activated, 2)
        with act.Fori(0, KS // 2) as i:
            for u in range(2):
                self.w.summed(act, i, u)
                act.wait_ge(self.used, 2 * i + u + 1)
                self.nc.scalar.activation(self.z[u], self.chip.bank(u), ACT.Silu).then_inc(self.activated, 1)

    def vector(self, dve):
        dve.sem_inc(self.used, 2)
        self.side.start(dve, 1)
        with dve.Fori(0, KS // 2) as i:
            for u in range(2):
                dve.wait_ge(self.activated, 2 * i + u + 3)
                y = one(self.y, 2 * i + u)[:, TC:T]
                self.nc.vector.tensor_tensor(y, y, self.z[u], ALU.mult).then_inc(self.used, 1)
                self.side.reduce(dve, 1, i, u)


ATT = A_WORK + KS * T
Y_ATT = ATT


class Attention(Stage):

    def __init__(self, chip):
        super().__init__(chip)
        self.w = Weights(chip, "w_qkv", KV, KD * 448)
        self.h_lat, self.h_ctx = chip.view(A_HL, KD, TL), chip.view(A_HC, KD, TC)
        self.y = chip.view(Y_ATT, KD, TL)
        at = ATT + KD * TL
        self.tables = chip.view(at, 2 * TL + P)
        self.cos, self.sin = chip.view(at, TL), chip.view(at + TL, TL)
        self.swap = chip.view(at + 2 * TL, P)
        at += 2 * TL + P
        self.mask = chip.view(at, 3 * P)
        at += 3 * P
        self.k = chip.view(at, T)
        at += T
        self.v = chip.view(at, NT, DH)
        at += NT * DH
        assert KD * 448 + 3 * TL <= WSLOT
        self.raw = [chip.view(A_W + self.w.slot(1) * WSLOT + KD * 448 + n * TL, TL) for n in range(3)]
        self.q = [chip.view(at + n * TL, TL) for n in range(2)]
        at += 2 * TL
        self.s = [chip.view(at + b * 4 * 640, 4, 640) for b in range(2)]
        at += 2 * 4 * 640
        self.pt = chip.view(at, 5, 512)
        assert at + 5 * 512 <= A_END
        small = A_SMALL
        self.mx, self.neg, self.den, self.es, self.inv = (chip.view(small + 4 * n, 4) for n in range(5))
        (self.tables_in, self.projected, self.copied, self.swapped, self.rotated, self.values_out,
         self.scored, self.masked, self.peaked, self.exped, self.normed, self.turned, self.pt_out,
         self.summed, self.out, self.cosined, self.ctx_out) = (
            chip.sem("att_" + n) for n in (
                "tables_in projected copied swapped rotated values_out scored masked peaked exped normed "
                "turned pt_out summed out cosined ctx_out").split())

    @staticmethod
    def window(n):
        a, b = max(0, n - 1) * P, min(4, n + 2) * P
        return a, b - a

    def key_tiles(self, n):
        a, w = self.window(n)
        return [2 + a // P + m for m in range(w // P)] + [0, 1]

    PT_PER = sum([4, 5, 5, 4])

    def body(self, eng, run):
        with eng.Fori(0, KV // 2) as i:
            for u in range(2):
                run(i, u, 2 * i + u)

    def sync(self, sp):
        sp.wait_ge(self.chip.stage_done, 4 * self.index)
        sp.dma_start(self.tables, self.chip.dram["rope_att"]).then_inc(self.tables_in, 16)
        sp.dma_start(self.mask, self.chip.dram["win_mask"]).then_inc(self.tables_in, 16)
        self.w.load(sp)

    def tensor(self, pe):
        t, c = self.nc.tensor, self.chip
        pe.wait_ge(self.tables_in, 32)

        def values(w, tiles):
            for m in tiles:
                h, at = (self.h_ctx, m * P) if m < 2 else (self.h_lat, (m - 2) * P)
                last = products(self.nc, c.bank(4, DH, DH * m), [(h[:, k, at:at + P], w[:, k, 384:448]) for k in range(KD)])
            return last

        def scores(g, n, heads):
            a, width = self.window(n)
            for h in heads:
                half = slice(64 * (h % 2), 64 * (h % 2) + 64)
                if n > 0 or h >= 2:
                    pe.wait_ge(self.masked, 16 * g + 4 * n + h - 1)
                    pe.wait_ge(self.ctx_out, 16 * g + 4 * n + h - 1)
                q = self.q[h // 2][half, P * n:P * n + P]
                t.matmul(c.bank(2 * (h % 2), width), q, self.k[half, TC + a:TC + a + width], start=True, stop=True)
                t.matmul(c.bank(2 * (h % 2) + 1, TC), q, self.k[half, 0:TC], start=True, stop=True).then_inc(self.scored, 1)

        def run(i, u, g):
            w = self.w.view(u, KD, 448)
            self.w.landed(pe, i, u)
            products(self.nc, c.bank(0), [(w[:, k, 256:384], self.h_lat[:, k]) for k in range(KD)]).then_inc(self.projected, 1)
            for m in range(2):
                products(self.nc, c.bank(1 + m), [(w[:, k, P * m:P * m + P], self.h_lat[:, k]) for k in range(KD)]
                         ).then_inc(self.projected, 1)
            products(self.nc, c.bank(3, TC), [(w[:, k, 256:384], self.h_ctx[:, k]) for k in range(KD)]).then_inc(self.projected, 1)
            pe.wait_ge(self.out, 4 * g + 4)
            for n in range(3):
                pe.wait_ge(self.copied, 3 * g + n + 1)
                t.matmul(c.bank(5 + n), self.swap, self.raw[n], start=True, stop=True).then_inc(self.swapped, 1)
            values(w, (0, 1))
            pe.wait_ge(self.rotated, 4 * g + 4)
            scores(g, 0, (0, 1))
            values(w, (2, 3))
            scores(g, 0, (2, 3))
            values(w, (4, 5)).then_inc(self.w.used(u), 1)
            pe.wait_ge(self.values_out, g + 1)
            for n in range(4):
                if n < 3:
                    scores(g, n + 1, (0, 1))
                pe.wait_ge(self.normed, 4 * g + n + 1)
                done = sum([4, 5, 5, 4][:n])
                for j, tile in enumerate(self.key_tiles(n)):
                    x = done + j
                    if x >= 2:
                        pe.wait_ge(self.pt_out, self.PT_PER * g + x - 1)
                    for h in range(4):
                        last = t.transpose(c.bank(4 + x % 2, P, P * h), self.s[n % 2][:, h, P * j:P * j + P], c.const("ident"))
                    last.then_inc(self.turned, 1)
                    if n < 3 and j in (1, 2):
                        scores(g, n + 1, (j + 1,))
                if n > 0:
                    pe.wait_ge(self.out, 4 * g + n + 4)
                for j, tile in enumerate(self.key_tiles(n)):
                    pe.wait_ge(self.pt_out, self.PT_PER * g + done + j + 1)
                    p = self.pt[:, j].rearrange("p (m e q) -> p m e q", e=2, q=P)
                    for e in range(2):
                        last = t.matmul(c.bank(6, 2 * P)[64 * e:64 * e + 64], self.v[:, tile], p[:, :, e],
                                        start=(j == 0), stop=(j == len(self.key_tiles(n)) - 1))
                last.then_inc(self.summed, 1)

        self.body(pe, run)

    def scalar(self, act):
        a, c = self.nc.scalar, self.chip

        def context(g, n, heads):
            start, width = self.window(n)
            for h in heads:
                act.wait_ge(self.scored, 16 * g + 4 * n + h + 1)
                a.activation(self.s[n % 2][:, h, width:width + TC], c.bank(2 * (h % 2) + 1, TC), ACT.Copy).then_inc(self.ctx_out, 1)

        def run(i, u, g):
            for n in range(3):
                act.wait_ge(self.projected, 4 * g + n + 1)
                a.activation(self.raw[n], c.bank(n), ACT.Copy).then_inc(self.copied, 1)
            act.wait_ge(self.projected, 4 * g + 4)
            a.activation(self.k[:, 0:TC], c.bank(3, TC), ACT.Copy).then_inc(self.rotated, 1)
            context(g, 0, range(4))
            self.w.summed(act, i, u)
            a.activation(self.v.rearrange("p t e -> p (t e)"), c.bank(4, NT * DH), ACT.Copy).then_inc(self.values_out, 1)
            for n in range(4):
                start, width = self.window(n)
                act.wait_ge(self.peaked, 4 * g + n + 1)
                a.activation(self.es, self.es, ACT.Exp)
                for h in range(4):
                    x = self.s[n % 2][:, h, 0:width + TC]
                    a.activation(x, x, ACT.Exp, bias=self.neg[:, h:h + 1], scale=DH ** -0.5, accum_out=self.den[:, h:h + 1]
                                 ).then_inc(self.exped, 1)
                if n < 3:
                    context(g, n + 1, (0, 1))
                done = sum([4, 5, 5, 4][:n])
                for j in range(len(self.key_tiles(n))):
                    act.wait_ge(self.turned, self.PT_PER * g + done + j + 1)
                    a.activation(self.pt[:, j], c.bank(4 + (done + j) % 2), ACT.Copy).then_inc(self.pt_out, 1)
                    if n < 3 and j in (1, 2):
                        context(g, n + 1, (j + 1,))

        self.body(act, run)

    def gpsimd(self, pool):
        g_ = self.nc.gpsimd
        pool.wait_ge(self.tables_in, 32)

        def run(i, u, g):
            for n in range(3):
                pool.wait_ge(self.copied, 3 * g + n + 1)
                pool.wait_ge(self.swapped, 3 * g + n + 1)
                g_.tensor_tensor(self.raw[n], self.raw[n], self.cos, ALU.mult).then_inc(self.cosined, 1)

        self.body(pool, run)

    def vector(self, dve):
        v, c = self.nc.vector, self.chip
        dve.wait_ge(self.tables_in, 32)
        dve.sem_inc(self.out, 4)

        def peaks(g, n):
            start, width = self.window(n)
            m0 = P if n == 0 else 0
            s = self.s[n % 2]
            for h in range(4):
                dve.wait_ge(self.scored, 16 * g + 4 * n + h + 1)
                v.tensor_tensor(s[:, h, 0:width], c.bank(2 * (h % 2), width), self.mask[:, m0:m0 + width], ALU.add
                                ).then_inc(self.masked, 1)
                dve.wait_ge(self.masked, 16 * g + 4 * n + h + 1)
                dve.wait_ge(self.ctx_out, 16 * g + 4 * n + h + 1)
                v.tensor_reduce(self.mx[:, h:h + 1], s[:, h, 0:width + TC], AX.X, ALU.max)
            sink = c.vec("sink")[:, bass.ds(4 * g, 4)]
            dve.drain()
            v.scalar_tensor_tensor(self.mx, self.mx, DH ** -0.5, sink, ALU.mult, ALU.max)
            dve.drain()
            v.tensor_scalar(self.neg, self.mx, -1.0, None, ALU.mult)
            v.tensor_tensor(self.es, sink, self.mx, ALU.subtract).then_inc(self.peaked, 1)

        def out(g, n):
            dve.wait_ge(self.summed, 4 * g + n + 1)
            v.tensor_copy(self.y[:, bass.ds(2 * g, 2), P * n:P * n + P], c.bank(6, 2 * P).rearrange("p (m q) -> p m q", q=P)
                          ).then_inc(self.out, 1)

        def run(i, u, g):
            for n in range(3):
                to = self.k[:, TC:T] if n == 0 else self.q[n - 1]
                dve.wait_ge(self.swapped, 3 * g + n + 1)
                v.tensor_tensor(to, c.bank(5 + n), self.sin, ALU.mult)
                dve.drain()
                dve.wait_ge(self.cosined, 3 * g + n + 1)
                v.tensor_tensor(to, to, self.raw[n], ALU.add).then_inc(self.rotated, 1)
            peaks(g, 0)
            for n in range(4):
                start, width = self.window(n)
                for h in range(4):
                    dve.wait_ge(self.exped, 16 * g + 4 * n + h + 1)
                    den, inv = self.den[:, h:h + 1], self.inv[:, h:h + 1]
                    v.tensor_tensor(den, den, self.es[:, h:h + 1], ALU.add)
                    dve.drain()
                    v.reciprocal(inv, den)
                    dve.drain()
                    x = self.s[n % 2][:, h, 0:width + TC]
                    last = v.tensor_scalar(x, x, inv, None, ALU.mult)
                last.then_inc(self.normed, 1)
                if n > 0:
                    out(g, n - 1)
                if n < 3:
                    peaks(g, n + 1)
            out(g, 3)

        self.body(dve, run)


class Merge(Stage):

    def __init__(self, chip):
        super().__init__(chip)
        self.w = Weights(chip, "w_merge", KD, 40 * P)
        self.h = chip.view(A_HL, KD, TL)
        self.y_ssd, self.y_att = chip.view(XBC, KX, T), chip.view(Y_ATT, KD, TL)
        at = ATT + KD * TL
        self.out = chip.view(at, KD, TL)
        at += KD * TL
        self.gates = [[chip.view(at + (2 * u + n) * TL, TL) for n in range(2)] for u in range(2)]
        self.gated, self.merged = chip.sem("merge_gated"), chip.sem("merge_merged")
        self.gate_sums = chip.sem("merge_gate_sums")

    def sync(self, sp):
        self.w.load(sp)

    def tensor(self, pe):
        with pe.Fori(0, KD // 2) as i:
            for u in range(2):
                self.w.landed(pe, i, u)
                pe.wait_ge(self.merged, 2 * i + u + 1)
                w = self.w.view(u, 40, P)
                bank = [self.chip.bank(4 * u + n) for n in range(4)]
                products(self.nc, bank[0], [(w[:, k], self.h[:, k]) for k in range(KD)])
                products(self.nc, bank[1], [(w[:, 24 + k], self.h[:, k]) for k in range(KD)]).then_inc(self.gate_sums, 1)
                products(self.nc, bank[2], [(w[:, 8 + k], self.y_ssd[:, k, TC:T]) for k in range(KS)])
                products(self.nc, bank[3], [(w[:, 32 + k], self.y_att[:, k]) for k in range(KD)]).then_inc(self.w.used(u), 1)

    def scalar(self, act):
        with act.Fori(0, KD // 2) as i:
            for u in range(2):
                act.wait_ge(self.gate_sums, 2 * i + u + 1)
                act.wait_ge(self.merged, 2 * i + u + 1)
                for n in range(2):
                    last = self.nc.scalar.activation(self.gates[u][n], self.chip.bank(4 * u + n), ACT.Sigmoid)
                last.then_inc(self.gated, 1)

    def vector(self, dve):
        v = self.nc.vector
        dve.sem_inc(self.merged, 2)
        with dve.Fori(0, KD // 2) as i:
            for u in range(2):
                dve.wait_ge(self.gated, 2 * i + u + 1)
                self.w.summed(dve, i, u)
                for n in range(2):
                    v.tensor_tensor(self.gates[u][n], self.gates[u][n], self.chip.bank(4 * u + 2 + n), ALU.mult)
                dve.drain()
                v.tensor_tensor(one(self.out, 2 * i + u), self.gates[u][0], self.gates[u][1], ALU.add).then_inc(self.merged, 1)


class Residual(Stage):

    def __init__(self, chip, name, kt, y, gate, y_ctx=None, gate_ctx=None, side=None):
        super().__init__(chip)
        self.w = Weights(chip, name, KD, kt * P)
        self.kt, self.side = kt, side
        self.parts = [(chip.view(A_XL, KD, TL), y, gate, TL)]
        if y_ctx is not None:
            self.parts.append((chip.view(A_XC, KD, TC), y_ctx, gate_ctx, TC))
        self.added = chip.sem(name + "_added")

    def sync(self, sp):
        self.w.load(sp)

    def gpsimd(self, pool):
        if self.side:
            self.side.rows_of(pool)
            pairs(pool, KD, lambda i, u: self.side.load(pool, 2, i, u))

    def scalar(self, act):
        if self.side:
            self.side.silu(act, 2)

    def tensor(self, pe):
        with pe.Fori(0, KD // 2) as i:
            for u in range(2):
                self.w.landed(pe, i, u)
                pe.wait_ge(self.added, 2 * i + u + 1)
                w = self.w.view(u, self.kt, P)
                for n, (x, y, gate, t) in enumerate(self.parts):
                    last = products(self.nc, self.chip.bank(2 * u + n, t), [(w[:, k], y(k)) for k in range(self.kt)])
                last.then_inc(self.w.used(u), 1)

    def vector(self, dve):
        dve.sem_inc(self.added, 2)
        if self.side:
            self.side.start(dve, 2)
        with dve.Fori(0, KD // 2) as i:
            for u in range(2):
                self.w.summed(dve, i, u)
                j = 2 * i + u
                for n, (x, y, gate, t) in enumerate(self.parts):
                    last = self.nc.vector.scalar_tensor_tensor(one(x, j), self.chip.bank(2 * u + n, t), gate[:, bass.ds(j, 1)],
                                                               one(x, j), ALU.mult, ALU.add)
                last.then_inc(self.added, 1)
                if self.side:
                    self.side.reduce(dve, 2, i, u)


FFN_G = A_WORK
FPAD = TL + 2


class FfnUp(Stage):

    def __init__(self, chip):
        super().__init__(chip)
        self.w = Weights(chip, "w_up", KF, 2 * D)
        self.h = chip.view(A_HL, KD, TL)
        self.g = chip.view(FFN_G, KF, TL)
        at = FFN_G + KF * TL
        self.raw = [[chip.view(at + (2 * u + n) * FPAD, FPAD) for n in range(2)] for u in range(2)]
        at += 4 * FPAD
        self.acc = [[chip.view(at + (2 * u + n) * TL, TL) for n in range(2)] for u in range(2)]
        self.padded, self.copied, self.convolved, self.activated, self.gated = (
            chip.sem("ffn_" + s) for s in ("padded", "copied", "convolved", "activated", "gated"))

    def sync(self, sp):
        self.w.load(sp)

    def tensor(self, pe):
        with pe.Fori(0, KF // 2) as i:
            for u in range(2):
                self.w.landed(pe, i, u)
                pe.wait_ge(self.copied, 2 * i + u + 1)
                w = self.w.view(u, 2, KD, P)
                for n in range(2):
                    last = products(self.nc, self.chip.bank(2 * u + n), [(w[:, n, k], self.h[:, k]) for k in range(KD)])
                last.then_inc(self.w.used(u), 1)

    def scalar(self, act):
        a = self.nc.scalar
        act.sem_inc(self.copied, 2)
        act.wait_ge(self.padded, 1)
        with act.Fori(0, KF // 2) as i:
            for u in range(2):
                self.w.summed(act, i, u)
                act.wait_ge(self.convolved, 2 * i + u + 1)
                for n in range(2):
                    last = a.activation(self.raw[u][n][:, 1:1 + TL], self.chip.bank(2 * u + n), ACT.Copy)
                last.then_inc(self.copied, 1)
            for u in range(2):
                act.wait_ge(self.convolved, 2 * i + u + 3)
                a.activation(self.acc[u][0], self.acc[u][0], ACT.Silu, bias=self.chip.vec_at("ffn_b", 2 * i + u)
                             ).then_inc(self.activated, 1)

    def vector(self, dve):
        v = self.nc.vector
        dve.sem_inc(self.convolved, 2)
        dve.sem_inc(self.gated, 2)
        for u in range(2):
            for n in range(2):
                v.memset(self.raw[u][n], 0.0)
        dve.drain().then_inc(self.padded, 1)
        with dve.Fori(0, KF // 2) as i:
            for u in range(2):
                j = 2 * i + u
                dve.wait_ge(self.copied, j + 3)
                dve.wait_ge(self.gated, j + 1)
                for n in range(2):
                    last = conv3(self.nc, dve, self.acc[u][n], self.raw[u][n],
                                 [self.chip.vec_at("ffn_w", 2 * KF * k + KF * n + j) for k in range(3)], TL)
                last.then_inc(self.convolved, 1)
            for u in range(2):
                j = 2 * i + u
                dve.wait_ge(self.activated, j + 1)
                dve.wait_ge(self.convolved, j + 3)
                v.scalar_tensor_tensor(one(self.g, j), self.acc[u][1], self.chip.vec_at("ffn_b", j + KF), self.acc[u][0],
                                       ALU.add, ALU.mult).then_inc(self.gated, 1)


class Store(Stage):

    def __init__(self, chip):
        super().__init__(chip)
        self.stored = chip.sem("stored")

    def sync(self, sp):
        sp.wait_ge(self.chip.stage_done, 4 * self.index)
        sp.dma_start(self.chip.dram["out"], self.chip.view(A_XL, KD * TL)).then_inc(self.stored, 16)
        sp.wait_ge(self.stored, 16)


def block1(chip):
    mod = chip.view(A_MOD1, 48, 2)
    x_lat, x_ctx = chip.view(A_XL, KD, TL), chip.view(A_XC, KD, TC)
    h_lat, h_ctx = chip.view(A_HL, KD, TL), chip.view(A_HC, KD, TC)
    part = lambda n, who: mod[:, 8 * n:8 * n + 8, who]
    g1, g2 = chip.vec("norm1_g"), chip.vec("norm2_g")
    job_lat = dict(x=x_lat, out=h_lat, gain=g1, scale=part(1, 0), shift=part(0, 0))
    job_ctx = dict(x=x_ctx, out=h_ctx, gain=g1, scale=part(1, 1), shift=part(0, 1))
    y = chip.view(XBC, KX, T)[:, 0:KS, TC:T]
    merged = chip.view(ATT + KD * TL, KD, TL)
    g = chip.view(FFN_G, KF, TL)
    side = SideModulation(chip)
    return [
        Inputs(chip),
        Modulation(chip, "w_mod1", 12, ("c", "c_ctx"), "b_mod", A_MOD1),
        Norm(chip, "norm_in", [job_lat, job_ctx], A_WORK),
        Xbc(chip, side), Dt(chip), SsdStates(chip), SsdOutput(chip),
        Norm(chip, "norm_again", [job_lat, job_ctx], SSDW),
        GateZ(chip, side),
        (load := LoadContext(chip)),
        Norm(chip, "norm_ssd", [dict(x=y, out=y, gain=chip.vec("ssd_g"))], SSDW),
        Attention(chip), Merge(chip),
        Residual(chip, "w_out1", KD, lambda k: merged[:, k], part(2, 0)),
        Norm(chip, "norm_ffn", [dict(x=x_lat, out=h_lat, gain=g2, scale=part(4, 0), shift=part(3, 0))], A_WORK),
        FfnUp(chip),
        Residual(chip, "w_down", KF, lambda k: g[:, k], part(5, 0), side=side),
        Norm(chip, "norm_out", [dict(x=x_lat, out=x_lat, gain=chip.vec("final_g"))], A_WORK),
        NewContext(chip, load),
    ]


SGU_V = A_WORK


class SguValues(Stage):

    def __init__(self, chip, layer, nt):
        super().__init__(chip)
        self.nt = nt
        self.w = Weights(chip, f"w_sgu_v{layer}", 4, 4 * D)
        self.h_lat, self.h_ctx = chip.view(A_HL, KD, TL), chip.view(A_HC, KD, TC)
        self.v = chip.view(SGU_V, KG, nt, P)
        self.junk = chip.view(SGU_V + KG * T, 4, P)
        self.sums = chip.view(A_SMALL, 4, nt)
        self.activated, self.summed = chip.sem(f"sgu{layer}_v"), chip.sem(f"sgu{layer}_v_summed")

    def sync(self, sp):
        self.w.load(sp)

    def tensor(self, pe):
        def body(i, u):
            self.w.landed(pe, i, u)
            w = self.w.view(u, KD, 512)
            for t in range(self.nt):
                h, at = (self.h_lat, t * P) if t < 4 else (self.h_ctx, (t - 4) * P)
                x = u * self.nt + t
                pe.wait_ge(self.activated, 2 * self.nt * i + x + 1)
                last = products(self.nc, self.chip.bank(x % 4), [(h[:, k, at:at + P], w[:, k]) for k in range(KD)])
                if t < self.nt - 1:
                    last.then_inc(self.summed, 1)
            last.then_inc(self.w.used(u), 1)
        pairs(pe, 4, body)

    def scalar(self, act):
        act.sem_inc(self.activated, 4)

        def body(i, u):
            for t in range(self.nt):
                x = u * self.nt + t
                if t < self.nt - 1:
                    act.wait_ge(self.summed, (self.nt - 1) * (2 * i + u) + t + 1)
                else:
                    self.w.summed(act, i, u)
                self.nc.scalar.activation(self.v[:, bass.ds(8 * i + 4 * u, 4), t], self.chip.bank(x % 4).rearrange("p (m f) -> p m f", f=P),
                                          ACT.Gelu_apprx_tanh).then_inc(self.activated, 1)
        pairs(act, 4, body)

    def vector(self, dve):
        def body(i, u):
            for t in range(self.nt):
                v = self.v[:, bass.ds(8 * i + 4 * u, 4), t]
                dve.drain()
                dve.wait_ge(self.activated, 2 * self.nt * i + u * self.nt + t + 5)
                self.nc.vector.tensor_tensor(self.junk, v, v, ALU.mult)
                dve.drain()
                self.nc.vector.tensor_reduce(one(self.sums, 2 * i + u)[:, t:t + 1], self.junk.rearrange("p m f -> p (m f)"), AX.X, ALU.add)
        pairs(dve, 4, body)


class SguMix(Stage):

    def __init__(self, chip, layer, j, nt):
        super().__init__(chip)
        self.nt, self.j, self.layer = nt, j, layer
        t = nt * P
        self.w = Weights(chip, f"w_sgu_uz{layer}", KG, 17 * P)
        self.h = [(chip.view(A_HL, KD, TL), TL, 0), (chip.view(A_HC, KD, TC), TC, TL)][:2 if nt == 6 else 1]
        self.v = chip.view(SGU_V, KG, nt, P)
        self.s = chip.view(SGU_V, KG, t)
        at = SGU_V + KG * T
        self.staged_v = [chip.view(at + u * T, nt, P) for u in range(2)]
        self.u = [chip.view(at + (2 + u) * T, t) for u in range(2)]
        self.z = [chip.view(at + (4 + u) * T, t) for u in range(2)]
        self.tmp = [chip.view(at + (6 + u) * T, t) for u in range(2)]
        self.bs = chip.view(at + 8 * T, SGU_G, P)
        self.sums = chip.view(A_SMALL, 4, nt)
        self.total, self.inv = chip.view(A_SMALL + 32, nt), chip.view(A_SMALL + 40, nt)
        (self.bs_in, self.totalled, self.rooted, self.inverted, self.staged, self.mixed, self.u_done,
         self.activated, self.gated) = (
            chip.sem(f"sgu{layer}_{n}") for n in "bs_in totalled rooted inverted staged mixed u_done activated gated".split())

    def banks(self, u):
        return [(self.chip.bank(n + 3 * u), self.chip.bank(*c)) for n, c in enumerate(((7, TC), (6, TC), (6, TC, TC)))]

    def sync(self, sp):
        sp.wait_ge(self.chip.stage_done, 4 * self.index)
        sp.dma_start(self.bs.rearrange("p g q -> p (g q)"), self.chip.dram[f"sgu_bs{self.layer}"]).then_inc(self.bs_in, 16)
        self.w.load(sp)

    def gpsimd(self, pool):
        pool.wait_ge(self.inverted, 1)

        def body(i, u):
            pool.wait_ge(self.gated, 2 * i + u + 1)
            self.nc.gpsimd.tensor_tensor(self.staged_v[u], one(self.v, 2 * i + u), over(self.inv, P), ALU.mult
                                         ).then_inc(self.staged, 1)
        pairs(pool, KG, body)

    def tensor(self, pe):
        def body(i, u):
            j = 2 * i + u
            self.w.landed(pe, i, u)
            w = self.w.view(u, 17, P)
            mix, ub, zb = self.banks(u)
            pe.wait_ge(self.gated, j + 1)
            pe.wait_ge(self.staged, j + 1)
            for t in range(4):
                self.nc.tensor.matmul(mix[0][:, t * P:t * P + P], self.staged_v[u][:, t], w[:, 16], start=True, stop=True)
            for n, b in ((0, ub), (8, zb)):
                products(self.nc, b[0], [(w[:, n + k], self.h[0][0][:, k]) for k in range(KD)]).then_inc(self.u_done, 1)
            if self.nt > 4:
                pe.wait_ge(self.gated, j + 2)
                for t in range(4, self.nt):
                    self.nc.tensor.matmul(mix[1][:, (t - 4) * P:(t - 3) * P], self.staged_v[u][:, t], w[:, 16], start=True, stop=True)
                for n, b in ((0, ub), (8, zb)):
                    products(self.nc, b[1], [(w[:, n + k], self.h[1][0][:, k]) for k in range(KD)])
            pe.drain().then_inc(self.w.used(u), 1)
        pairs(pe, KG, body)

    def scalar(self, act):
        a = self.nc.scalar
        act.wait_ge(self.totalled, 1)
        a.activation(self.total, self.total, ACT.Sqrt, scale=1.0 / SGU_W, bias=EPS).then_inc(self.rooted, 1)

        def body(i, u):
            mix, ub, zb = self.banks(u)
            self.w.summed(act, i, u)
            act.wait_ge(self.gated, 2 * i + u + 1)
            for n, (_, t, at) in enumerate(self.h):
                a.activation(self.u[u][:, at:at + t], ub[n], ACT.Gelu_apprx_tanh)
            for n, (_, t, at) in enumerate(self.h):
                last = a.activation(self.z[u][:, at:at + t], zb[n], ACT.Silu)
            last.then_inc(self.activated, 1)
        pairs(act, KG, body)

    def vector(self, dve):
        v = self.nc.vector
        v.tensor_reduce(self.total, self.sums.rearrange("p c t -> p t c"), AX.X, ALU.add).then_inc(self.totalled, 1)
        dve.wait_ge(self.rooted, 1)
        v.reciprocal(self.inv, self.total).then_inc(self.inverted, 1)
        dve.wait_ge(self.bs_in, 16)
        dve.sem_inc(self.gated, 2)

        def body(i, u):
            mix, ub, zb = self.banks(u)
            self.w.summed(dve, i, u)
            dve.wait_ge(self.gated, 2 * i + u + 1)
            for n, (_, t, at) in enumerate(self.h):
                c = t // P
                v.scalar_tensor_tensor(self.tmp[u][:, at:at + t].rearrange("p (c q) -> p c q", q=P), mix[n].rearrange("p (c q) -> p c q", q=P),
                                       self.chip.vec_at("sgu_gain", KG * self.j + 2 * i + u),
                                       across(one(self.bs, i), c), ALU.mult, ALU.add)
            dve.drain()
            dve.wait_ge(self.activated, 2 * i + u + 1)
            v.tensor_tensor(self.tmp[u], self.tmp[u], self.u[u], ALU.mult)
            dve.drain()
            v.tensor_tensor(one(self.s, 2 * i + u), self.tmp[u], self.z[u], ALU.mult).then_inc(self.gated, 1)
        pairs(dve, KG, body)


def modulated(chip, layer, n):
    m = chip.view(A_MOD2, 96, 2)
    return [m[:, 24 * layer + 8 * n:24 * layer + 8 * n + 8, who] for who in range(2)]


def norm2(chip, layer, ctx):
    lat = dict(x=chip.view(A_XL, KD, TL), out=chip.view(A_HL, KD, TL), shift=modulated(chip, layer, 0)[0], scale=modulated(chip, layer, 1)[0])
    con = dict(x=chip.view(A_XC, KD, TC), out=chip.view(A_HC, KD, TC), shift=modulated(chip, layer, 0)[1], scale=modulated(chip, layer, 1)[1])
    return Norm(chip, f"norm_layer{layer}", [lat, con] if ctx else [lat], A_WORK)


def sgu_layer(chip, layer, j, nt):
    s = chip.view(SGU_V, KG, nt * P)
    gate = modulated(chip, layer, 2)
    ctx = (lambda k: s[:, k, TL:T], gate[1]) if nt == 6 else (None, None)
    return [norm2(chip, layer, nt == 6), SguValues(chip, layer, nt), SguMix(chip, layer, j, nt),
            Residual(chip, f"w_sgu_out{layer}", KG, lambda k: s[:, k, 0:TL], gate[0], *ctx)]


class Project(Stage):

    def __init__(self, chip, name, n, parts, out):
        super().__init__(chip)
        self.w = Weights(chip, name, n, D)
        self.n, self.parts, self.out = n, parts, out
        self.copied = chip.sem(name + "_copied")

    def sync(self, sp):
        self.w.load(sp)

    def tensor(self, pe):
        def body(i, u):
            self.w.landed(pe, i, u)
            pe.wait_ge(self.copied, 2 * i + u + 1)
            w = self.w.view(u, KD, P)
            for n, (x, t, at) in enumerate(self.parts):
                last = products(self.nc, self.chip.bank(2 * u + n, t), [(w[:, k], x[:, k]) for k in range(KD)])
            last.then_inc(self.w.used(u), 1)
        pairs(pe, self.n, body)

    def scalar(self, act):
        act.sem_inc(self.copied, 2)

        def body(i, u):
            self.w.summed(act, i, u)
            out = one(self.out, 2 * i + u) if self.n > 1 else self.out[:, 0]
            for n, (x, t, at) in enumerate(self.parts):
                last = self.nc.scalar.activation(out[:, at:at + t], self.chip.bank(2 * u + n, t), ACT.Copy)
            last.then_inc(self.copied, 1)
        pairs(act, self.n, body)


CQ = A_WORK
CKV = CQ + 6 * TL
KROPE = CKV + 2 * T
O_MLA = KROPE + T
MLAW = O_MLA + MH * TL


def nothing(*_):
    pass


class Mla(Stage):
    WORDS = 6 * QK + 2 * (NOPE + VD)

    def __init__(self, chip):
        super().__init__(chip)
        self.w = Weights(chip, "w_mla_head", MH, self.WORDS)
        self.cq, self.ckv = chip.view(CQ, 6, TL), chip.view(CKV, 2, T)
        self.k_rope = chip.view(KROPE, T)
        self.o = chip.view(O_MLA, MH, TL)
        at = MLAW
        self.tables = chip.view(at, 2 * TL + P)
        self.cos, self.sin, self.swap = chip.view(at, TL)[0:64], chip.view(at + TL, TL)[0:64], chip.view(at + 2 * TL, P)[0:64]
        at += 2 * TL + P
        self.sq_rope = chip.view(at, T)[0:64]
        at += T
        spare = [A_W + u * WSLOT + self.WORDS for u in range(2)]
        assert max(4 * T, 4 * TL) <= WSLOT - self.WORDS
        q_at, k_at = (at, spare[1]), (at + 3 * TL, spare[0])
        self.qn = [chip.view(x, TL) for x in q_at]
        self.qr = [chip.view(x + TL, TL)[0:64] for x in q_at]
        self.q_rot = [chip.view(x + 2 * TL, TL)[0:64] for x in q_at]
        self.kn = [chip.view(x, T) for x in k_at]
        self.kr = [chip.view(x + T, T)[0:64] for x in k_at]
        self.v = [chip.view(x + 2 * T, NT, VD) for x in k_at]
        self.iq, self.ik = chip.view(spare[1] + 3 * TL, TL), chip.view(spare[0] + 3 * T, T)
        at += 3 * TL + 3 * T
        self.sq_qn, self.sq_qr, self.sq_kn = chip.view(at, TL), chip.view(at + TL, TL)[0:64], chip.view(at + 2 * TL, T)
        at += 2 * TL + T
        self.p = [chip.view(at, T), chip.view(at + T, T)]
        at += 2 * T
        self.pt = chip.view(at, NT, TL)
        at += NT * TL
        assert at <= A_END, at
        self.mx, self.neg, self.den, self.inv = (chip.view(A_SMALL + 4 * n, 4) for n in range(4))
        (self.tables_in, self.shared, self.raw, self.squared, self.ssq, self.rooted, self.q_ready, self.turned,
         self.values_out, self.scored, self.peaked, self.exped, self.normed, self.p_turned, self.pt_out, self.summed,
         self.out, self.shared_turned) = (
            chip.sem("mla_" + n) for n in (
                "tables_in shared raw squared ssq rooted q_ready turned values_out scored peaked exped normed "
                "p_turned pt_out summed out shared_turned").split())

    def s_bank(self, n):
        return self.wide(2 * (n % 2))

    def wide(self, b):
        return self.chip.psum[:, b:b + 2].rearrange("p b w -> p (b w)")[:, 0:T]

    def sync(self, sp):
        sp.wait_ge(self.chip.stage_done, 4 * self.index)
        sp.dma_start(self.tables, self.chip.dram["rope_mla"]).then_inc(self.tables_in, 16)
        self.w.load(sp)

    def heads(self, eng, queries, begin, rest, attend):
        queries(0, 0, 0)
        rest(0, 0, 0)
        begin()
        queries(0, 1, 1)
        with eng.Fori(0, MH // 2 - 1) as i:
            for u in range(2):
                h = 2 * i + u
                rest(i + u, 1 - u, h + 1)
                attend(h, u, True, lambda: queries(i + 1, u, h + 2))
        rest(MH // 2 - 1, 1, MH - 1)
        attend(MH - 2, 0, True, nothing)
        attend(MH - 1, 1, False, nothing)

    def tensor(self, pe):
        t, c = self.nc.tensor, self.chip
        pe.wait_ge(self.tables_in, 16)
        pe.wait_ge(self.shared, 1)
        t.matmul(c.bank(7), self.swap, self.k_rope[0:64, 0:TL], start=True, stop=True).then_inc(self.shared_turned, 1)
        ones = c.const("ones")

        def words(u):
            both = self.w.view(u, self.WORDS)
            return (both[:, 0:6 * QK].rearrange("p (k m) -> p k m", m=QK),
                    both[:, 6 * QK:].rearrange("p (k m) -> p k m", m=NOPE + VD))

        def queries(i, u, h):
            self.w.landed(pe, i, u)
            wq, _ = words(u)
            products(self.nc, c.bank(0), [(wq[:, k, 0:NOPE], self.cq[:, k]) for k in range(6)])
            products(self.nc, c.bank(1)[0:64], [(wq[:, k, NOPE:QK], self.cq[:, k]) for k in range(6)]).then_inc(self.raw, 1)

        def begin():
            pe.wait_ge(self.rooted, 2)
            swap(0, 0)

        def rest(i, u, h):
            _, wkv = words(u)
            for b, a, n in ((2, 0, TL), (3, TL, TC)):
                last = products(self.nc, c.bank(b, n), [(wkv[:, k, 0:NOPE], self.ckv[:, k, a:a + n]) for k in range(2)])
            last.then_inc(self.raw, 1)
            for m in range(NT):
                last = products(self.nc, c.bank(4 + m // 4, VD, VD * (m % 4)),
                                [(self.ckv[:, k, P * m:P * m + P], wkv[:, k, NOPE:]) for k in range(2)])
            last.then_inc(self.w.used(u), 1)
            pe.wait_ge(self.squared, 2 * h + 1)
            pe.wait_ge(self.out, h + 1)
            t.matmul(c.bank(6), ones, self.sq_qn, start=True, stop=False)
            t.matmul(c.bank(6), ones[0:64], self.sq_qr, start=False, stop=True).then_inc(self.ssq, 1)
            pe.wait_ge(self.squared, 2 * h + 2)
            pe.wait_ge(self.values_out, h + 1)
            for b, a, n in ((4, 0, TL), (5, TL, TC)):
                t.matmul(c.bank(b, n), ones, self.sq_kn[:, a:a + n], start=True, stop=False)
                last = t.matmul(c.bank(b, n), ones[0:64], self.sq_rope[:, a:a + n], start=False, stop=True)
            last.then_inc(self.ssq, 1)

        def swap(h, u):
            pe.wait_ge(self.q_ready, 3 * h + 4)
            t.matmul(c.bank(7), self.swap, self.qr[u], start=True, stop=True).then_inc(self.turned, 1)

        def attend(h, u, more, ahead):
            pe.wait_ge(self.q_ready, 3 * h + 6)
            for n in range(4):
                if n >= 2:
                    pe.wait_ge(self.exped, 4 * h + n - 1)
                q = slice(P * n, P * n + P)
                s = self.s_bank(n)
                for a, w, rot in ((0, TL, self.q_rot[u]), (TL, TC, self.qr[u])):
                    t.matmul(s[:, a:a + w], self.qn[u][:, q], self.kn[u][:, a:a + w], start=True, stop=False)
                    last = t.matmul(s[:, a:a + w], rot[:, q], self.kr[u][:, a:a + w], start=False, stop=True)
                last.then_inc(self.scored, 1)
                if n == 1:
                    pe.wait_ge(self.rooted, 2 * h + (4 if more else 2))
                if n >= 1:
                    self.turn(pe, h, n - 1)
            pe.wait_ge(self.exped, 4 * h + 3)
            ahead()
            self.turn(pe, h, 3)
            pe.wait_ge(self.pt_out, 4 * h + 4)
            products(self.nc, c.bank(6), [(self.v[u][:, m], self.pt[:, m]) for m in range(NT)]).then_inc(self.summed, 1)
            if more:
                swap(h + 1, 1 - u)

        self.heads(pe, queries, begin, rest, attend)

    def turn(self, pe, h, n):
        pe.wait_ge(self.normed, 4 * h + n + 1)
        if n >= 1:
            pe.wait_ge(self.pt_out, 4 * h + n)
        for m in range(NT):
            last = self.nc.tensor.transpose(self.chip.bank(4 + m // 4, P, P * (m % 4)), self.p[n % 2][:, P * m:P * m + P], self.chip.const("ident"))
        last.then_inc(self.p_turned, 1)

    def scalar(self, act):
        a, c = self.nc.scalar, self.chip

        def queries(i, u, h):
            act.wait_ge(self.raw, 2 * h + 1)
            act.wait_ge(self.q_ready, 3 * h + 1)
            a.activation(self.sq_qn, c.bank(0), ACT.Square)
            a.activation(self.sq_qr, c.bank(1)[0:64], ACT.Square).then_inc(self.squared, 1)
            a.activation(self.qn[u], c.bank(0), ACT.Copy)
            a.activation(self.qr[u], c.bank(1)[0:64], ACT.Copy)

        def rest(i, u, h):
            act.wait_ge(self.raw, 2 * h + 2)
            act.wait_ge(self.q_ready, 3 * h + 2)
            a.activation(self.sq_kn, self.wide(2), ACT.Square).then_inc(self.squared, 1)
            a.activation(self.kn[u], self.wide(2), ACT.Copy)
            self.w.summed(act, i, u)
            a.activation(self.v[u].rearrange("p t e -> p (t e)"), self.wide(4), ACT.Copy).then_inc(self.values_out, 1)
            act.wait_ge(self.ssq, 2 * h + 1)
            a.activation(self.sq_qn, c.bank(6), ACT.Sqrt, scale=1.0 / QK, bias=EPS).then_inc(self.rooted, 1)
            act.wait_ge(self.ssq, 2 * h + 2)
            a.activation(self.sq_kn, self.wide(4), ACT.Sqrt, scale=1.0 / QK, bias=EPS).then_inc(self.rooted, 1)

        def attend(h, u, more, ahead):
            for n in range(4):
                act.wait_ge(self.peaked, 4 * h + n + 1)
                if n >= 2:
                    act.wait_ge(self.p_turned, 4 * h + n - 1)
                a.activation(self.p[n % 2], self.s_bank(n), ACT.Exp, bias=self.neg[:, n:n + 1], scale=QK ** -0.5,
                             accum_out=self.den[:, n:n + 1]).then_inc(self.exped, 1)
                if n >= 1:
                    self.out_turned(act, h, n - 1)
            self.out_turned(act, h, 3)
            ahead()

        self.heads(act, queries, nothing, rest, attend)

    def out_turned(self, act, h, n):
        act.wait_ge(self.p_turned, 4 * h + n + 1)
        self.nc.scalar.activation(self.pt[:, :, P * n:P * n + P], self.wide(4).rearrange("p (m q) -> p m q", q=P), ACT.Copy
                                  ).then_inc(self.pt_out, 1)

    def vector(self, dve):
        v, c = self.nc.vector, self.chip
        dve.wait_ge(self.tables_in, 16)
        dve.sem_inc(self.out, 2)
        dve.sem_inc(self.q_ready, 3)
        kr = self.k_rope[0:64]
        v.tensor_tensor(self.sq_rope, kr, kr, ALU.mult)
        dve.drain()
        v.tensor_scalar(kr, kr, c.vec("gk_rope")[0:64], None, ALU.mult).then_inc(self.shared, 1)
        dve.wait_ge(self.shared_turned, 1)
        v.tensor_tensor(self.q_rot[0], c.bank(7)[0:64], self.sin, ALU.mult)
        v.tensor_tensor(kr[:, 0:TL], kr[:, 0:TL], self.cos, ALU.mult)
        dve.drain()
        v.tensor_tensor(kr[:, 0:TL], kr[:, 0:TL], self.q_rot[0], ALU.add)
        dve.drain()

        def queries(h, u):
            dve.drain()
            dve.wait_ge(self.rooted, 2 * h + 1)
            v.reciprocal(self.iq, self.sq_qn)
            dve.drain()
            v.scalar_tensor_tensor(self.qr[u], self.qr[u], c.vec("gq_rope")[0:64], self.iq[0:64], ALU.mult, ALU.mult
                                   ).then_inc(self.q_ready, 1)
            v.scalar_tensor_tensor(self.qn[u], self.qn[u], c.vec("gq_nope"), self.iq, ALU.mult, ALU.mult)

        def key_norms(h, u):
            dve.wait_ge(self.rooted, 2 * h + 2)
            v.reciprocal(self.ik, self.sq_kn)
            dve.drain()

        def keys(h, u):
            v.scalar_tensor_tensor(self.kn[u], self.kn[u], c.vec("gk_nope"), self.ik, ALU.mult, ALU.mult)
            v.tensor_tensor(self.kr[u], kr, self.ik[0:64], ALU.mult).then_inc(self.q_ready, 1)

        def rotate(h, u):
            dve.wait_ge(self.turned, h + 1)
            v.tensor_tensor(self.q_rot[u], c.bank(7)[0:64], self.sin, ALU.mult)
            v.tensor_tensor(self.iq[0:64], self.qr[u], self.cos, ALU.mult)
            dve.drain()
            v.tensor_tensor(self.q_rot[u], self.q_rot[u], self.iq[0:64], ALU.add).then_inc(self.q_ready, 1)

        def begin():
            for part in (queries, key_norms, keys, rotate):
                part(0, 0)

        def attend(h, u, more, ahead):
            for n in range(4):
                dve.wait_ge(self.scored, 4 * h + n + 1)
                v.tensor_reduce(self.mx[:, n:n + 1], self.s_bank(n), AX.X, ALU.max)
                dve.drain()
                v.tensor_scalar(self.neg[:, n:n + 1], self.mx[:, n:n + 1], -QK ** -0.5, None, ALU.mult).then_inc(self.peaked, 1)
                self.normalise(dve, h, n)
            if more:
                queries(h + 1, 1 - u)
                key_norms(h + 1, 1 - u)
            dve.wait_ge(self.summed, h + 1)
            v.tensor_copy(one(self.o, h), c.bank(6)).then_inc(self.out, 1)
            if more:
                keys(h + 1, 1 - u)
                rotate(h + 1, 1 - u)

        self.heads(dve, nothing, begin, nothing, attend)

    def normalise(self, dve, h, n):
        v = self.nc.vector
        dve.wait_ge(self.exped, 4 * h + n + 1)
        v.reciprocal(self.inv[:, n:n + 1], self.den[:, n:n + 1])
        dve.drain()
        v.tensor_scalar(self.p[n % 2], self.p[n % 2], self.inv[:, n:n + 1], None, ALU.mult).then_inc(self.normed, 1)


class GateO(Stage):

    def __init__(self, chip):
        super().__init__(chip)
        self.w = Weights(chip, "w_mla_z", MH, D)
        self.h = chip.view(A_HL, KD, TL)
        self.y = chip.view(O_MLA, MH, TL)
        self.z = [chip.view(MLAW + u * TL, TL) for u in range(2)]
        self.activated, self.used = chip.sem("mla_z_activated"), chip.sem("mla_z_used")

    def sync(self, sp):
        self.w.load(sp)

    def tensor(self, pe):
        def body(i, u):
            self.w.landed(pe, i, u)
            pe.wait_ge(self.activated, 2 * i + u + 1)
            w = self.w.view(u, KD, P)
            products(self.nc, self.chip.bank(u), [(w[:, k], self.h[:, k]) for k in range(KD)]).then_inc(self.w.used(u), 1)
        pairs(pe, MH, body)

    def scalar(self, act):
        act.sem_inc(self.activated, 2)

        def body(i, u):
            self.w.summed(act, i, u)
            act.wait_ge(self.used, 2 * i + u + 1)
            self.nc.scalar.activation(self.z[u], self.chip.bank(u), ACT.Silu).then_inc(self.activated, 1)
        pairs(act, MH, body)

    def vector(self, dve):
        dve.sem_inc(self.used, 2)

        def body(i, u):
            dve.wait_ge(self.activated, 2 * i + u + 3)
            y = one(self.y, 2 * i + u)
            self.nc.vector.tensor_tensor(y, y, self.z[u], ALU.mult).then_inc(self.used, 1)
        pairs(dve, MH, body)


def mla_layer(chip, layer):
    h_lat, h_ctx = chip.view(A_HL, KD, TL), chip.view(A_HC, KD, TC)
    both = [(h_lat, TL, 0), (h_ctx, TC, TL)]
    cq, ckv = chip.view(CQ, 6, TL), chip.view(CKV, 2, T)
    o = chip.view(O_MLA, MH, TL)
    kvn = chip.vec("kv_norm")
    return [norm2(chip, layer, True),
            Project(chip, "w_mla_q", 6, both[:1], cq), Project(chip, "w_mla_kv", 2, both, ckv),
            Project(chip, "w_mla_rope", 1, both, chip.view(KROPE, 1, T)),
            Norm(chip, "norm_rank", [dict(x=cq, out=cq, gain=chip.vec("q_norm")), dict(x=ckv[:, :, 0:TL], out=ckv[:, :, 0:TL], gain=kvn),
                                     dict(x=ckv[:, :, TL:T], out=ckv[:, :, TL:T], gain=kvn)], MLAW),
            Mla(chip), GateO(chip),
            Residual(chip, "w_mla_out", MH, lambda k: o[:, k], modulated(chip, layer, 2)[0])]


MIDS = A_WORK
RWKV = MIDS + 2 * T
TERMS = 5
BATCH = 4
BATCHES = NC // BATCH
DECAYS = A_SMALL
LOG_DECAY = float(np.exp(-0.5))


class RwkvFeatures(Stage):
    ORDER = (4, 5, 0, 1, 2, 3)

    def __init__(self, chip):
        super().__init__(chip)
        names = {4: "w_rwkv_lw", 5: "w_rwkv_la", 0: "w_rwkv_r", 1: "w_rwkv_k", 2: "w_rwkv_v", 3: "w_rwkv_z"}
        self.w = {c: Weights(chip, names[c], 1 if c > 3 else KD, D) for c in self.ORDER}
        self.parts = [(chip.view(A_HC, KD, TC), 0, TC), (chip.view(A_HL, KD, TL), TC, TL)]
        at = RWKV
        self.xx = chip.view(at, KD, T)
        self.xs = [chip.view(at + (1 + u) * KD * T, KD, T) for u in range(2)]
        at += 3 * KD * T
        self.out = [chip.view(at + u * T, T) for u in range(2)]
        self.mids = chip.view(MIDS, 2, T)
        self.mixed, self.multiplied, self.copied, self.out_free = (
            chip.sem("rwkv_" + s) for s in ("mixed", "multiplied", "copied", "out_free"))
        self.stored = chip.lasting("rwkv_stored")

    def wide(self, u):
        return self.chip.psum[:, 2 * u:2 * u + 2].rearrange("p b w -> p (b w)")[:, 0:T]

    def sync(self, sp):
        for c in self.ORDER:
            self.w[c].load(sp)

    def before(self, n):
        return sum(self.w[c].n for c in self.ORDER[:n])

    def vector(self, dve):
        v = self.nc.vector
        for h, at, n in self.parts:
            xx = self.xx[:, :, at:at + n]
            v.tensor_tensor(xx[:, :, 1:n - 1], h[:, :, 0:n - 2], h[:, :, 2:n], ALU.add)
            v.tensor_copy(xx[:, :, 0:1], h[:, :, 1:2])
            v.tensor_copy(xx[:, :, n - 1:n], h[:, :, n - 2:n - 1])
        dve.drain()
        for h, at, n in self.parts:
            xx = self.xx[:, :, at:at + n]
            v.scalar_tensor_tensor(xx, xx, 0.5, h, ALU.mult, ALU.subtract)
        dve.drain()
        for n, c in enumerate(self.ORDER):
            if n >= 2:
                dve.wait_ge(self.multiplied, n - 1)
            for k in range(KD):
                for h, at, w in self.parts:
                    last = v.scalar_tensor_tensor(self.xs[n % 2][:, k, at:at + w], self.xx[:, k, at:at + w],
                                                  self.chip.vec("mu", 8 * c + k, 1), h[:, k], ALU.mult, ALU.add)
                if n == 0 or k == KD - 1:
                    last.then_inc(self.mixed, 1)

    def tensor(self, pe):
        for n, c in enumerate(self.ORDER):
            if n > 0:
                pe.wait_ge(self.mixed, KD + n)
            xs, weights = self.xs[n % 2], self.w[c]

            def body(i, u):
                weights.landed(pe, i, u)
                pe.wait_ge(self.copied, self.before(n) + 2 * i + u + 1)
                w = weights.view(u, KD, P)
                b = (self.before(n) + u) % 2
                for k in range(KD):
                    if n == 0:
                        pe.wait_ge(self.mixed, k + 1)
                    for at, width in ((0, TL), (TL, TC)):
                        last = self.nc.tensor.matmul(self.wide(b)[:, at:at + width], w[:, k], xs[:, k, at:at + width],
                                                     start=(k == 0), stop=(k == KD - 1))
                last.then_inc(weights.used(u), 1)
            pairs(pe, weights.n, body)
            pe.drain().then_inc(self.multiplied, 1)

    def scalar(self, act):
        a = self.nc.scalar
        act.sem_inc(self.copied, 2)
        act.sem_inc(self.out_free, 2)
        for n, c in enumerate(self.ORDER):
            func = {3: ACT.Silu, 4: ACT.Tanh}.get(c, ACT.Copy)

            def body(i, u):
                self.w[c].summed(act, i, u)
                b = (self.before(n) + u) % 2
                if c > 3:
                    out = self.mids[:, c - 4]
                else:
                    act.wait_ge(self.out_free, self.before(n) - 2 + 2 * i + u + 1)
                    out = self.out[b]
                a.activation(out, self.wide(b), func).then_inc(self.copied, 1)
            pairs(act, self.w[c].n, body)

    def gpsimd(self, pool):
        for n, c in enumerate(self.ORDER):
            if c > 3:
                continue

            def body(i, u):
                pool.wait_ge(self.copied, self.before(n) + 2 * i + u + 3)
                self.nc.gpsimd.dma_start(self.chip.dram["rkvz"][bass.ds(i * 8 + (4 * u + c), 1)].rearrange("o p w -> (o p) w"),
                                         self.out[(self.before(n) + u) % 2]).then_inc(self.stored, 16)
                pool.wait_ge(self.stored, 16 * (self.before(n) - 2) + 32 * i + 16 * u + 16)
                pool.sem_inc(self.out_free, 1)
            pairs(pool, KD, body)


class RwkvTerms(Stage):

    def __init__(self, chip):
        super().__init__(chip)
        self.w = Weights(chip, "w_lora2", 1, KD * 2 * P)
        self.mids = chip.view(MIDS, 2, T)
        at = RWKV
        self.starts, at = chip.view(at, T), at + T
        self.x = [chip.view(at + u * 4 * T, 4, T) for u in range(2)]
        at += 8 * T
        terms_at = ((at, at + TERMS * T), (A_HL, A_W + (1 - self.w.slot(0)) * WSLOT + D))
        self.out = [[chip.view(x, NC, TERMS, CH) for x in both] for both in terms_at]
        at += 2 * TERMS * T
        assert D + TERMS * T <= WSLOT
        row = lambda n: chip.view(at + n * T, T)
        self.sg, self.a = [row(0), row(1)], [row(2), row(3)]
        self.kk_raw, self.norm, self.kk = row(4), row(5), row(6)
        self.ci, self.ce = [row(7), row(8)], [row(9), row(10)]
        self.kka, self.kd = [row(11), row(12)], [row(13), row(14)]
        assert at + 15 * T <= A_END, at
        at = A_HL + TERMS * T
        self.rrk, self.products = row(0), row(1)
        at += 2 * T
        self.slice = [chip.view(at + u * 2 * P, 2, P) for u in range(2)]
        assert at + 4 * P <= A_W
        self.decays = chip.view(DECAYS, KD, 2, NC)
        self.one_minus_ka = chip.view(DECAYS + KD * 2 * NC, KD)
        self.loaded = [chip.sem(f"terms_loaded{u}") for u in range(2)]
        self.stored = [chip.sem(f"terms_stored{u}") for u in range(2)]
        self.bonus_stored = [chip.sem(f"terms_bonus_stored{u}") for u in range(2)]
        (self.starts_in, self.scaled, self.sliced, self.lora, self.activated, self.raw_done, self.squared,
         self.norm_sum, self.rooted, self.scanned, self.kk_done, self.kd_done, self.directed, self.exped, self.weighted,
         self.bonus_sum, self.done) = (
            chip.sem("terms_" + n) for n in (
                "starts_in scaled sliced lora activated raw_done squared norm_sum rooted scanned kk_done "
                "kd_done directed exped weighted bonus_sum done").split())

    STORED = 4 * 16

    def wide(self, q):
        return self.chip.psum[:, 2 * q:2 * q + 2].rearrange("p b w -> p (b w)")[:, 0:T]

    def lora_bank(self, q, d):
        return self.wide((1, 2, 3, 1)[2 * q + d])

    def each(self, eng, first, step, last):
        first(0, 0, 0)
        with eng.Fori(0, KD // 2 - 1) as i:
            for u in range(2):
                step(2 * i + u, u, i, True)
        step(KD - 2, 0, KD // 2 - 1, False)
        last(KD - 1, 1, KD // 2 - 1)

    def sync(self, sp):
        d = self.chip.dram
        sp.wait_ge(self.chip.stage_done, 4 * self.index)
        sp.dma_start(self.starts, d["scan_const"][:, 0:T]).then_inc(self.starts_in, 16)
        self.w.load(sp)

        def load(m, u):
            src = (d["rkvz"][bass.ds(4 * m, 4)] if not isinstance(m, int) else d["rkvz"][4 * m:4 * m + 4]).rearrange("c p w -> p c w")
            sp.dma_start(self.x[u], src).then_inc(self.loaded[u], 16)

        def store(m, u, i, more):
            to = d["terms"][bass.ds(3 * m, 3)] if not isinstance(m, int) else d["terms"][3 * m:3 * m + 3]
            bonus = d["bonus"][bass.ds(m, 1)].rearrange("o p w -> (o p) w") if not isinstance(m, int) else d["bonus"][m]
            width = BATCH * TERMS * CH
            flat = [o.rearrange("p c n e -> p (c n e)").rearrange("p (b w) -> p b w", w=width) for o in self.out[u]]
            sp.wait_ge(self.done, m + 2)
            sp.wait_ge(self.loaded[u], 16 * i + 16)
            sp.dma_start(bonus, self.x[u][:, 1]).then_inc(self.bonus_stored[u], 16)
            if more:
                sp.wait_ge(self.bonus_stored[u], 16 * i + 16)
                load(m + 2, u)
            sp.dma_start(to[:, :, 0].rearrange("b p w -> p b w"), flat[0]).then_inc(self.stored[u], 16)
            for b, chunks in enumerate((0, 2, 1)):
                sp.dma_start(to[b, :, 1], flat[1][:, chunks]).then_inc(self.stored[u], 16)

        load(0, 0)
        load(1, 1)
        with sp.Fori(0, KD // 2 - 1) as i:
            for u in range(2):
                store(2 * i + u, u, i, True)
        for u in range(2):
            store(KD - 2 + u, u, KD // 2 - 1, False)

    def gpsimd(self, pool):
        g = self.nc.gpsimd
        self.w.landed(pool, 0, 0)
        pool.sem_inc(self.directed, 2)
        lora2 = self.w.view(0, KD, 2 * P)

        def cut(m, u):
            g.tensor_copy(self.slice[u].rearrange("p q e -> p (q e)"), one(lora2, m)).then_inc(self.sliced, 1)

        def directed(m, u, i):
            pool.wait_ge(self.loaded[u], 16 * i + 16)
            pool.wait_ge(self.scaled, 2 * m + 1)
            for d in range(2):
                last = g.tensor_tensor(self.kd[d], self.kd[d], self.x[u][:, 1], ALU.mult)
            last.then_inc(self.kd_done, 1)

        def weighted(m, u, i):
            g.tensor_tensor(self.products, self.kd[0], self.kd[1], ALU.add)
            pool.drain()
            pool.wait_ge(self.scaled, 2 * m + 2)
            g.tensor_tensor(self.products, self.products, self.rrk, ALU.mult).then_inc(self.weighted, 1)
            pool.wait_ge(self.kk_done, m + 1)
            for d in range(2):
                g.tensor_tensor(self.kka[d], self.kk, self.a[d], ALU.mult).then_inc(self.directed, 1)

        def first(m, u, i):
            cut(0, 0)
            cut(1, 1)
            directed(0, 0, 0)
            pool.drain()
            weighted(0, 0, 0)

        def step(m, u, i, more):
            directed(m + 1, 1 - u, i + u)
            pool.drain()
            if more:
                cut(m + 2, u)
            weighted(m + 1, 1 - u, i + u)

        self.each(pool, first, step, nothing)
        for u in range(2):
            pool.wait_ge(self.stored[u], self.STORED * (KD // 2) + self.STORED)
            pool.wait_ge(self.bonus_stored[u], 16 * (KD // 2))

    def tensor(self, pe):
        t = self.nc.tensor

        def halves(out, w, x):
            for at, width in ((0, TL), (TL, TC)):
                last = t.matmul(out[:, at:at + width], w, x[:, at:at + width], start=True, stop=True)
            return last

        def lora(m, u):
            pe.wait_ge(self.sliced, m + 1)
            for q in range(2):
                for d in range(2):
                    if (q, d) == (1, 1):
                        pe.wait_ge(self.activated, 4 * m + 1)
                    hs = slice(LORA * d, LORA * d + LORA)
                    halves(self.lora_bank(q, d), self.slice[u][hs, q], self.mids[hs, q]).then_inc(self.lora, 1)

        def norm(m):
            pe.wait_ge(self.squared, m + 1)
            pe.wait_ge(self.done, m + 1)
            halves(self.wide(0), self.chip.const("pair_ones"), self.norm).then_inc(self.norm_sum, 1)

        def bonus(m):
            pe.wait_ge(self.weighted, m + 1)
            pe.wait_ge(self.rooted, m + 1)
            halves(self.wide(0), self.chip.const("pair_ones"), self.products).then_inc(self.bonus_sum, 1)

        def first(m, u, i):
            lora(m, u)
            norm(m)
            bonus(m)

        def step(m, u, i, more):
            first(m + 1, 1 - u, i)

        self.w.landed(pe, 0, 0)
        self.each(pe, first, step, nothing)
        pe.drain().then_inc(self.w.used(0), 1)

    def scalar(self, act):
        a = self.nc.scalar
        for u in range(2):
            act.sem_inc(self.stored[u], self.STORED)
        a.activation(self.one_minus_ka, self.chip.vec("k_a"), ACT.Copy, scale=-1.0, bias=1.0)
        act.drain()

        def factors(m, u, i):
            for q, (out, bias) in enumerate(((self.sg, "w0"), (self.a, "a0"))):
                if q == 1:
                    act.wait_ge(self.directed, 2 * m + 2)
                for d in range(2):
                    act.wait_ge(self.lora, 4 * m + 2 * q + d + 1)
                    a.activation(out[d], self.lora_bank(q, d), ACT.Sigmoid, bias=self.chip.vec_at(bias, m + 8 * d)).then_inc(self.activated, 1)
            act.wait_ge(self.activated, 4 * m + 4)
            act.wait_ge(self.done, m + 1)
            for d in range(2):
                last = a.activation(self.kd[d], self.a[d], ACT.Identity, scale=self.chip.vec_at("k_a", m), bias=self.one_minus_ka[:, bass.ds(m, 1)])
            last.then_inc(self.scaled, 1)
            act.wait_ge(self.raw_done, m + 1)
            a.activation(self.norm, self.kk_raw, ACT.Square).then_inc(self.squared, 1)
            act.wait_ge(self.loaded[u], 16 * i + 16)
            a.activation(self.rrk, self.x[u][:, 0], ACT.Identity, scale=self.chip.vec_at("r_k", m)).then_inc(self.scaled, 1)
            act.wait_ge(self.norm_sum, m + 1)
            a.activation(self.norm, self.wide(0), ACT.Sqrt, bias=1e-12).then_inc(self.rooted, 1)

        def terms(m, u, i):
            act.wait_ge(self.stored[u], self.STORED * i + self.STORED)
            by_chunk = lambda x: x.rearrange("p (c e) -> p c e", e=CH)
            for d in range(2):
                act.wait_ge(self.scanned, 2 * m + d + 1)
                ci, ce, out = by_chunk(self.ci[d]), by_chunk(self.ce[d]), self.out[u][d]
                a.activation(out[:, :, 0], ce, ACT.Exp, scale=-LOG_DECAY)
                a.activation(out[:, :, 1], ci, ACT.Exp, scale=-LOG_DECAY)
                a.activation(out[:, :, 2], ci, ACT.Exp, scale=LOG_DECAY)
                whole = ci[:, :, CH - 1] if d == 0 else ci[:, :, 0]
                a.activation(one(self.decays, m)[:, d], whole, ACT.Exp, scale=-LOG_DECAY).then_inc(self.exped, 1)
            for d in range(2):
                a.activation(self.out[u][d][:, :, 4], by_chunk(self.x[u][:, 2]), ACT.Copy)
            act.drain().then_inc(self.exped, 1)

        def step(m, u, i, more):
            terms(m, u, i)
            factors(m + 1, 1 - u, i + u)

        self.each(act, factors, step, terms)

    def vector(self, dve):
        v = self.nc.vector
        by_chunk = lambda x: x.rearrange("p (c e) -> p c e", e=CH)
        dve.sem_inc(self.done, 1)
        dve.wait_ge(self.starts_in, 16)

        def factors(m, u, i):
            dve.wait_ge(self.loaded[u], 16 * i + 16)
            v.tensor_scalar(self.kk_raw, self.x[u][:, 1], self.chip.vec_at("k_k", m), None, ALU.mult).then_inc(self.raw_done, 1)
            for d in range(2):
                dve.wait_ge(self.activated, 4 * m + d + 1)
                v.tensor_tensor_scan(self.ci[d], self.starts, self.sg[d], 0.0, ALU.mult, ALU.add)
                dve.drain()
                if d == 0:
                    v.tensor_tensor(self.ce[d], self.ci[d], self.sg[d], ALU.subtract).then_inc(self.scanned, 1)
                else:
                    ci = by_chunk(self.ci[d])
                    v.tensor_tensor(by_chunk(self.ce[d]), ci[:, :, CH - 1:CH].broadcast_to([P, NC, CH]), ci, ALU.subtract)
                    dve.drain()
                    v.tensor_tensor(self.ci[d], self.ce[d], self.sg[d], ALU.add).then_inc(self.scanned, 1)
            dve.wait_ge(self.rooted, m + 1)
            v.reciprocal(self.kk, self.norm)
            dve.drain()
            v.tensor_tensor(self.kk, self.kk, self.kk_raw, ALU.mult).then_inc(self.kk_done, 1)
            dve.drain()

        def terms(m, u, i):
            dve.wait_ge(self.kd_done, m + 1)
            for d in range(2):
                dve.wait_ge(self.exped, 3 * m + d + 1)
                o = self.out[u][d]
                v.tensor_tensor(o[:, :, 3], o[:, :, 2], by_chunk(self.kd[d]), ALU.mult)
                v.tensor_tensor(o[:, :, 0], o[:, :, 0], by_chunk(self.kk), ALU.mult)
                v.tensor_tensor(o[:, :, 1], o[:, :, 1], by_chunk(self.x[u][:, 0]), ALU.mult)
                dve.drain()
                dve.wait_ge(self.directed, 2 * m + d + 3)
                v.tensor_tensor(o[:, :, 2], o[:, :, 2], by_chunk(self.kka[d]), ALU.mult)
            dve.wait_ge(self.exped, 3 * m + 3)
            dve.wait_ge(self.bonus_sum, m + 1)
            v.tensor_tensor(self.x[u][:, 1], self.wide(0), self.x[u][:, 2], ALU.mult)
            dve.drain().then_inc(self.done, 1)

        def step(m, u, i, more):
            terms(m, u, i)
            factors(m + 1, 1 - u, i + u)

        self.each(dve, factors, step, terms)


Y_RWKV = A_HL
SCAN_MASKS = [("lo", CH), ("up", CH), ("lo_diag", CH), ("up_diag", CH), ("lo1", CH), ("up1", CH)] + \
    [(f"level{s}", CH) for s in (2, 4, 8, 16, 32)] + [("ident64", CH)]
LEVELS = (2, 4, 8, 16, 32)


class RwkvScan(Stage):

    def __init__(self, chip):
        super().__init__(chip)
        at = A_WORK
        self.masks_at, at = at, at + len(SCAN_MASKS) * CH
        self.terms, at = chip.view(at, BATCHES, 2 * BATCH * TERMS * CH), at + BATCHES * 2 * BATCH * TERMS * CH
        single = lambda i: [chip.view(at + (2 * i + d) * BATCH * CH, BATCH, 1, CH) for d in range(2)]
        self.t, self.tt, self.z, self.v, self.qa, self.nh = (single(i) for i in range(6))
        at += 12 * BATCH * CH
        double = lambda i: [chip.view(at + (2 * i + d) * BATCH * 2 * CH, BATCH, 2, CH) for d in range(2)]
        self.p_lg, self.mb_b, self.mg_g = (double(i) for i in range(3))
        at += 6 * BATCH * 2 * CH
        self.spread_at = at
        wide = lambda i: [chip.view(at + (2 * i + d) * BATCH * P, BATCH, P) for d in range(2)]
        self.p_sp, self.b_sp, self.g_sp, self.vin_sp, self.lbt_sp, self.tt_sp, self.z_sp, self.v_sp = (wide(i) for i in range(8))
        self.w1_sp, self.w2_sp, self.a_sp = (wide(i) for i in range(8, 11))
        self.h_sp = self.z_sp
        at += 22 * BATCH * P
        self.state_sp = [chip.view(at + d * P, 1, P) for d in range(2)]
        at += 2 * P
        self.spread_words = at - self.spread_at
        self.state = [chip.view(at + d * CH, CH) for d in range(2)]
        at += 2 * CH
        assert at <= A_END, at
        self.y = chip.view(Y_RWKV, KD * NC, CH)
        self.decays = chip.view(DECAYS, KD * 2 * NC)
        (self.masks_in, self.zeroed, self.landed, self.ready, self.taken) = (
            chip.sem("scan_" + n) for n in "masks_in zeroed landed ready taken".split())
        (self.sources_spread, self.sums, self.evacuated, self.tokens_out, self.t_ready, self.tt_ready,
         self.tt_spread, self.z_sums, self.z_masked, self.z_spread, self.t_sums, self.tt_sums,
         self.v_sums, self.v_out, self.w_sums, self.w_out, self.corrected, self.a_ready,
         self.state_ready, self.state_spread, self.state_sums, self.y_sums, self.y_added) = (
            [chip.sem(f"scan{d}_{n}") for d in range(2)] for n in (
                "sources_spread sums evacuated tokens_out t_ready tt_ready tt_spread z_sums z_masked "
                "z_spread t_sums tt_sums v_sums v_out w_sums w_out corrected a_ready state_ready "
                "state_spread state_sums y_sums y_added").split())

    def mask(self, name):
        i = [n for n, _ in SCAN_MASKS].index(name)
        return across(self.chip.view(self.masks_at + i * CH, CH), BATCH)

    def spread(self, emit, to, of):
        for h in range(2):
            hs = slice(CH * h, CH * h + CH)
            last = emit(to[hs, :, CH * h:CH * h + CH], of[hs])
        return last

    def passes(self, eng, body, start=lambda m: None):
        with eng.Fori(0, KD) as m:
            start(m)
            body(3 * m, m, 0, (0, 0))
            with eng.Fori(0, 2) as j:
                body(3 * m + j + 1, m, j + 1, (j * 4 + 4, j * -4 + 8))

    def source(self, pos, d):
        x = self.terms[:, 0] if isinstance(pos, int) else one(self.terms, pos)
        return x.rearrange("p (d c n e) -> p d c n e", d=2, n=TERMS, e=CH)[:, d]

    def bank(self, d, b):
        return self.chip.bank(4 * d + b)

    def slots(self, d, b, n):
        return self.chip.bank(4 * d + b, BATCH * n * CH).rearrange("p (c n e) -> p c n e", n=n, e=CH)

    def step(self, s, d):
        return s if d == 0 else BATCH - 1 - s

    def sync(self, sp):
        d = self.chip.dram
        sp.wait_ge(self.chip.stage_done, 4 * self.index)
        sp.dma_start(self.chip.view(self.masks_at, len(SCAN_MASKS) * CH), d["scan_const"][:, T:]).then_inc(self.masks_in, 16)
        with sp.Fori(0, KD) as m:
            for b in range(BATCHES):
                sp.wait_ge(self.taken, 3 * m + b + 1)
                sp.dma_start(self.terms[:, b], d["terms"][bass.ds(3 * m + b, 1)].rearrange("o p d w -> (o p) (d w)")
                             ).then_inc(self.landed, 16)
                sp.wait_ge(self.landed, 48 * m + 16 * b + 16)
                sp.sem_inc(self.ready, 1)

    def gpsimd(self, pool):
        g = self.nc.gpsimd
        g.memset(self.chip.view(self.spread_at, self.spread_words), 0.0)
        g.memset(self.y, 0.0)
        pool.drain().then_inc(self.zeroed, 1)

        def body(n, m, pos, chunk):
            pool.wait_ge(self.ready, n + 1)
            for d in range(2):
                x = self.source(pos, d)
                pool.wait_ge(self.v_sums[d], n + 1)
                for to, term in ((self.b_sp, 2), (self.p_sp, 0), (self.g_sp, 3), (self.vin_sp, 4)):
                    last = g.tensor_tensor(to[d].rearrange("p c (h e) -> p c h e", e=CH), x[:, :, term].unsqueeze(2).broadcast_to([P, BATCH, 2, CH]),
                                           across(self.chip.const("pair_ones").rearrange("p (h e) -> p h e", e=CH), BATCH), ALU.mult)
                last.then_inc(self.sources_spread[d], 1)
        self.passes(pool, body)

    def tensor(self, pe):
        t = self.nc.tensor
        pe.wait_ge(self.masks_in, 16)
        for d in range(2):
            pe.sem_inc(self.v_sums[d], 1)
        ident = self.chip.view(self.masks_at + (len(SCAN_MASKS) - 1) * CH, CH)

        def each(out, lhs, rhs):
            for s in range(BATCH):
                last = t.matmul(out(s), lhs[:, s], rhs(s), start=True, stop=True)
            return last

        def body(n, m, pos, chunk):
            pe.wait_ge(self.ready, n + 1)
            for d in range(2):
                x = self.source(pos, d)
                two = lambda b: lambda s: self.bank(d, b)[:, 2 * CH * s:2 * CH * s + 2 * CH]
                one_ = lambda b, at: lambda s: self.bank(d, b)[:, at + CH * s:at + CH * s + CH]
                if d == 0:
                    for e in range(2):
                        pe.wait_ge(self.sources_spread[e], n + 1)
                        each(lambda s: self.bank(e, 1)[:, 2 * CH * s:2 * CH * s + 2 * CH], self.b_sp[e],
                             lambda s: self.source(pos, e)[:, s, 0:2].rearrange("p n e -> p (n e)")).then_inc(self.sums[e], 1)
                pe.wait_ge(self.y_added[d], n + 1)
                each(two(0), self.p_sp[d], lambda s: x[:, s, 2:4].rearrange("p n e -> p (n e)")).then_inc(self.sums[d], 1)
                each(one_(2, 0), self.g_sp[d], lambda s: x[:, s, 1])
                each(one_(2, BATCH * CH), self.p_sp[d], lambda s: ident).then_inc(self.sums[d], 1)
                each(one_(3, 0), self.b_sp[d], lambda s: ident)
                each(one_(3, BATCH * CH), self.g_sp[d], lambda s: ident).then_inc(self.sums[d], 1)
            for l in range(len(LEVELS)):
                last_level = l == len(LEVELS) - 1
                for d in range(2):
                    if l == 0:
                        pe.wait_ge(self.evacuated[d], n + 1)
                    pe.wait_ge(self.t_ready[d], 5 * n + l + 1)
                    each(one_of(self.bank(d, 0)), self.lbt_sp[d], lambda s: self.t[d][:, s, 0]).then_inc(self.z_sums[d], 1)
                    if l == 0:
                        pe.wait_ge(self.tokens_out[d], n + 1)
                        each(one_of(self.bank(d, 3)), self.vin_sp[d], lambda s: ident).then_inc(self.v_sums[d], 1)
                for d in range(2):
                    pe.wait_ge(self.tt_spread[d], 6 * n + l + 1)
                    pe.wait_ge(self.z_masked[d], 5 * n + l + 1)
                    if not last_level:
                        each(one_of(self.bank(d, 1)), self.tt_sp[d], lambda s: self.z[d][:, s, 0]).then_inc(self.t_sums[d], 1)
                    pe.wait_ge(self.z_spread[d], 5 * n + l + 1)
                    each(one_of(self.bank(d, 2)), self.z_sp[d], lambda s: self.tt[d][:, s, 0]).then_inc(self.tt_sums[d], 1)
            pair_of = lambda b: lambda s: b[:, 2 * CH * s:2 * CH * s + 2 * CH]
            flat = lambda x: lambda s: x[:, s].rearrange("p n e -> p (n e)")
            for d in range(2):
                pe.wait_ge(self.v_out[d], n + 1)
                pe.wait_ge(self.tt_spread[d], 6 * n + 6)
                each(pair_of(self.bank(d, 3)), self.tt_sp[d], flat(self.p_lg[d])).then_inc(self.w_sums[d], 1)
            for d in range(2):
                pe.wait_ge(self.w_out[d], n + 1)
                each(pair_of(self.bank(d, 1)), self.w2_sp[d], flat(self.mb_b[d])).then_inc(self.corrected[d], 1)
                each(pair_of(self.bank(d, 0)), self.w1_sp[d], flat(self.mb_b[d])).then_inc(self.corrected[d], 1)
            new = lambda s, d: self.bank(d, (2, 0)[s % 2])[:, 0:CH]
            y = lambda s, d: one_of(self.bank(d, 3))(self.step(s, d))

            def share_of_v(s):
                for d in range(2):
                    c = self.step(s, d)
                    if s == 0:
                        pe.wait_ge(self.a_ready[d], 2 * n + 1)
                    t.matmul(y(s, d), self.v_sp[d][:, c], self.nh[d][:, c, 0], start=True, stop=False)
                    t.matmul(new(s, d), self.h_sp[d][:, c], self.v[d][:, c, 0], start=True, stop=False)

            share_of_v(0)
            for s in range(BATCH):
                for d in range(2):
                    if s == 0:
                        pe.wait_ge(self.a_ready[d], 2 * n + 2)
                    pe.wait_ge(self.state_ready[d], 13 * m + 4 * pos + s + 1)
                    t.matmul(new(s, d), self.a_sp[d][:, self.step(s, d)], self.state[d], start=False, stop=True).then_inc(self.state_sums[d], 1)
                for d in range(2):
                    pe.wait_ge(self.state_spread[d], 13 * m + 4 * pos + s + 1)
                    t.matmul(y(s, d), self.state_sp[d][:, 0], self.qa[d][:, self.step(s, d), 0], start=False, stop=True).then_inc(self.y_sums[d], 1)
                if s + 1 < BATCH:
                    share_of_v(s + 1)
        one_of = lambda b: lambda s: b[:, CH * s:CH * s + CH]
        self.passes(pe, body)

    def scalar(self, act):
        a = self.nc.scalar
        act.wait_ge(self.zeroed, 1)
        copy = lambda to, of: a.activation(to, of, ACT.Copy)
        half = lambda d, b, x: self.bank(d, b)[:, BATCH * CH * x:BATCH * CH * x + BATCH * CH].rearrange("p (c e) -> p c e", e=CH)

        def body(n, m, pos, chunk):
            for d in range(2):
                act.wait_ge(self.tt_ready[d], 6 * n + 1)
                self.spread(copy, self.tt_sp[d], self.tt[d][:, :, 0]).then_inc(self.tt_spread[d], 1)
                act.wait_ge(self.sums[d], 4 * n + 4)
                copy(self.mb_b[d][:, :, 1], half(d, 3, 0))
                copy(self.mg_g[d][:, :, 1], half(d, 3, 1)).then_inc(self.tokens_out[d], 1)
            for l in range(len(LEVELS)):
                if l == 0:
                    for d in range(2):
                        act.wait_ge(self.v_sums[d], n + 2)
                        copy(self.v[d][:, :, 0], half(d, 3, 0))
                        self.spread(copy, self.v_sp[d], half(d, 3, 0)).then_inc(self.v_out[d], 1)
                for d in range(2):
                    act.wait_ge(self.tt_ready[d], 6 * n + l + 2)
                    self.spread(copy, self.tt_sp[d], self.tt[d][:, :, 0]).then_inc(self.tt_spread[d], 1)
            act.wait_ge(self.w_sums[1], n + 1)
            w = self.slots(1, 3, 2)
            self.spread(copy, self.w1_sp[1], w[:, :, 0])
            self.spread(copy, self.w2_sp[1], w[:, :, 1]).then_inc(self.w_out[1], 1)
        self.passes(act, body)

    def vector(self, dve):
        v = self.nc.vector
        dve.wait_ge(self.masks_in, 16)
        dve.wait_ge(self.zeroed, 1)
        dve.sem_inc(self.taken, 3)
        for d in range(2):
            dve.sem_inc(self.y_added[d], 1)
        after, before = ("lo", "up"), ("up", "lo")
        add, mult, sub = ALU.add, ALU.mult, ALU.subtract

        def start(m):
            for d in range(2):
                v.memset(self.state[d], 0.0)
                v.memset(self.state_sp[d], 0.0)
                dve.drain().then_inc(self.state_ready[d], 1)
                dve.sem_inc(self.state_spread[d], 1)

        def body(n, m, pos, chunk):
            for d in range(2):
                dve.wait_ge(self.sums[d], 4 * n + 1)
                lbt, lb = self.slots(d, 1, 2), self.slots(d, 0, 2)
                v.tensor_tensor(self.tt[d][:, :, 0], lbt[:, :, 0], self.mask(before[d] + "1"), mult)
                for h in range(2):
                    hs = slice(CH * h, CH * h + CH)
                    v.tensor_tensor(self.lbt_sp[d][hs, :, CH * h:CH * h + CH], lbt[hs, :, 0], self.mask(before[d])[hs], mult)
                dve.drain()
                v.tensor_tensor(self.tt[d][:, :, 0], self.tt[d][:, :, 0], self.mask("ident64"), add).then_inc(self.tt_ready[d], 1)
                dve.wait_ge(self.sums[d], 4 * n + 2)
                v.tensor_tensor(self.t[d][:, :, 0], lb[:, :, 0], self.mask(after[d] + "1"), mult)
                v.tensor_tensor(self.mb_b[d][:, :, 0], lbt[:, :, 1], self.mask(before[d] + "_diag"), mult)
                dve.drain()
                v.tensor_tensor(self.t[d][:, :, 0], self.t[d][:, :, 0], self.mask("ident64"), add).then_inc(self.t_ready[d], 1)
                v.tensor_tensor(self.p_lg[d][:, :, 1], lb[:, :, 1], self.mask(after[d]), mult)
                dve.wait_ge(self.sums[d], 4 * n + 3)
                third = self.bank(d, 2).rearrange("p (n c e) -> p n c e", n=2, e=CH)
                v.tensor_tensor(self.mg_g[d][:, :, 0], third[:, 0], self.mask(before[d] + "_diag"), mult)
                v.tensor_copy(self.p_lg[d][:, :, 0], third[:, 1])
                dve.drain().then_inc(self.evacuated[d], 1)
            for l, level in enumerate(LEVELS):
                for d in range(2):
                    dve.wait_ge(self.z_sums[d], 5 * n + l + 1)
                    v.tensor_tensor(self.z[d][:, :, 0], self.slots(d, 0, 1)[:, :, 0], self.mask(f"level{level}"), mult).then_inc(self.z_masked[d], 1)
                    dve.drain()
                    self.spread(v.tensor_copy, self.z_sp[d], self.z[d][:, :, 0]).then_inc(self.z_spread[d], 1)
                for d in range(2):
                    if level != LEVELS[-1]:
                        dve.wait_ge(self.t_sums[d], 4 * n + l + 1)
                        v.tensor_tensor(self.t[d], self.t[d], self.slots(d, 1, 1), add).then_inc(self.t_ready[d], 1)
                    dve.wait_ge(self.tt_sums[d], 5 * n + l + 1)
                    v.tensor_tensor(self.tt[d], self.tt[d], self.slots(d, 2, 1), add).then_inc(self.tt_ready[d], 1)
            dve.wait_ge(self.w_sums[0], n + 1)
            w = self.slots(0, 3, 2)
            self.spread(v.tensor_copy, self.w1_sp[0], w[:, :, 0])
            self.spread(v.tensor_copy, self.w2_sp[0], w[:, :, 1]).then_inc(self.w_out[0], 1)
            for d in range(2):
                x = self.source(pos, d)
                ident = self.mask("ident64")
                minus = lambda to, a, b: v.tensor_tensor(to, a, b, sub)
                both = lambda to, a, b: self.spread(lambda t_, i: minus(t_, i[0], i[1]), to, Halves(a, b))
                c1, c2 = self.slots(d, 0, 2), self.slots(d, 1, 2)
                dve.wait_ge(self.corrected[d], 2 * n + 1)
                minus(self.nh[d][:, :, 0], self.mg_g[d][:, :, 0], c2[:, :, 0])
                both(self.h_sp[d], self.mg_g[d][:, :, 1], c2[:, :, 1]).then_inc(self.a_ready[d], 1)
                dve.wait_ge(self.corrected[d], 2 * n + 2)
                minus(self.qa[d][:, :, 0], x[:, :, 1], c1[:, :, 0])
                both(self.a_sp[d], ident, c1[:, :, 1])
                dve.drain().then_inc(self.a_ready[d], 1)
            dve.sem_inc(self.taken, 1)
            for s in range(BATCH):
                dve.drain()
                for d in range(2):
                    dve.wait_ge(self.state_sums[d], 4 * n + s + 1)
                    at = m * (2 * NC) + NC * d + self.step(s, d) + chunk[d]
                    v.tensor_scalar(self.state[d], self.bank(d, (2, 0)[s % 2])[:, 0:CH], self.decays[:, bass.ds(at, 1)], None, mult
                                    ).then_inc(self.state_ready[d], 1)
                dve.drain()
                for d in range(2):
                    dve.wait_ge(self.y_sums[d], 4 * n + s + 1)
                    self.spread(v.tensor_copy, self.state_sp[d], self.state[d].unsqueeze(1)).then_inc(self.state_spread[d], 1)
            for d in range(2):
                y = self.y[:, bass.ds(m * NC + chunk[d], BATCH)]
                v.tensor_tensor(y, y, self.slots(d, 3, 1)[:, :, 0], add).then_inc(self.y_added[d], 1)
                dve.drain()
        self.passes(dve, body, start)


class Halves:

    def __init__(self, *views):
        self.views = views

    def __getitem__(self, hs):
        return [v[hs] for v in self.views]


class RwkvOutput(Stage):

    def __init__(self, chip):
        super().__init__(chip)
        self.y = chip.view(Y_RWKV, KD, T)
        at = RWKV
        self.bonus = [chip.view(at + u * T, T) for u in range(2)]
        self.z = [chip.view(at + (2 + u) * T, T) for u in range(2)]
        self.squares, self.inv = [chip.view(at + (4 + u) * T, T) for u in range(2)], chip.view(at + 6 * T, T)
        self.loaded = [chip.sem(f"rwkv_out_loaded{u}") for u in range(2)]
        (self.mean_sum, self.centred, self.squared, self.var_sum, self.rooted, self.inverted, self.scaled, self.done) = (
            chip.sem("rwkv_out_" + n) for n in "mean_sum centred squared var_sum rooted inverted scaled done".split())

    def wide(self, q):
        return self.chip.psum[:, 2 * q:2 * q + 2].rearrange("p b w -> p (b w)")[:, 0:T]

    def each(self, eng, ahead, finish):
        ahead(0, 0)
        with eng.Fori(0, KD // 2 - 1) as i:
            for u in range(2):
                ahead(2 * i + u + 1, 1 - u)
                finish(2 * i + u, u, i)
        ahead(KD - 1, 1)
        for u in range(2):
            finish(KD - 2 + u, u, KD // 2 - 1)

    def sync(self, sp):
        sp.wait_ge(self.chip.stage_done, 4 * self.index)

        def body(i, u):
            m = 2 * i + u
            sp.wait_ge(self.done, m + 1)
            for to, of in ((self.bonus[u], self.chip.dram["bonus"][bass.ds(m, 1)]), (self.z[u], self.chip.dram["rkvz"][bass.ds(4 * m + 3, 1)])):
                sp.dma_start(to, of.rearrange("o p w -> (o p) w")).then_inc(self.loaded[u], 16)
        pairs(sp, KD, body)

    def tensor(self, pe):
        def sums(out, x):
            for at, width in ((0, TL), (TL, TC)):
                last = self.nc.tensor.matmul(out[:, at:at + width], self.chip.const("pair_ones"), x[:, at:at + width], start=True, stop=True)
            return last

        def ahead(m, u):
            sums(self.wide(u), one(self.y, m)).then_inc(self.mean_sum, 1)

        def finish(m, u, i):
            pe.wait_ge(self.squared, m + 1)
            pe.wait_ge(self.rooted, m + 1)
            sums(self.wide(2 + u), self.squares[u]).then_inc(self.var_sum, 1)
        self.each(pe, ahead, finish)

    def scalar(self, act):
        a = self.nc.scalar
        act.sem_inc(self.rooted, 2)

        def ahead(m, u):
            act.wait_ge(self.centred, m + 1)
            act.wait_ge(self.inverted, m + 1)
            a.activation(self.squares[u], one(self.y, m), ACT.Square).then_inc(self.squared, 1)

        def finish(m, u, i):
            act.wait_ge(self.var_sum, m + 1)
            a.activation(self.squares[u], self.wide(2 + u), ACT.Sqrt, scale=1.0 / RW, bias=64e-5).then_inc(self.rooted, 1)
        self.each(act, ahead, finish)

    def vector(self, dve):
        v = self.nc.vector
        dve.sem_inc(self.inverted, 2)

        def ahead(m, u):
            y = one(self.y, m)
            dve.wait_ge(self.mean_sum, m + 1)
            v.scalar_tensor_tensor(y, self.wide(u), -1.0 / RW, y, ALU.mult, ALU.add).then_inc(self.centred, 1)

        def finish(m, u, i):
            y = one(self.y, m)
            dve.drain()
            dve.wait_ge(self.rooted, m + 3)
            v.reciprocal(self.inv, self.squares[u]).then_inc(self.inverted, 1)
            dve.drain()
            v.tensor_tensor(y, y, self.inv, ALU.mult)
            dve.drain()
            v.tensor_scalar(y, y, self.chip.vec_at("ln_gain", m), self.chip.vec_at("ln_bias", m), ALU.mult, ALU.add).then_inc(self.scaled, 1)
        self.each(dve, ahead, finish)

    def gpsimd(self, pool):
        g = self.nc.gpsimd
        pool.sem_inc(self.done, 2)

        def body(i, u):
            y = one(self.y, 2 * i + u)
            pool.wait_ge(self.scaled, 2 * i + u + 1)
            pool.wait_ge(self.loaded[u], 32 * i + 32)
            g.tensor_tensor(y, y, self.bonus[u], ALU.add)
            pool.drain()
            g.tensor_tensor(y, y, self.z[u], ALU.mult).then_inc(self.done, 1)
        pairs(pool, KD, body)


def rwkv_layer(chip, layer):
    y = chip.view(Y_RWKV, KD, T)
    gate = modulated(chip, layer, 2)
    return [norm2(chip, layer, True), RwkvFeatures(chip), RwkvTerms(chip), RwkvScan(chip), RwkvOutput(chip),
            Residual(chip, "w_rwkv_out", KD, lambda k: y[:, k, TC:T], gate[0], lambda k: y[:, k, 0:TC], gate[1])]


def program(nc, dram, stages_of=None):
    with ExitStack() as ctx:
        chip = Chip(nc, dram, ctx)
        stages = (stages_of or all_stages)(chip)
        assert [stage.index for stage in stages] == list(range(len(stages)))
        block = ctx.enter_context(nc.Block())

        def walk(eng, run, between=lambda n: None):
            for n, stage in enumerate(stages):
                if n > 0:
                    eng.wait_ge(chip.stage_done, 4 * n)
                    between(n)
                    eng.drain()
                run(stage)
                eng.drain().then_inc(chip.stage_done, 1)

        @block.sync
        def _(sp):
            for stage in stages:
                stage.sync(sp)
                sp.sem_inc(chip.loads_issued, 1)

        @block.tensor
        def _(pe):
            walk(pe, lambda stage: stage.tensor(pe))

        @block.scalar
        def _(act):
            walk(act, lambda stage: stage.scalar(act))

        @block.vector
        def _(dve):
            walk(dve, lambda stage: stage.vector(dve))

        @block.gpsimd
        def _(pool):
            def clear(n):
                pool.wait_ge(chip.loads_issued, n)
                chip.clear_sems(pool, n - 1)

            walk(pool, lambda stage: stage.gpsimd(pool), clear)


SCRATCH = {"states": (2 * SsdStates.STEPS, P, D_SSD), "rkvz": (4 * KD, P, T), "bonus": (KD, P, T),
           "terms": (KD * BATCHES, P, 2, BATCH * TERMS * CH)}


def layers(chip):
    return block1(chip) + [
        *sgu_layer(chip, 0, 0, 6), *rwkv_layer(chip, 1), *mla_layer(chip, 2), *sgu_layer(chip, 3, 1, 4)]


def all_stages(chip):
    return layers(chip) + [Store(chip)]


def kernel(**inputs):
    import concourse.bacc as bacc
    from concourse.bass_utils import run_bass_kernel_spmd

    nc = bacc.Bacc("TRN2", target_bir_lowering=False, num_devices=1)
    arrays = {n: np.ascontiguousarray(a, dtype=np.float32) for n, a in prepare(inputs).items()}
    dram = {n: nc.dram_tensor(n, a.shape, F32, kind="ExternalInput").ap() for n, a in arrays.items()}
    for n, shape in SCRATCH.items():
        dram[n] = nc.dram_tensor(n, shape, F32, kind="Internal").ap()
    dram["out"] = nc.dram_tensor("out", (P, KD * TL), F32, kind="ExternalOutput").ap()
    program(nc, dram)
    got = run_bass_kernel_spmd(nc, [arrays], core_ids=[0]).results[0]["out"]
    return np.asarray(got).reshape(P, KD, TL).transpose(2, 1, 0).reshape(1, TL, D)
```
